# Optimizing a Trainium2 kernel written in Bass

```python
import math
import jax, jax.numpy as jnp
from jax import lax
import numpy as np

D_MODEL = 1024
BATCH = 1
SEQ = 512
DEPTH = 1
DEC_BATCH = 8
DEC_SEQ = 1
PAST_LEN = 4096
PAGE_SIZE = 128

S5_GROUP = 16
S5_GROUPS = D_MODEL // 32
S5_WIDTH = S5_GROUPS * S5_GROUP
S5_STATE = 64
S5_DT_MIN = 0.001
S5_DT_MAX = 0.1

M2_INNER = D_MODEL
M2_HEADDIM = 64
M2_HEADS = M2_INNER // M2_HEADDIM
M2_GROUPS = 4
M2_HPG = M2_HEADS // M2_GROUPS
M2_STATE = 128
M2_CONV = 4
M2_CHUNK = 128
M2_CONV_DIM = M2_INNER + 2 * M2_GROUPS * M2_STATE
M2_DT_MIN = 0.001
M2_DT_MAX = 0.1

PEER_HEADS = 8
PEER_NKEYS = 128
PEER_TOPK = 16
PEER_DKEY = 256
PEER_DHALF = PEER_DKEY // 2
PEER_EXPERTS = PEER_NKEYS * PEER_NKEYS
PEER_BLOCK = 128

IN_DIM = S5_WIDTH + M2_INNER + M2_CONV_DIM + M2_HEADS + 2 * D_MODEL
NORM_EPS = 1e-6
GNORM_EPS = 1e-5

kernel_name = "hybrid_s5_ssd_peer_decode_step"

def rmsnorm(x, g):
    xf = x.astype(jnp.float32)
    out = xf * lax.rsqrt(jnp.mean(xf * xf, axis=-1, keepdims=True) + NORM_EPS)
    return (out * g.astype(jnp.float32)).astype(x.dtype)

def modulate(h, shift, scale):
    return h * (1 + scale[:, None, :]) + shift[:, None, :]

def _complex_affine_combine(e1, e2):
    a1r, a1i, b1r, b1i = e1
    a2r, a2i, b2r, b2i = e2
    return (a2r * a1r - a2i * a1i,
            a2r * a1i + a2i * a1r,
            a2r * b1r - a2i * b1i + b2r,
            a2r * b1i + a2i * b1r + b2i)

def s5_branch(u, a_re, a_im, log_dt, b_re, b_im, c_re, c_im, d, w_glu, b_glu, s0_re, s0_im):
    f32 = jnp.float32
    bsz, L, _ = u.shape
    ug = u.astype(f32).reshape(bsz, L, S5_GROUPS, S5_GROUP)
    dt = jnp.exp(log_dt.astype(f32))[:, None]
    ar = a_re.astype(f32)
    ai = a_im.astype(f32)
    mag = jnp.exp(dt * ar)
    abar_re = mag * jnp.cos(dt * ai)
    abar_im = mag * jnp.sin(dt * ai)
    den = ar * ar + ai * ai
    nr = abar_re - 1.0
    f_re = (nr * ar + abar_im * ai) / den
    f_im = (abar_im * ar - nr * ai) / den
    br = b_re.astype(f32)
    bi = b_im.astype(f32)
    bbar_re = f_re[..., None] * br - f_im[..., None] * bi
    bbar_im = f_re[..., None] * bi + f_im[..., None] * br
    bu_re = jnp.einsum('gph,blgh->blgp', bbar_re, ug)
    bu_im = jnp.einsum('gph,blgh->blgp', bbar_im, ug)
    if s0_re is not None:
        sr = s0_re.astype(f32)
        si = s0_im.astype(f32)
        bu_re = bu_re.at[:, 0].add(abar_re * sr - abar_im * si)
        bu_im = bu_im.at[:, 0].add(abar_re * si + abar_im * sr)
    shp = bu_re.shape
    elems = (jnp.broadcast_to(abar_re, shp), jnp.broadcast_to(abar_im, shp), bu_re, bu_im)
    _, _, s_re, s_im = lax.associative_scan(_complex_affine_combine, elems, axis=1)
    y = (jnp.einsum('ghp,blgp->blgh', c_re.astype(f32), s_re)
         - jnp.einsum('ghp,blgp->blgh', c_im.astype(f32), s_im)
         + d.astype(f32) * ug)
    y = jax.nn.gelu(y.reshape(bsz, L, S5_WIDTH), approximate=False)
    y = y * jax.nn.sigmoid(y @ w_glu.astype(f32) + b_glu.astype(f32))
    return y.astype(u.dtype), s_re[:, -1].astype(u.dtype), s_im[:, -1].astype(u.dtype)

def causal_conv(xbc, conv_w, conv_b, buf):
    bsz, L, C = xbc.shape
    if buf is None:
        buf = jnp.zeros((bsz, M2_CONV - 1, C), xbc.dtype)
    xp = jnp.concatenate([buf.astype(xbc.dtype), xbc], axis=1)
    out = conv_b + xp[:, 0:L] * conv_w[0]
    for k in range(1, M2_CONV):
        out = out + xp[:, k:k + L] * conv_w[k]
    return jax.nn.silu(out), xp[:, xp.shape[1] - (M2_CONV - 1):]

def ssd(x, dt, a, bm, cm, h0):
    bsz, L = x.shape[0], x.shape[1]
    q = M2_CHUNK if L % M2_CHUNK == 0 else L
    nc = L // q
    x = x.reshape(bsz, nc, q, M2_GROUPS, M2_HPG, M2_HEADDIM)
    dt = dt.reshape(bsz, nc, q, M2_GROUPS, M2_HPG)
    bm = bm.reshape(bsz, nc, q, M2_GROUPS, M2_STATE)
    cm = cm.reshape(bsz, nc, q, M2_GROUPS, M2_STATE)
    cs = jnp.cumsum(dt * a, axis=2)
    seg = cs[:, :, :, None] - cs[:, :, None, :]
    mask = jnp.tril(jnp.ones((q, q), dtype=bool))[:, :, None, None]
    decay = jnp.exp(jnp.where(mask, seg, -jnp.inf))
    xdt = x * dt[..., None]
    cb = jnp.einsum('bcign,bcjgn->bcijg', cm, bm)
    y_diag = jnp.einsum('bcijgr,bcjgrp->bcigrp', cb[..., None] * decay, xdt)
    decay_st = jnp.exp(cs[:, :, -1:] - cs)
    states = jnp.einsum('bcjgn,bcjgr,bcjgrp->bcgrpn', bm, decay_st, xdt)
    chunk_decay = jnp.exp(cs[:, :, -1])

    def step(h, inp):
        dec, st = inp
        return dec[..., None, None] * h + st, h

    h_last, h_prev = lax.scan(step, h0, (jnp.moveaxis(chunk_decay, 1, 0), jnp.moveaxis(states, 1, 0)))
    h_prev = jnp.moveaxis(h_prev, 0, 1)
    y_off = jnp.einsum('bcign,bcgrpn,bcigr->bcigrp', cm, h_prev, jnp.exp(cs))
    y = (y_diag + y_off).reshape(bsz, L, M2_GROUPS, M2_HPG, M2_HEADDIM)
    return y, h_last

def mamba2_branch(z, xbc, dt_raw, conv_w, conv_b, dt_bias, a_log, d_skip, g_norm, conv_buf, h0):
    f32 = jnp.float32
    bsz, L, _ = z.shape
    xbc, new_buf = causal_conv(xbc, conv_w, conv_b, conv_buf)
    xs = xbc[..., :M2_INNER].astype(f32).reshape(bsz, L, M2_GROUPS, M2_HPG, M2_HEADDIM)
    bm = xbc[..., M2_INNER:M2_INNER + M2_GROUPS * M2_STATE].astype(f32).reshape(bsz, L, M2_GROUPS, M2_STATE)
    cm = xbc[..., M2_INNER + M2_GROUPS * M2_STATE:].astype(f32).reshape(bsz, L, M2_GROUPS, M2_STATE)
    dt = jax.nn.softplus(dt_raw.astype(f32) + dt_bias.astype(f32)).reshape(bsz, L, M2_GROUPS, M2_HPG)
    a = -jnp.exp(a_log.astype(f32)).reshape(M2_GROUPS, M2_HPG)
    if h0 is None:
        h0 = jnp.zeros((bsz, M2_GROUPS, M2_HPG, M2_HEADDIM, M2_STATE), f32)
    else:
        h0 = h0.astype(f32).reshape(bsz, M2_GROUPS, M2_HPG, M2_HEADDIM, M2_STATE)
    y, h_last = ssd(xs, dt, a, bm, cm, h0)
    y = y + d_skip.astype(f32).reshape(M2_GROUPS, M2_HPG)[..., None] * xs
    y = y.reshape(bsz, L, M2_INNER) * jax.nn.silu(z.astype(f32))
    yg = y.reshape(bsz, L, M2_GROUPS, M2_INNER // M2_GROUPS)
    yg = yg * lax.rsqrt(jnp.mean(yg * yg, axis=-1, keepdims=True) + GNORM_EPS)
    y = yg.reshape(bsz, L, M2_INNER) * g_norm.astype(f32)
    h_last = h_last.reshape(bsz, M2_HEADS, M2_HEADDIM, M2_STATE)
    return y.astype(z.dtype), new_buf, h_last.astype(z.dtype)

def peer(x2, w_query, sub_keys, expert_down, expert_up):
    f32 = jnp.float32
    bsz, L, D = x2.shape
    T = bsz * L
    nblk = -(-T // PEER_BLOCK)
    xt = x2.reshape(T, D)
    xt = jnp.pad(xt, ((0, nblk * PEER_BLOCK - T), (0, 0))).reshape(nblk, PEER_BLOCK, D)
    keys = sub_keys.astype(f32)

    def block(xb):
        qv = (xb @ w_query).astype(f32).reshape(PEER_BLOCK, PEER_HEADS, 2, PEER_DHALF)
        s = jnp.einsum('thsd,hskd->thsk', qv, keys)
        sv, si = lax.top_k(s, PEER_TOPK)
        cand = sv[:, :, 0, :, None] + sv[:, :, 1, None, :]
        cidx = si[:, :, 0, :, None] * PEER_NKEYS + si[:, :, 1, None, :]
        fv, fi = lax.top_k(cand.reshape(PEER_BLOCK, PEER_HEADS, PEER_TOPK * PEER_TOPK), PEER_TOPK)
        eidx = jnp.take_along_axis(cidx.reshape(PEER_BLOCK, PEER_HEADS, PEER_TOPK * PEER_TOPK), fi, axis=-1)
        g = jax.nn.softmax(fv, axis=-1)
        u = expert_down[eidx]
        act = jax.nn.gelu(jnp.einsum('thkd,td->thk', u, xb).astype(f32), approximate=False) * g
        v = expert_up[eidx]
        return jnp.einsum('thk,thkd->td', act.astype(v.dtype), v)

    out = lax.map(block, xt)
    return out.reshape(nblk * PEER_BLOCK, D)[:T].reshape(bsz, L, D).astype(x2.dtype)

def trunk(x, c, state, w_ada, b_ada, g_norm1, g_norm2, w_in, s5_a_re, s5_a_im, s5_log_dt, s5_b_re, s5_b_im,
          s5_c_re, s5_c_im, s5_d, s5_w_glu, s5_b_glu, w_branch_a, conv_w, conv_b, dt_bias, a_log, d_skip,
          g_ssm_norm, w_branch_b, w_out, w_query, sub_keys, expert_down, expert_up, g_final, w_ada_final,
          b_ada_final):
    sc = jax.nn.silu(c)
    o1 = S5_WIDTH
    o2 = o1 + M2_INNER
    o3 = o2 + M2_CONV_DIM
    o4 = o3 + M2_HEADS
    new_re, new_im, new_ssm, new_conv = [], [], [], []
    for l in range(DEPTH):
        if state is None:
            s0r, s0i, h0, buf = None, None, None, None
        else:
            s0r, s0i, h0, buf = state[0][l], state[1][l], state[2][l], state[3][l]
        mod = sc @ w_ada[l] + b_ada[l]
        sh1, sc1, gt1, sh2, sc2, gt2 = jnp.split(mod, 6, axis=-1)
        h = modulate(rmsnorm(x, g_norm1[l]), sh1, sc1)
        proj = h @ w_in[l]
        u = proj[..., :o1]
        z = proj[..., o1:o2]
        xbc = proj[..., o2:o3]
        dt_raw = proj[..., o3:o4]
        gates = jax.nn.sigmoid(proj[..., o4:])
        ya, sr, si = s5_branch(u, s5_a_re[l], s5_a_im[l], s5_log_dt[l], s5_b_re[l], s5_b_im[l], s5_c_re[l],
                               s5_c_im[l], s5_d[l], s5_w_glu[l], s5_b_glu[l], s0r, s0i)
        yb, nbuf, hl = mamba2_branch(z, xbc, dt_raw, conv_w[l], conv_b[l], dt_bias[l], a_log[l], d_skip[l],
                                     g_ssm_norm[l], buf, h0)
        merged = gates[..., :D_MODEL] * (ya @ w_branch_a[l]) + gates[..., D_MODEL:] * (yb @ w_branch_b[l])
        x = x + gt1[:, None, :] * (merged @ w_out[l])
        h2 = modulate(rmsnorm(x, g_norm2[l]), sh2, sc2)
        x = x + gt2[:, None, :] * peer(h2, w_query[l], sub_keys[l], expert_down[l], expert_up[l])
        new_re.append(sr)
        new_im.append(si)
        new_ssm.append(hl)
        new_conv.append(nbuf)
    shf, scf = jnp.split(sc @ w_ada_final + b_ada_final, 2, axis=-1)
    y = modulate(rmsnorm(x, g_final), shf, scf)
    return y, jnp.stack(new_re), jnp.stack(new_im), jnp.stack(new_ssm), jnp.stack(new_conv)

def setup_inputs(seed: int = 0) -> dict:
    key = jax.random.key(seed)
    ks = iter(jax.random.split(key, 48))
    f32 = jnp.float32
    nrm = lambda shape, s: jax.random.normal(next(ks), shape, f32) * s
    D = D_MODEL
    inp = {}
    inp['x_prompt'] = nrm((BATCH, SEQ, D), 1.0)
    inp['x_sample'] = nrm((DEC_BATCH, DEC_SEQ, D), 1.0)
    inp['state_s5_re'] = nrm((DEPTH, DEC_BATCH, S5_GROUPS, S5_STATE), 0.1)
    inp['state_s5_im'] = nrm((DEPTH, DEC_BATCH, S5_GROUPS, S5_STATE), 0.1)
    inp['state_ssm'] = nrm((DEPTH, DEC_BATCH, M2_HEADS, M2_HEADDIM, M2_STATE), 0.1)
    inp['state_conv'] = nrm((DEPTH, DEC_BATCH, M2_CONV - 1, M2_CONV_DIM), 1.0)
    inp['c_prompt'] = nrm((BATCH, D), 1.0)
    inp['c_sample'] = nrm((DEC_BATCH, D), 1.0)
    inp['w_ada'] = nrm((DEPTH, D, 6 * D), 0.5 * D ** -0.5)
    inp['b_ada'] = nrm((DEPTH, 6 * D), 0.01)
    inp['g_norm1'] = 1.0 + nrm((DEPTH, D), 0.05)
    inp['g_norm2'] = 1.0 + nrm((DEPTH, D), 0.05)
    inp['w_in'] = nrm((DEPTH, D, IN_DIM), D ** -0.5)
    inp['s5_a_re'] = -0.5 + nrm((DEPTH, S5_GROUPS, S5_STATE), 0.01)
    inp['s5_a_im'] = jnp.pi * jnp.arange(S5_STATE, dtype=f32) + nrm((DEPTH, S5_GROUPS, S5_STATE), 0.01)
    inp['s5_log_dt'] = jax.random.uniform(next(ks), (DEPTH, S5_GROUPS), f32, math.log(S5_DT_MIN), math.log(S5_DT_MAX))
    inp['s5_b_re'] = nrm((DEPTH, S5_GROUPS, S5_STATE, S5_GROUP), (2 * S5_GROUP) ** -0.5)
    inp['s5_b_im'] = nrm((DEPTH, S5_GROUPS, S5_STATE, S5_GROUP), (2 * S5_GROUP) ** -0.5)
    inp['s5_c_re'] = nrm((DEPTH, S5_GROUPS, S5_GROUP, S5_STATE), S5_STATE ** -0.5)
    inp['s5_c_im'] = nrm((DEPTH, S5_GROUPS, S5_GROUP, S5_STATE), S5_STATE ** -0.5)
    inp['s5_d'] = nrm((DEPTH, S5_GROUPS, S5_GROUP), 1.0)
    inp['s5_w_glu'] = nrm((DEPTH, S5_WIDTH, S5_WIDTH), S5_WIDTH ** -0.5)
    inp['s5_b_glu'] = nrm((DEPTH, S5_WIDTH), 0.01)
    inp['w_branch_a'] = nrm((DEPTH, S5_WIDTH, D), S5_WIDTH ** -0.5)
    inp['conv_w'] = nrm((DEPTH, M2_CONV, M2_CONV_DIM), M2_CONV ** -0.5)
    inp['conv_b'] = nrm((DEPTH, M2_CONV_DIM), 0.01)
    dt0 = jnp.exp(jax.random.uniform(next(ks), (DEPTH, M2_HEADS), f32, math.log(M2_DT_MIN), math.log(M2_DT_MAX)))
    inp['dt_bias'] = dt0 + jnp.log(-jnp.expm1(-dt0))
    inp['a_log'] = jnp.log(jax.random.uniform(next(ks), (DEPTH, M2_HEADS), f32, 1.0, 16.0))
    inp['d_skip'] = 1.0 + nrm((DEPTH, M2_HEADS), 0.1)
    inp['g_ssm_norm'] = 1.0 + nrm((DEPTH, M2_INNER), 0.05)
    inp['w_branch_b'] = nrm((DEPTH, M2_INNER, D), M2_INNER ** -0.5)
    inp['w_out'] = nrm((DEPTH, D, D), D ** -0.5)
    inp['w_query'] = nrm((DEPTH, D, PEER_HEADS * PEER_DKEY), D ** -0.5)
    inp['sub_keys'] = nrm((DEPTH, PEER_HEADS, 2, PEER_NKEYS, PEER_DHALF), PEER_DHALF ** -0.5)
    inp['expert_down'] = nrm((DEPTH, PEER_EXPERTS, D), D ** -0.5)
    inp['expert_up'] = nrm((DEPTH, PEER_EXPERTS, D), PEER_HEADS ** -0.5)
    inp['g_final'] = 1.0 + nrm((D,), 0.05)
    inp['w_ada_final'] = nrm((D, 2 * D), 0.5 * D ** -0.5)
    inp['b_ada_final'] = nrm((2 * D,), 0.01)
    return inp

def reference(x_prompt, x_sample, state_s5_re, state_s5_im, state_ssm, state_conv, c_prompt, c_sample,
              w_ada, b_ada, g_norm1, g_norm2, w_in, s5_a_re, s5_a_im, s5_log_dt, s5_b_re, s5_b_im, s5_c_re,
              s5_c_im, s5_d, s5_w_glu, s5_b_glu, w_branch_a, conv_w, conv_b, dt_bias, a_log, d_skip, g_ssm_norm,
              w_branch_b, w_out, w_query, sub_keys, expert_down, expert_up, g_final, w_ada_final, b_ada_final):
    weights = (w_ada, b_ada, g_norm1, g_norm2, w_in, s5_a_re, s5_a_im, s5_log_dt, s5_b_re, s5_b_im, s5_c_re,
               s5_c_im, s5_d, s5_w_glu, s5_b_glu, w_branch_a, conv_w, conv_b, dt_bias, a_log, d_skip, g_ssm_norm,
               w_branch_b, w_out, w_query, sub_keys, expert_down, expert_up, g_final, w_ada_final, b_ada_final)
    y_prompt, s5_re_p, s5_im_p, ssm_p, conv_p = trunk(x_prompt, c_prompt, None, *weights)
    y_sample, s5_re_s, s5_im_s, ssm_s, conv_s = trunk(
        x_sample, c_sample, (state_s5_re, state_s5_im, state_ssm, state_conv), *weights)
    return (y_prompt, y_sample, s5_re_p, s5_im_p, ssm_p, conv_p, s5_re_s, s5_im_s, ssm_s, conv_s)


_drawn_inputs = setup_inputs


def setup_inputs(seed=0):
    import zlib

    import numpy as np

    out = dict(_drawn_inputs(seed))
    spreads = {}
    factors = {'g_norm2': 4.202,
     's5_a_re': 70.934,
     's5_c_re': 8.0,
     's5_c_im': 8.0,
     's5_w_glu': 2.954,
     's5_b_glu': 200.0,
     'conv_b': 3.03,
     'd_skip': 6.007,
     'g_ssm_norm': 6.183,
     'b_ada_final': 4.316}
    for name, (base, spread) in spreads.items():
        noise = np.random.default_rng([zlib.crc32(name.encode()), seed]).standard_normal(out[name].shape)
        drawn = base * np.exp(spread * noise) if base else spread * noise
        out[name] = __import__('jax').numpy.asarray(drawn.astype(out[name].dtype))
    for name, factor in factors.items():
        out[name] = (out[name] * factor).astype(out[name].dtype)
    return out
```

```python
import math
from contextlib import ExitStack

import numpy as np

import concourse.bass as bass
from concourse import mybir

F32 = mybir.dt.float32
U32 = mybir.dt.uint32
I32 = mybir.dt.int32
ALU = mybir.AluOpType
ACT = mybir.ActivationFunctionType
AX_X = mybir.AxisListType.X

P = 128
D = 1024
KD = D // P
L = 512
NS = 8
T = L + NS
NB = L // P
HALF = T // 2
NC_ROWS = NS + 1
NMOD = 8
EPS = 1e-6
G_EPS = 1e-5

S5W = 512
NG5 = 32
G5 = 16
ST5 = 64
NS5 = NG5 * ST5 // P
TB5 = 256

CD = 2048
NCV = CD // P
NH = 16
HD = 64
SN = 128
NGR = 4
HPG = 4

PH = 8
NK = 128
TOPK = 16
DQ = PH * 256
NEG = -3.0e38


class Link:

    def __init__(self, eng, sem):
        self.eng, self.sem, self.n = eng, sem, 0

    def __call__(self, ins):
        self.n += 1
        ins.then_inc(self.sem, 1)
        self.eng.wait_ge(self.sem, self.n)


class Arena:
    def __init__(self, tensor):
        self.t = tensor

    def __call__(self, at, *shape, rows=P):
        n = int(np.prod(shape))
        v = self.t[0:rows, at:at + n]
        if len(shape) == 2:
            return v.rearrange("p (a b) -> p a b", b=shape[1])
        if len(shape) == 3:
            return v.rearrange("p (a b c) -> p a b c", b=shape[1], c=shape[2])
        return v


class Map:
    W = 53000
    IDENT = 0
    ONES = 128
    HT = 256
    ZS = HT + KD * T
    GB = ZS + KD * T
    MG = GB + KD * T
    LOCAL = MG + KD * T
    X1 = LOCAL
    H2 = X1 + 5 * D
    SC = H2 + 5 * D
    SCS = SC + NB * PH * 2 * NK
    QLOCAL = SCS + 2 * NK


def two(ps_tile):
    return ps_tile[:, :, 0:HALF]


def cols(ap):
    return ap.rearrange("p (a b) -> p a b", b=HALF)


def constants(nc, mem, sem):
    ident, ones = mem(Map.IDENT, P), mem(Map.ONES, P)
    s_const = sem("s_const")
    with nc.Block() as block:
        @block.gpsimd
        def _(pool):
            link = Link(pool, s_const)
            link(nc.gpsimd.memset(mem(Map.IDENT, 2 * P), 1.0))
            link(nc.gpsimd.affine_select(out=ident, in_=ident, compare_op=ALU.is_equal, fill=0.0,
                                         base=0, pattern=[[-1, P]], channel_multiplier=1))


def stage_condition(nc, mem, sem, ps, A, mod_d):
    M = Map.LOCAL
    ring = [mem(M + i * KD * 512, KD, 512) for i in range(4)]
    M += 4 * KD * 512
    bias = mem(M, NMOD * D, rows=NC_ROWS); M += NMOD * D
    x = mem(M, 5, D); M += 5 * D
    c = mem(M, D, rows=NC_ROWS); M += D
    sc = mem(M, D, rows=NC_ROWS); M += D
    cT = mem(M, KD, NC_ROWS); M += KD * NC_ROWS
    stat = mem(M, 5); M += 8
    rstd = mem(M, 5); M += 8
    assert M <= Map.W
    g1 = mem(Map.ZS, D)
    shift = mem(Map.ZS + D, 2, D)
    scale = mem(Map.GB, 2, D)
    mod = mem(Map.MG, 4, D, rows=NC_ROWS)
    hT = mem(Map.HT, KD, T)
    ident = mem(Map.IDENT, P)

    s_c, s_bias, s_x, s_g = sem("cd_c"), sem("cd_bias"), sem("cd_x"), sem("cd_g")
    s_w = [sem(f"cd_w{i}") for i in range(4)]
    s_silu, s_cps, s_cT = sem("cd_silu"), sem("cd_cps"), sem("cd_cT")
    s_mm, s_mod = sem("cd_mm"), sem("cd_mod")
    s_modw = [sem(f"cd_modw{i}") for i in range(4)]
    s_rows = sem("cd_rows")
    s_zero, s_sq, s_var, s_rstd = sem("cd_zero"), sem("cd_sq"), sem("cd_var"), sem("cd_rstd")
    s_h, s_hps, s_hT = sem("cd_h"), sem("cd_hps"), sem("cd_hT")
    s_dve = sem("cd_dve")
    NCH = NMOD * D // 512
    hparts = [(b, half) for b in range(5) for half in range(2)]

    def rows_of(b):
        return P if b < NB else NS

    with nc.Block() as block:
        @block.sync
        def _(sp):
            sp.dma_start(c[0:NS, :], A["c_sample"]).then_inc(s_c, 16)
            sp.dma_start(c[NS:NC_ROWS, :], A["c_prompt"]).then_inc(s_c, 16)
            wa = A["w_ada"][0].rearrange("(k p) n -> p k n", p=P)
            wf = A["w_ada_final"].rearrange("(k p) n -> p k n", p=P)

            def load_w(i):
                src = wa[:, :, i * 512:(i + 1) * 512] if i < 12 else wf[:, :, (i - 12) * 512:(i - 11) * 512]
                if i >= 4:
                    sp.wait_ge(s_mm, i - 3)
                sp.dma_start(ring[i % 4], src).then_inc(s_w[i % 4], 16)

            load_w(0)
            sp.dma_start(bias[:, 0:6 * D], A["b_ada"][0:1, :].partition_broadcast(NC_ROWS)).then_inc(s_bias, 16)
            sp.dma_start(bias[:, 6 * D:], A["b_ada_final"].rearrange("(a n) -> a n", a=1)
                         .partition_broadcast(NC_ROWS)).then_inc(s_bias, 16)
            load_w(1)
            sp.dma_start(x[:, 0:NB, :], A["x_prompt"][0].rearrange("(b p) d -> p b d", p=P)).then_inc(s_x, 16)
            sp.dma_start(x[0:NS, NB, :], A["x_sample"].rearrange("b s d -> (b s) d")).then_inc(s_x, 16)
            sp.dma_start(g1, A["g_norm1"][0:1, :].partition_broadcast(P)).then_inc(s_g, 16)
            for i in range(2, NCH):
                load_w(i)

        @block.scalar
        def _(act):
            act.wait_ge(s_c, 32)
            nc.scalar.activation(sc, c, ACT.Silu).then_inc(s_silu, 1)
            act.wait_ge(s_x, 32)
            act.wait_ge(s_zero, 1)
            junk = mem(Map.HT, D)
            for b in range(5):
                n = rows_of(b)
                nc.scalar.activation(junk[0:n, :], x[0:n, b, :], ACT.Square,
                                     accum_out=stat[0:n, b:b + 1]).then_inc(s_sq, 1)
                act.wait_ge(s_sq, b + 1)
            act.wait_ge(s_var, 1)
            nc.scalar.activation(rstd, stat, ACT.Sqrt).then_inc(s_rstd, 1)

            def store_mod(m):
                act.wait_ge(s_mod, 2 * m + 2)
                act.dma_start(mod_d[:, m * D:(m + 1) * D], mod[:, m % 4, :]).then_inc(s_modw[m % 4], 16)

            store_mod(0)
            store_mod(1)
            act.wait_ge(s_modw[0], 16)
            act.wait_ge(s_modw[1], 16)
            for dst, m in ((shift, 0), (scale, 1)):
                act.dma_start(dst[:, 0, :], mod_d[NS:NC_ROWS, m * D:(m + 1) * D].partition_broadcast(P)).then_inc(s_rows, 16)
                act.dma_start(dst[0:NS, 1, :], mod_d[0:NS, m * D:(m + 1) * D]).then_inc(s_rows, 16)
            for m in range(2, NMOD):
                store_mod(m)
            for n, (b, half) in enumerate(hparts):
                act.wait_ge(s_hps, n + 1)
                m = rows_of(b)
                nc.scalar.activation(hT[:, 4 * half:4 * half + 4, b * P:b * P + m],
                                     ps[:, 4 + n % 4, :].rearrange("p (k t) -> p k t", k=4)[:, :, 0:m],
                                     ACT.Copy).then_inc(s_hT, 1)
            for w in s_modw:
                act.wait_ge(w, 16 * NMOD // 4)

        @block.tensor
        def _(pe):
            pe.wait_ge(s_silu, 1)
            for k in range(KD):
                last = nc.tensor.transpose(ps[:, 4, k * 16:k * 16 + NC_ROWS], sc[:, k * P:(k + 1) * P],
                                           ident[0:NC_ROWS, 0:NC_ROWS])
            last.then_inc(s_cps, 1)
            pe.wait_ge(s_cT, 1)
            for i in range(NCH):
                pe.wait_ge(s_w[i % 4], 16 * (i // 4 + 1))
                if i >= 4:
                    pe.wait_ge(s_mod, i - 3)
                for k in range(KD):
                    last = nc.tensor.matmul(ps[0:NC_ROWS, i % 4, :], cT[:, k, :], ring[i % 4][:, k, :],
                                            start=(k == 0), stop=(k == KD - 1))
                last.then_inc(s_mm, 1)
            for n, (b, half) in enumerate(hparts):
                pe.wait_ge(s_h, b + 1)
                if n >= 4:
                    pe.wait_ge(s_hT, n - 3)
                m = rows_of(b)
                for k in range(4):
                    kk = 4 * half + k
                    last = nc.tensor.transpose(ps[:, 4 + n % 4, k * P:k * P + m],
                                               x[0:m, b, kk * P:(kk + 1) * P], ident[0:m, 0:m])
                last.then_inc(s_hps, 1)

        @block.vector
        def _(dve):
            link = Link(dve, s_dve)
            nc.vector.memset(stat, 1.0).then_inc(s_zero, 1)
            dve.wait_ge(s_cps, 1)
            nc.vector.tensor_copy(cT, ps[:, 4, 0:KD * 16].rearrange("p (k c) -> p k c", c=16)[:, :, 0:NC_ROWS])\
                .then_inc(s_cT, 1)
            dve.wait_ge(s_sq, 5)
            link(nc.vector.tensor_scalar(stat, stat, 1.0 / D, EPS, ALU.mult, ALU.add))
            nc.vector.reciprocal(stat, stat).then_inc(s_var, 1)
            dve.wait_ge(s_bias, 32)

            def evict(i):
                dve.wait_ge(s_mm, i + 1)
                if i >= 8:
                    dve.wait_ge(s_modw[(i // 2) % 4], 16)
                nc.vector.tensor_tensor(mod[:, (i // 2) % 4, (i % 2) * 512:(i % 2 + 1) * 512],
                                        ps[0:NC_ROWS, i % 4, :], bias[:, i * 512:(i + 1) * 512],
                                        ALU.add).then_inc(s_mod, 1)

            for i in range(6):
                evict(i)
            dve.wait_ge(s_rstd, 1)
            dve.wait_ge(s_g, 16)
            dve.wait_ge(s_rows, 64)
            link(nc.vector.scalar_tensor_tensor(out=scale[:, 0, :], in0=scale[:, 0, :], scalar=1.0, in1=g1,
                                                op0=ALU.add, op1=ALU.mult))
            link(nc.vector.scalar_tensor_tensor(out=scale[0:NS, 1, :], in0=scale[0:NS, 1, :], scalar=1.0,
                                                in1=g1[0:NS, :], op0=ALU.add, op1=ALU.mult))
            for b in range(5):
                n, r = rows_of(b), b // NB
                link(nc.vector.scalar_tensor_tensor(out=x[0:n, b, :], in0=x[0:n, b, :], scalar=rstd[0:n, b:b + 1],
                                                    in1=scale[0:n, r, :], op0=ALU.mult, op1=ALU.mult))
                nc.vector.tensor_tensor(x[0:n, b, :], x[0:n, b, :], shift[0:n, r, :], ALU.add).then_inc(s_h, 1)
                evict(6 + 2 * b)
                evict(7 + 2 * b)


C_U, C_Z, C_X, C_DT, C_G = 0, S5W, S5W + D, S5W + D + CD, S5W + D + CD + NH
TWO_PI = 2.0 * math.pi
CW1 = 6.28125
CW2 = float(np.float32(int((TWO_PI - CW1) * 2 ** 20) / 2 ** 20))
CW3 = TWO_PI - CW1 - CW2
ROUND = 1.5 * 2.0 ** 23
NLEV = 9
V_MAG, V_AR, V_AI, V_FR, V_FI, V_COS = 0, 1, 2, 3, 4, 5
V_SIN = V_COS + NLEV
NV = V_SIN + NLEV


def stage_s5(nc, mem, sem, ps, A, O):
    hT, zs, gB, mg = (mem(m, KD, T) for m in (Map.HT, Map.ZS, Map.GB, Map.MG))
    ident = mem(Map.IDENT, P)
    M = Map.LOCAL

    def take(n):
        nonlocal M
        M += n
        return M - n

    gA = mem(take(KD * T), KD, T)
    ring = [mem(take(KD * 512), KD, 512) for _ in range(2)]
    tabs = take(2 * NS5 * TB5)
    RC, RS = mem(tabs, NS5, TB5), mem(tabs + NS5 * TB5, NS5, TB5)
    u = mem(take(4 * T), 4, T)
    LB = mem(take(2 * 4 * P), 2, 4, P)
    CTW = NS5 * P + P
    ct = take(2 * CTW)
    CT = [mem(ct + i * CTW, NS5, P) for i in range(2)]
    parbase = Map.ZS
    par = mem(parbase, NV, P, rows=NS5)
    PT = mem(take(NV * NS5), NV, NS5)
    tmp = Map.ZS + NV * P
    ye = take(4 * 512)
    vec = mem(take(P), P, rows=8)
    vT = mem(take(8), 8)
    ldt = mem(take(8), 8, rows=NS5)
    fin = mem(take(2 * NS5), 2, NS5)
    work = take(8 * 512)
    s0 = mem(work + 2560, 2, P)
    s0T = mem(take(2 * P), 2, P)
    sn = mem(take(2 * P), 2, NS, NS5)
    so = mem(work + 2048, 2, P)
    fo = mem(work + 2304, 2, P, rows=NS5)
    mark = mem(take(1), 1)
    assert M <= Map.W, M
    bn = mem(work, 2, NS5, G5)
    bb = mem(work + 512, 2, NS5, G5)
    t16 = mem(work + 1024, NS5, G5)
    cn = mem(work + 1536, 2, 4, P)
    X = mem(Map.LOCAL, 2, NS5 * P)
    X3 = mem(Map.LOCAL, 2 * NS5, P)
    tt = [mem(work + i * 2048, NS5, P) for i in range(2)]
    wk = [mem(work + i * 512, 2, 256) for i in range(8)]
    yg = mem(tabs, 4, T)
    ya = mem(tabs + 4 * T, 4, T)
    sg = mem(tabs + 8 * T, T)

    s_par, s_vec, s_bc, s_st = sem("s5_par"), sem("s5_vec"), sem("s5_bc"), sem("s5_st")
    s_w = [sem(f"s5_w{i}") for i in range(2)]
    s_proj, s_pev = sem("s5_proj"), sem("s5_pev")
    s_exp, s_ang, s_trig, s_parok = sem("s5_exp"), sem("s5_ang"), sem("s5_trig"), sem("s5_parok")
    s_tps, s_PT, s_X, s_Xps, s_LB = sem("s5_tps"), sem("s5_PT"), sem("s5_X"), sem("s5_Xps"), sem("s5_LB")
    s_cps, s_CT, s_zero = sem("s5_cps"), sem("s5_CT"), sem("s5_zero")
    s_bu, s_buread, s_S, s_Sread = sem("s5_bu"), sem("s5_buread"), sem("s5_S"), sem("s5_Sread")
    s_y, s_yread, s_g, s_gelu = sem("s5_y"), sem("s5_yread"), sem("s5_g"), sem("s5_gelu")
    s_new, s_glu, s_sig, s_ya, s_br, s_brread = (sem("s5_" + n) for n in ("new", "glu", "sig", "ya", "br", "brread"))
    s_ops, s_ocp, s_out, s_dve, s_act, s_fin = (sem("s5_" + n) for n in ("ops", "ocp", "out", "dve", "act", "fin"))
    s_wg, s_wbr = sem("s5_wg"), sem("s5_wbr")

    dest = ([(u[:, i, :], ACT.Copy) for i in range(4)] + [(zs[:, i, :], ACT.Silu) for i in range(KD)]
            + [(gA[:, i, :], ACT.Sigmoid) for i in range(KD)] + [(gB[:, i, :], ACT.Sigmoid) for i in range(KD)])
    col0 = [C_U, C_Z, C_Z + 512, C_G, C_G + 512, C_G + D, C_G + D + 512]
    NP = len(dest)
    glu_w = mem(0 + Map.LOCAL + KD * T, 4, 512)
    br_w = mem(Map.LOCAL + KD * T + KD * 512, 4, D)

    def S_of(i):
        return (wk[4 + 2 * (i % 2)], wk[5 + 2 * (i % 2)])

    with nc.Block() as block:
        @block.sync
        def _(sp):
            w = A["w_in"][0].rearrange("(k p) n -> p k n", p=P)
            sp.dma_start(ring[0], w[:, :, C_U:C_U + 512]).then_inc(s_w[0], 16)
            for v, name in ((V_AR, "s5_a_re"), (V_AI, "s5_a_im")):
                sp.dma_start(par[:, v, :], A[name][0].rearrange("(s g) p -> s (g p)", g=2)).then_inc(s_par, 16)
            sp.dma_start(ldt[:, 0:2], A["s5_log_dt"][0].rearrange("(s g) -> s g", g=2)).then_inc(s_par, 16)
            sp.dma_start(vec[0:4, :], A["s5_d"][0].rearrange("(u g) h -> u (g h)", u=4)).then_inc(s_vec, 16)
            sp.dma_start(vec[4:8, :], A["s5_b_glu"][0].rearrange("(u c) -> u c", u=4)).then_inc(s_vec, 16)
            for i, (b, c) in enumerate((("s5_b_re", "s5_c_re"), ("s5_b_im", "s5_c_im"))):
                sp.dma_start(bn[:, i, :, :], A[b][0].rearrange("(s g) p h -> (g p) s h", g=2)).then_inc(s_bc, 16)
                for dup in range(2):
                    sp.dma_start(cn[:, i, :, dup * 64:dup * 64 + 64],
                                 A[c][0].rearrange("(u g) h p -> (g h) u p", u=4)).then_inc(s_bc, 16)
            for i, name in enumerate(("state_s5_re", "state_s5_im")):
                sp.dma_start(s0[:, i, :], A[name][0].rearrange("b (s g) p -> (b s) (g p)", g=2)).then_inc(s_st, 16)
            for i in range(1, 7):
                if i >= 2:
                    sp.wait_ge(s_proj, 4 * (i - 1))
                sp.dma_start(ring[i % 2], w[:, :, col0[i]:col0[i] + 512]).then_inc(s_w[i % 2], 16)
            sp.wait_ge(s_proj, NP)
            sp.dma_start(glu_w, A["s5_w_glu"][0].rearrange("(k p) n -> p k n", p=P)).then_inc(s_wg, 16)
            sp.dma_start(br_w, A["w_branch_a"][0].rearrange("(k p) n -> p k n", p=P)).then_inc(s_wbr, 16)
            sp.wait_ge(s_ocp, 4)
            for i in range(2):
                sp.dma_start(O[2 + i][0, 0].rearrange("(s g) p -> s (g p)", g=2), fo[:, i, :]).then_inc(s_out, 16)
                sp.dma_start(O[6 + i][0].rearrange("b (s g) p -> (b s) (g p)", g=2), so[:, i, :]).then_inc(s_out, 16)
            sp.wait_ge(s_out, 64)

        @block.gpsimd
        def _(pool):
            nc.gpsimd.memset(mem(ct, 2 * CTW), 0.0).then_inc(s_zero, 1)

        @block.scalar
        def _(act):
            link = Link(act, s_act)

            def evict(n):
                act.wait_ge(s_proj, n + 1)
                nc.scalar.activation(cols(dest[n][0]), two(ps[:, 5:7, :]), dest[n][1]).then_inc(s_pev, 1)

            act.wait_ge(s_par, 48)
            nc.scalar.activation(ldt[:, 2:4], ldt[:, 0:2], ACT.Exp).then_inc(s_exp, 1)
            act.wait_ge(s_ang, 1)
            nc.scalar.activation(par[:, V_MAG, :], par[:, V_MAG, :], ACT.Exp).then_inc(s_exp, 1)
            for n in range(4):
                evict(n)
            act.wait_ge(s_ang, 2)
            sc = mem(parbase + V_COS * P, 2 * NLEV * P, rows=NS5)
            nc.scalar.activation(sc, sc, ACT.Sin).then_inc(s_trig, 1)
            act.wait_ge(s_Xps, 1)
            for i in range(2):
                nc.scalar.activation(LB[:, i, :, :], ps[:, i, :].rearrange("p (u n) -> p u n", u=4),
                                     ACT.Copy).then_inc(s_LB, 1)
            act.wait_ge(s_cps, 1)
            act.wait_ge(s_zero, 1)
            for i in range(2):
                for ut in range(4):
                    for half in range(2):
                        rows = slice(64 * half, 64 * half + 64)
                        dst = mem(ct + i * CTW + 512 * ut, 4, 160)[rows, :, 16 * half:16 * half + 16]
                        src = ps[rows, 2 + i, ut * P:(ut + 1) * P].rearrange("p (q r) -> p q r", q=4)[
                            :, :, 16 * half:16 * half + 16]
                        nc.scalar.activation(dst, src, ACT.Copy, scale=1.0 - 2.0 * i).then_inc(s_CT, 1)
            n = 4
            for i in range(NS5):
                for _ in range(2 if i % 2 else 1):
                    evict(n)
                    n += 1
                act.wait_ge(s_S, i + 1)
                for j in range(2):
                    nc.scalar.activation(fin[:, j, i:i + 1], S_of(i)[j][:, 1, 255:256], ACT.Copy).then_inc(s_fin, 1)
            assert n == NP
            for ut in range(4):
                act.wait_ge(s_g, ut + 1)
                nc.scalar.activation(yg[:, ut, 0:L], yg[:, ut, 0:L], ACT.Gelu).then_inc(s_gelu, 1)
            act.wait_ge(s_g, 5)
            nc.scalar.activation(yg[:, :, L:T], yg[:, :, L:T], ACT.Gelu).then_inc(s_gelu, 1)
            for m in range(4):
                act.wait_ge(s_glu, m + 1)
                if m:
                    act.wait_ge(s_ya, m)
                nc.scalar.activation(cols(sg), two(ps[:, 2 * (m % 2):2 * (m % 2) + 2, :]), ACT.Sigmoid,
                                     bias=vT[:, 4 + m:5 + m]).then_inc(s_sig, 1)
            act.wait_ge(s_ops, 1)
            for i in range(2):
                nc.scalar.activation(fo[:, i, :], ps[0:NS5, 4, i * P:(i + 1) * P], ACT.Copy).then_inc(s_ocp, 1)
                nc.scalar.activation(so[:, i, :], ps[:, 4, (2 + i) * P:(3 + i) * P], ACT.Copy).then_inc(s_ocp, 1)

        @block.tensor
        def _(pe):
            def proj(n):
                i, m = n // 4, n % 4
                if m == 0:
                    pe.wait_ge(s_w[i % 2], 16 * (i // 2 + 1))
                if n:
                    pe.wait_ge(s_pev, n)
                for k in range(KD):
                    for h in range(2):
                        last = nc.tensor.matmul(ps[:, 5 + h, 0:HALF], ring[i % 2][:, k, m * P:(m + 1) * P],
                                                hT[:, k, h * HALF:(h + 1) * HALF], start=(k == 0), stop=(k == KD - 1))
                last.then_inc(s_proj, 1)

            for n in range(4):
                proj(n)
            pe.wait_ge(s_parok, 1)
            for v in range(NV):
                last = nc.tensor.transpose(ps[:, 4, v * NS5:(v + 1) * NS5], par[:, v, :], ident[0:NS5, 0:NS5])
            pe.wait_ge(s_vec, 32)
            last = nc.tensor.transpose(ps[:, 4, NV * NS5:NV * NS5 + 8], vec, ident[0:8, 0:8])
            pe.wait_ge(s_st, 32)
            for i in range(2):
                last = nc.tensor.transpose(ps[:, 7, i * P:(i + 1) * P], s0[:, i, :], ident)
            last.then_inc(s_tps, 1)
            pe.wait_ge(s_X, 1)
            for i in range(2):
                for ut in range(4):
                    for q in range(4):
                        last = nc.tensor.matmul(ps[:, i, ut * P:(ut + 1) * P], X3[:, NS5 * i + 4 * ut + q, :], ident,
                                                start=(q == 0), stop=(q == 3))
            last.then_inc(s_Xps, 1)
            pe.wait_ge(s_bc, 96)
            for i in range(2):
                for ut in range(4):
                    last = nc.tensor.transpose(ps[:, 2 + i, ut * P:(ut + 1) * P], cn[:, i, ut, :], ident)
            last.then_inc(s_cps, 1)

            def bu(i):
                if i == 0:
                    pe.wait_ge(s_LB, 2)
                    pe.wait_ge(s_PT, 1)
                    pe.wait_ge(s_pev, 4)
                if i == 1:
                    pe.wait_ge(s_CT, 16)
                if i >= 2:
                    pe.wait_ge(s_buread, i - 1)
                ut, q = i // 4, i % 4
                rows = slice(32 * q, 32 * q + 32)
                for j in range(2):
                    nc.tensor.matmul(ps[:, 2 * (i % 2) + j, :], LB[rows, j, ut, :], u[rows, ut, 0:L],
                                     start=True, stop=True)
                if i:
                    pe.wait_ge(s_bu, i)
                for j in range(2):
                    last = nc.tensor.matmul(ps[:, 4, j * P + i * NS:j * P + (i + 1) * NS], LB[rows, j, ut, :],
                                            u[rows, ut, L:T], start=True, stop=True)
                last.then_inc(s_bu, 1)

            def y(i):
                ut, q = i // 4, i % 4
                pe.wait_ge(s_S, i + 1)
                if q == 0 and ut:
                    pe.wait_ge(s_yread, ut)
                for j in range(2):
                    last = nc.tensor.matmul(ps[:, 7, :], CT[j][:, i, :], S_of(i)[j].rearrange("p a b -> p (a b)"),
                                            start=(q == 0 and j == 0), stop=(q == 3 and j == 1))
                last.then_inc(s_y, 1)

            n = 4
            bu(0)
            for i in range(NS5):
                for _ in range(2 if i % 2 else 1):
                    proj(n)
                    n += 1
                if i + 1 < NS5:
                    bu(i + 1)
                if i >= 1:
                    y(i - 1)
            y(NS5 - 1)
            pe.wait_ge(s_new, 1)
            for ut in range(4):
                for q in range(4):
                    for j in range(2):
                        last = nc.tensor.matmul(ps[:, 3, ut * NS:(ut + 1) * NS], CT[j][:, 4 * ut + q, :],
                                                sn[:, j, :, 4 * ut + q], start=(q == 0 and j == 0),
                                                stop=(q == 3 and j == 1))
            last.then_inc(s_y, 1)
            pe.wait_ge(s_fin, 2 * NS5)
            for i in range(2):
                nc.tensor.transpose(ps[0:NS5, 4, i * P:(i + 1) * P], fin[:, i, :], ident)
                last = nc.tensor.transpose(ps[:, 4, (2 + i) * P:(3 + i) * P],
                                           sn[:, i, :, :].rearrange("p b s -> p (b s)"), ident)
            last.then_inc(s_ops, 1)
            pe.wait_ge(s_gelu, 5)
            pe.wait_ge(s_wg, 16)
            for m in range(4):
                if m >= 2:
                    pe.wait_ge(s_sig, m - 1)
                for k in range(4):
                    for h in range(2):
                        last = nc.tensor.matmul(ps[:, 2 * (m % 2) + h, 0:HALF], glu_w[:, k, m * P:(m + 1) * P],
                                                yg[:, k, h * HALF:(h + 1) * HALF], start=(k == 0), stop=(k == 3))
                last.then_inc(s_glu, 1)
            pe.wait_ge(s_ya, 4)
            pe.wait_ge(s_wbr, 16)
            for m in range(KD):
                if m >= 2:
                    pe.wait_ge(s_brread, m - 1)
                for k in range(4):
                    for h in range(2):
                        last = nc.tensor.matmul(ps[:, 2 * (m % 2) + h, 0:HALF], br_w[:, k, m * P:(m + 1) * P],
                                                ya[:, k, h * HALF:(h + 1) * HALF], start=(k == 0), stop=(k == 3))
                last.then_inc(s_br, 1)

        @block.vector
        def _(dve):
            link = Link(dve, s_dve)
            V = nc.vector
            t = [mem(tmp + i * P, P, rows=NS5) for i in range(8)]
            ar, ai, mag = par[:, V_AR, :], par[:, V_AI, :], par[:, V_MAG, :]
            dve.wait_ge(s_exp, 1)
            dtb = ldt[:, 2:4].unsqueeze(2).to_broadcast([NS5, 2, 64])
            g2 = lambda x: x.rearrange("p (g n) -> p g n", g=2)
            V.tensor_tensor(g2(mag), g2(ar), dtb, ALU.mult).then_inc(s_ang, 1)
            link(V.tensor_tensor(g2(t[0]), g2(ai), dtb, ALU.mult))
            for j in range(NLEV):
                s, c = par[:, V_SIN + j, :], par[:, V_COS + j, :]
                link(V.tensor_scalar(t[1], t[0], 2.0 ** j / TWO_PI, ROUND, ALU.mult, ALU.add))
                link(V.tensor_scalar(t[1], t[1], ROUND, None, ALU.subtract))
                link(V.tensor_scalar(s, t[0], 2.0 ** j, None, ALU.mult))
                for cw in (CW1, CW2, CW3):
                    link(V.scalar_tensor_tensor(out=s, in0=t[1], scalar=-cw, in1=s, op0=ALU.mult, op1=ALU.add))
                link(V.tensor_scalar(s, s, 3.1415925, -3.1415925, ALU.min, ALU.max))
                link(V.tensor_scalar(t[2], s, -1.0, None, ALU.mult))
                link(V.tensor_tensor(t[2], t[2], s, ALU.max))
                link(V.tensor_scalar(c, t[2], -1.0, math.pi / 2, ALU.mult, ALU.add))
            V.memset(t[3], 0.0).then_inc(s_ang, 1)
            link(V.tensor_tensor(t[4], ar, ar, ALU.mult))
            link(V.tensor_tensor(t[5], ai, ai, ALU.mult))
            link(V.tensor_tensor(t[4], t[4], t[5], ALU.add))
            link(V.reciprocal(t[4], t[4]))
            dve.wait_ge(s_trig, 1)
            dve.wait_ge(s_exp, 2)
            link(V.tensor_tensor(t[0], mag, par[:, V_COS, :], ALU.mult))
            link(V.tensor_tensor(t[1], mag, par[:, V_SIN, :], ALU.mult))
            link(V.tensor_scalar(t[2], t[0], -1.0, None, ALU.add))
            fr, fi = par[:, V_FR, :], par[:, V_FI, :]
            link(V.tensor_tensor(t[5], t[2], ar, ALU.mult))
            link(V.tensor_tensor(t[6], t[1], ai, ALU.mult))
            link(V.tensor_tensor(t[5], t[5], t[6], ALU.add))
            link(V.tensor_tensor(fr, t[5], t[4], ALU.mult))
            link(V.tensor_tensor(t[5], t[1], ar, ALU.mult))
            link(V.tensor_tensor(t[6], t[2], ai, ALU.mult))
            link(V.tensor_tensor(t[5], t[5], t[6], ALU.subtract))
            link(V.tensor_tensor(fi, t[5], t[4], ALU.mult))
            link(V.tensor_copy(ar, t[0]))
            V.tensor_copy(ai, t[1]).then_inc(s_parok, 1)
            link(V.memset(X, 0.0))
            dve.wait_ge(s_tps, 1)
            link(V.tensor_copy(vT, ps[:, 4, NV * NS5:NV * NS5 + 8]))
            link(V.tensor_copy(s0T, ps[:, 7, 0:2 * P].rearrange("p (i n) -> p i n", i=2)))
            V.tensor_copy(PT, ps[:, 4, 0:NV * NS5].rearrange("p (v s) -> p v s", v=NV)).then_inc(s_PT, 1)
            dve.wait_ge(s_PT, 1)
            dve.wait_ge(s_bc, 96)
            frb, fib = (PT[:, v, :].unsqueeze(2).to_broadcast([P, NS5, G5]) for v in (V_FR, V_FI))
            for j, (p, q, op) in enumerate(((0, 1, ALU.subtract), (1, 0, ALU.add))):
                link(V.tensor_tensor(bb[:, j, :, :], frb, bn[:, p, :, :], ALU.mult))
                link(V.tensor_tensor(t16, fib, bn[:, q, :, :], ALU.mult))
                link(V.tensor_tensor(bb[:, j, :, :], bb[:, j, :, :], t16, op))
            for j in range(2):
                for ut in range(4):
                    for g in range(2):
                        rows = slice(64 * g, 64 * g + 64)
                        flat = X[rows, j, 512 * ut:512 * ut + 512]
                        for q in range(4):
                            last = V.tensor_copy(flat[:, 160 * q + 16 * g:160 * q + 16 * g + 16],
                                                 bb[rows, j, 4 * ut + q, :])
                            link(last)
            V.memset(t[7], 0.0).then_inc(s_X, 1)
            link(V.memset(RC[:, :, 0:1], 1.0))
            link(V.memset(RS[:, :, 0:1], 0.0))
            dve.wait_ge(s_cps, 1)
            for j in range(NLEV - 1):
                m = 2 ** j
                ec, es = (PT[:, v + j, :].unsqueeze(2).to_broadcast([P, NS5, m]) for v in (V_COS, V_SIN))
                a, b = tt[0][:, :, 0:m], tt[1][:, :, 0:m]
                link(V.tensor_tensor(a, RC[:, :, 0:m], ec, ALU.mult))
                link(V.tensor_tensor(b, RS[:, :, 0:m], es, ALU.mult))
                link(V.tensor_tensor(RC[:, :, m:2 * m], a, b, ALU.subtract))
                link(V.tensor_tensor(a, RC[:, :, 0:m], es, ALU.mult))
                link(V.tensor_tensor(b, RS[:, :, 0:m], ec, ALU.mult))
                link(V.tensor_tensor(RS[:, :, m:2 * m], a, b, ALU.add))

            def y_of(ut):
                dve.wait_ge(s_y, 4 * ut + 4)
                V.scalar_tensor_tensor(out=yg_early(ut), in0=u[:, ut, 0:L], scalar=vT[:, ut:ut + 1], in1=ps[:, 7, :],
                                       op0=ALU.mult, op1=ALU.add).then_inc(s_yread, 1)

            def yg_early(ut):
                return mem(ye + ut * 512, 512)

            for i in range(NS5):
                br, bi = (ps[:, 2 * (i % 2) + j, :].rearrange("p (a b) -> p a b", a=2) for j in range(2))
                c, s = (x[:, i:i + 1, :].to_broadcast([P, 2, TB5]) for x in (RC, RS))
                wr, wi, t1, t2 = wk[0], wk[1], wk[2], wk[3]
                sr, si = S_of(i)
                dve.wait_ge(s_bu, i + 1)
                link(V.tensor_tensor(t1, br, c, ALU.mult))
                link(V.tensor_tensor(t2, bi, s, ALU.mult))
                link(V.tensor_tensor(wr, t1, t2, ALU.add))
                link(V.tensor_tensor(t1, bi, c, ALU.mult))
                V.tensor_tensor(t2, br, s, ALU.mult).then_inc(s_buread, 1)
                dve.wait_ge(s_buread, i + 1)
                link(V.tensor_tensor(wi, t1, t2, ALU.subtract))
                magb = PT[:, V_MAG, i:i + 1].to_broadcast([P, TB5])
                ec, es = PT[:, V_COS + NLEV - 1, i:i + 1], PT[:, V_SIN + NLEV - 1, i:i + 1]
                link(V.tensor_tensor_scan(wr[:, 0, :], magb, wr[:, 0, :], 0.0, ALU.mult, ALU.add))
                link(V.tensor_tensor_scan(wi[:, 0, :], magb, wi[:, 0, :], 0.0, ALU.mult, ALU.add))
                er, ei = wr[:, 0, 255:256], wi[:, 0, 255:256]
                q = [t1[:, 0, x:x + 1] for x in range(4)]
                link(V.tensor_tensor(q[0], ei, es, ALU.mult))
                link(V.tensor_tensor(q[1], ei, ec, ALU.mult))
                link(V.scalar_tensor_tensor(out=q[2], in0=er, scalar=ec, in1=q[0], op0=ALU.mult, op1=ALU.subtract))
                link(V.scalar_tensor_tensor(out=q[3], in0=er, scalar=es, in1=q[1], op0=ALU.mult, op1=ALU.add))
                link(V.tensor_tensor_scan(wr[:, 1, :], magb, wr[:, 1, :], q[2], ALU.mult, ALU.add))
                link(V.tensor_tensor_scan(wi[:, 1, :], magb, wi[:, 1, :], q[3], ALU.mult, ALU.add))
                if i >= 2:
                    dve.wait_ge(s_y, i - 1)
                    dve.wait_ge(s_fin, 2 * (i - 1))
                link(V.tensor_tensor(t1, wr, c, ALU.mult))
                link(V.tensor_tensor(t2, wi, s, ALU.mult))
                link(V.tensor_tensor(sr, t1, t2, ALU.subtract))
                link(V.tensor_tensor(t1, wr, s, ALU.mult))
                link(V.tensor_tensor(t2, wi, c, ALU.mult))
                V.tensor_tensor(si, t1, t2, ALU.add).then_inc(s_S, 1)
                dve.wait_ge(s_S, i + 1)
                if i >= 4 and i % 4 == 1:
                    y_of(i // 4 - 1)
            y_of(3)
            dve.wait_ge(s_yread, 4)
            bus = [ps[:, 4, j * P:(j + 1) * P].rearrange("p (s b) -> p s b", b=NS) for j in range(2)]
            old = [s0T[:, j, :].rearrange("p (b s) -> p s b", s=NS5) for j in range(2)]
            new = [sn[:, j, :, :].rearrange("p b s -> p s b") for j in range(2)]
            abr, abi = (PT[:, v, :].unsqueeze(2).to_broadcast([P, NS5, NS]) for v in (V_AR, V_AI))
            w1, w2 = (mem(work + 1024 + x * P, NS5, NS) for x in range(2))
            for j, (p, q, op) in enumerate(((0, 1, ALU.subtract), (1, 0, ALU.add))):
                link(V.tensor_tensor(w1, abr, old[p], ALU.mult))
                link(V.tensor_tensor(w2, abi, old[q], ALU.mult))
                link(V.tensor_tensor(w1, w1, w2, op))
                link(V.tensor_tensor(new[j], w1, bus[j], ALU.add))
            V.memset(mark, 0.0).then_inc(s_new, 1)
            for ut in range(4):
                V.tensor_copy(yg[:, ut, 0:L], yg_early(ut)).then_inc(s_g, 1)
            dve.wait_ge(s_y, NS5 + 1)
            for ut in range(4):
                last = V.scalar_tensor_tensor(out=yg[:, ut, L:T], in0=u[:, ut, L:T], scalar=vT[:, ut:ut + 1],
                                              in1=ps[:, 3, ut * NS:(ut + 1) * NS], op0=ALU.mult, op1=ALU.add)
                if ut < 3:
                    link(last)
            last.then_inc(s_g, 1)
            for m in range(4):
                dve.wait_ge(s_sig, m + 1)
                V.tensor_tensor(ya[:, m, :], yg[:, m, :], sg, ALU.mult).then_inc(s_ya, 1)
            for m in range(KD):
                dve.wait_ge(s_br, m + 1)
                V.tensor_tensor(cols(mg[:, m, :]), two(ps[:, 2 * (m % 2):2 * (m % 2) + 2, :]),
                                cols(gA[:, m, :]), ALU.mult).then_inc(s_brread, 1)


def stage_ssd(nc, mem, sem, ps, A, O):
    hT, zs, gB, mg = (mem(m, KD, T) for m in (Map.HT, Map.ZS, Map.GB, Map.MG))
    ident, ones = mem(Map.IDENT, P), mem(Map.ONES, P)
    M = Map.LOCAL

    def take(n):
        nonlocal M
        M += n
        return M - n

    cv = mem(take(NCV * T), NCV, T)
    ring_at = take(2 * KD * 512)
    ring = [mem(ring_at + i * KD * 512, KD, 512) for i in range(2)]
    brw = mem(ring_at, KD, D)
    raw = [mem(take(528), 528) for _ in range(2)]
    scr = take(10240)
    ecs, lm, cs_c = mem(scr, NH, P), mem(scr + 2048, NH, P), mem(scr + 4096, NH, P)
    xdt, xdd = mem(scr + 6144, NH, HD), mem(scr + 7168, NH, HD)
    btm, cbm = mem(scr + 8192, NGR, P), mem(scr + 8704, NGR, P)
    st = mem(scr + 9216, NH, HD)
    sel = mem(take(NH * P), NH, P, rows=NH)
    ek = mem(take(KD * P), KD, P, rows=NH)
    mask = mem(take(P), P)
    vn = mem(scr + 4096, P, rows=88)
    vT = mem(take(88), 88)
    hn = mem(scr, CD, rows=3 * NS)
    hist = mem(take(NCV * 3 * NS), NCV, 3 * NS)
    tail = mem(take(NCV * 11), NCV, 11)
    tl = mem(scr + 7168, CD, rows=11)
    dtw = mem(take(KD * NH), KD, NH)
    hp = mem(take(8), 8, rows=NH)
    dtv, csv = mem(take(T), T, rows=NH), mem(take(L), L, rows=NH)
    rex = mem(take(17), 17, rows=NH)
    ex = mem(take(KD * 17), KD, 17)
    tm = mem(take(P), NB, 2, NH)
    xs_s = mem(take(KD * NS), KD, NS)
    ys_s = mem(take(KD * NS), KD, NS)
    bcs = mem(scr, D, rows=NS)
    h0 = [mem(scr + 1024 + i * 1024, KD, SN) for i in range(3)]
    tb = mem(scr + 4096, KD, SN)
    hout = mem(scr + 5120, KD, SN)
    sq = mem(scr, 2, T)
    rs = mem(scr + 2 * T, T)
    tmpo = mem(scr + 3 * T, T)
    dtt = [mem(scr + 6144 + i * T, T, rows=NH) for i in range(6)]
    assert M <= Map.W, M
    CW, CB, GN = 0, 4 * NCV, 5 * NCV

    s_w = [sem(f"sd_w{i}") for i in range(2)]
    (s_dtw, s_vn, s_hn, s_hp, s_brw) = (sem("sd_" + n) for n in ("dtw", "vn", "hn", "hp", "brw"))
    s_sel, s_gp = sem("sd_sel"), sem("sd_gp")
    s_dtp, s_proj, s_raw, s_conv, s_silu = (sem("sd_" + n) for n in ("dtp", "proj", "raw", "conv", "silu"))
    s_setps, s_setrd, s_dts, s_dexp, s_dta = (sem("sd_" + n) for n in ("setps", "setrd", "dts", "dexp", "dta"))
    s_tmps, s_tmrd = sem("sd_tmps"), sem("sd_tmrd")
    s_csb, s_seg, s_ecs, s_cl, s_el = (sem("sd_" + n) for n in ("csb", "seg", "ecs", "cl", "el"))
    s_cb, s_cbm, s_xt, s_xdt, s_xdd, s_bt, s_btm = (sem("sd_" + n) for n in
                                                    ("cb", "cbm", "xt", "xdt", "xdd", "bt", "btm"))
    s_m, s_cs, s_yps, s_yev, s_sps, s_st = (sem("sd_" + n) for n in ("m", "cs", "yps", "yev", "sps", "st"))
    s_tlps, s_tl, s_bcps, s_bcs, s_hops, s_ho = (sem("sd_" + n) for n in ("tlps", "tl", "bcps", "bcs", "hops", "ho"))
    s_h0 = [sem(f"sd_h0{i}") for i in range(3)]
    s_h0w = [sem(f"sd_h0w{i}") for i in range(3)]
    s_dec, s_bb, s_bbrd, s_hnew, s_yd = (sem("sd_" + n) for n in ("dec", "bb", "bbrd", "hnew", "yd"))
    s_yg, s_sq, s_nps, s_var, s_rt, s_yb, s_br, s_brrd = (sem("sd_" + n) for n in
                                                         ("yg", "sq", "nps", "var", "rt", "yb", "br", "brrd"))
    s_out, s_dve, s_act = sem("sd_out"), sem("sd_dve"), sem("sd_act")

    def chunk(c):
        return slice(c * P, (c + 1) * P)

    def by_group(x):
        return x.rearrange("p (g r) n -> p g r n", g=NGR)

    with nc.Block() as block:
        @block.sync
        def _(sp):
            w = A["w_in"][0].rearrange("(k p) n -> p k n", p=P)
            sp.dma_start(dtw, w[:, :, C_DT:C_DT + NH]).then_inc(s_dtw, 16)
            sp.dma_start(ring[0], w[:, :, C_X:C_X + 512]).then_inc(s_w[0], 16)
            for j, name in enumerate(("dt_bias", "a_log", "d_skip")):
                sp.dma_start(hp[:, j:j + 1], A[name][0].rearrange("(h a) -> h a", a=1)).then_inc(s_hp, 16)
            sp.dma_start(vn[0:64, :], A["conv_w"][0].rearrange("j (t c) -> (j t) c", c=P)).then_inc(s_vn, 16)
            sp.dma_start(vn[64:80, :], A["conv_b"][0].rearrange("(t c) -> t c", c=P)).then_inc(s_vn, 16)
            sp.dma_start(vn[80:88, :], A["g_ssm_norm"][0].rearrange("(t c) -> t c", c=P)).then_inc(s_vn, 16)
            sp.dma_start(hn, A["state_conv"][0].rearrange("b j c -> (b j) c")).then_inc(s_hn, 16)
            sp.dma_start(ring[1], w[:, :, C_X + 512:C_X + 1024]).then_inc(s_w[1], 16)
            for i in range(2, 4):
                sp.wait_ge(s_proj, 4 * (i - 1))
                sp.dma_start(ring[i % 2], w[:, :, C_X + i * 512:C_X + (i + 1) * 512]).then_inc(s_w[i % 2], 16)
            sp.dma_start(O[9][0, :, 0:2, :], A["state_conv"][0, :, 1:3, :]).then_inc(s_out, 16)
            sp.wait_ge(s_proj, NCV)
            sp.dma_start(brw, A["w_branch_b"][0].rearrange("(k p) n -> p k n", p=P)).then_inc(s_brw, 16)
            sp.wait_ge(s_ho, 8)
            sp.dma_start(O[4][0, 0].rearrange("(k q) p n -> (q p) k n", q=2), hout).then_inc(s_out, 16)
            sp.wait_ge(s_yps, NB)
            sp.wait_ge(s_st, NB)
            sp.wait_ge(s_m, NB)
            sp.wait_ge(s_hops, 1)
            for b in range(NS):
                if b >= 3:
                    sp.wait_ge(s_h0w[b % 3], 16 * (b // 3))
                    sp.wait_ge(s_yd, b - 2)
                sp.dma_start(h0[b % 3], A["state_ssm"][0, b].rearrange("(k q) p n -> (q p) k n", q=2))\
                    .then_inc(s_h0[b % 3], 16)
            sp.wait_ge(s_tl, 1)
            sp.dma_start(O[5][0, 0], tl[0:3, :]).then_inc(s_out, 16)
            sp.dma_start(O[9][0, :, 2, :], tl[3:11, :]).then_inc(s_out, 16)
            sp.wait_ge(s_out, 64)

        @block.gpsimd
        def _(pool):
            G = nc.gpsimd
            link = Link(pool, s_gp)
            for r in raw:
                link(G.memset(r, 0.0))
            link(G.memset(sel, 0.0))
            link(G.affine_select(out=sel, in_=sel, compare_op=ALU.not_equal, fill=1.0, base=0,
                                 pattern=[[-1, NH], [0, P]], channel_multiplier=1))
            link(G.memset(ek, 1.0))
            link(G.affine_select(out=ek, in_=ek, compare_op=ALU.is_ge, fill=0.0, base=0,
                                 pattern=[[P, KD], [1, P]], channel_multiplier=-HD))
            link(G.affine_select(out=ek, in_=ek, compare_op=ALU.is_ge, fill=0.0, base=HD - 1,
                                 pattern=[[-P, KD], [-1, P]], channel_multiplier=HD))
            link(G.memset(mask, 1.0))
            G.affine_select(out=mask, in_=mask, compare_op=ALU.is_ge, fill=0.0, base=0,
                            pattern=[[1, P]], channel_multiplier=-1).then_inc(s_sel, 1)
            for c in range(1, NB):
                pool.wait_ge(s_silu, NCV)
                pool.wait_ge(s_ecs, 2 * (c + 1))
                if c > 1:
                    pool.wait_ge(s_yps, c)
                G.tensor_tensor(by_group(cs_c), cv[:, 12:16, chunk(c)].unsqueeze(2).to_broadcast([P, NGR, HPG, P]),
                                by_group(ecs), ALU.mult).then_inc(s_cs, 1)
            for b in range(NS):
                pool.wait_ge(s_h0[b % 3], 16 * (b // 3 + 1))
                G.tensor_tensor(h0[b % 3], h0[b % 3], ex[:, :, 8 + b:9 + b].to_broadcast([P, KD, SN]),
                                ALU.mult).then_inc(s_dec, 1)

        @block.scalar
        def _(act):
            S = nc.scalar
            act.wait_ge(s_gp, 2)
            act.wait_ge(s_hp, 48)
            S.activation(hp[:, 4:5], hp[:, 1:2], ACT.Exp).then_inc(s_dexp, 1)
            act.wait_ge(s_dts, 1)
            S.activation(dtt[1], dtt[1], ACT.Exp).then_inc(s_dexp, 1)

            def silu(n):
                act.wait_ge(s_conv, n + 1)
                S.activation(cv[:, n, :], cv[:, n, :], ACT.Silu).then_inc(s_silu, 1)

            for n in range(NCV):
                act.wait_ge(s_proj, n + 1)
                if n >= 2:
                    act.wait_ge(s_conv, n - 1)
                S.activation(cols(raw[n % 2][:, 3:3 + T]), two(ps[:, 2 * (n % 2):2 * (n % 2) + 2, :]),
                             ACT.Copy).then_inc(s_raw, 1)
                act.wait_ge(s_raw, 2 * n + 1)
                S.activation(tail[:, n, :], raw[n % 2][:, L:L + 11], ACT.Copy).then_inc(s_raw, 1)
                if n >= 1:
                    silu(n - 1)
            silu(NCV - 1)
            act.wait_ge(s_dta, 1)
            S.activation(rex[:, 8:16], rex[:, 8:16], ACT.Exp).then_inc(s_dexp, 1)
            for c in range(NB):
                for half in range(2):
                    act.wait_ge(s_csb, 2 * c + half + 1)
                    if c >= 2:
                        act.wait_ge(s_cs, c - 1)
                    if c >= 1:
                        act.wait_ge(s_st, c)
                    S.activation(ecs[:, 8 * half:8 * half + 8, :], ps[:, 0:2, :].rearrange("p a (h i) -> p (a h) i", i=P),
                                 ACT.Exp).then_inc(s_ecs, 1)
                act.wait_ge(s_cl, c + 1)
                S.activation(lm, lm, ACT.Exp).then_inc(s_el, 1)
                act.wait_ge(s_bt, c + 1)
                if c:
                    act.wait_ge(s_sps, c)
                S.activation(btm, ps[:, 5, :].rearrange("p (g n) -> p g n", g=NGR), ACT.Copy).then_inc(s_btm, 1)
            act.wait_ge(s_hops, 1)
            for k in range(KD):
                S.activation(hout[:, k, :], ps[:, 2 + k // 4, (k % 4) * P:(k % 4 + 1) * P], ACT.Copy).then_inc(s_ho, 1)
            act.wait_ge(s_bcps, 1)
            S.activation(bcs, ps[0:NS, 6:8, :].rearrange("p a n -> p (a n)"), ACT.Copy).then_inc(s_bcs, 1)
            for b in range(NS):
                act.wait_ge(s_hnew, b + 1)
                act.dma_start(O[8][0, b].rearrange("(k q) p n -> (q p) k n", q=2), h0[b % 3]).then_inc(s_h0w[b % 3], 16)
            for g in range(NGR):
                act.wait_ge(s_yg, 2 * g + 2)
                if g:
                    act.wait_ge(s_nps, g)
                else:
                    for i in range(3):
                        act.wait_ge(s_h0w[i], 16 * ((NS - 1 - i) // 3 + 1))
                for j in range(2):
                    S.activation(sq[:, j, :], cv[:, 2 * g + j, :], ACT.Square).then_inc(s_sq, 1)
                act.wait_ge(s_var, g + 1)
                S.activation(rs, rs, ACT.Sqrt).then_inc(s_rt, 1)
            act.wait_ge(s_tlps, 1)
            S.activation(tl, ps[0:11, 0:4, :].rearrange("p a n -> p (a n)"), ACT.Copy).then_inc(s_tl, 1)

        @block.tensor
        def _(pe):
            mm = nc.tensor.matmul
            pe.wait_ge(s_dtw, 16)
            for k in range(KD):
                for h in range(2):
                    last = mm(ps[0:NH, 6 + h, 0:HALF], dtw[:, k, :], hT[:, k, h * HALF:(h + 1) * HALF],
                              start=(k == 0), stop=(k == KD - 1))
            last.then_inc(s_dtp, 1)
            pe.wait_ge(s_vn, 48)
            pe.wait_ge(s_hn, 16)
            nc.tensor.transpose(ps[:, 4, 0:88], vn, ident[0:88, 0:88])
            for n in range(NCV):
                last = nc.tensor.transpose(ps[:, 5, n * 24:(n + 1) * 24], hn[:, n * P:(n + 1) * P],
                                           ident[0:24, 0:24])
            last.then_inc(s_setps, 1)
            for n in range(NCV):
                i, m = n // 4, n % 4
                if m == 0:
                    pe.wait_ge(s_w[i % 2], 16 * (i // 2 + 1))
                if n >= 2:
                    pe.wait_ge(s_raw, 2 * (n - 2) + 1)
                for k in range(KD):
                    for h in range(2):
                        last = mm(ps[:, 2 * (n % 2) + h, 0:HALF], ring[i % 2][:, k, m * P:(m + 1) * P],
                                  hT[:, k, h * HALF:(h + 1) * HALF], start=(k == 0), stop=(k == KD - 1))
                last.then_inc(s_proj, 1)
            pe.wait_ge(s_dta, 2)
            for c in range(NB):
                nc.tensor.transpose(ps[:, 4, c * 32:c * 32 + 16], csv[:, chunk(c)], ident[0:NH, 0:NH])
                nc.tensor.transpose(ps[:, 4, c * 32 + 16:c * 32 + 32], dtv[:, chunk(c)], ident[0:NH, 0:NH])
            pe.wait_ge(s_dexp, 3)
            pe.wait_ge(s_sel, 1)
            for k in range(KD):
                last = mm(ps[:, 4, 128 + 17 * k:145 + 17 * k], ek[:, k, :], rex, start=True, stop=True)
            last.then_inc(s_tmps, 1)
            pe.wait_ge(s_silu, NCV)
            pe.wait_ge(s_raw, 2 * NCV)
            for c in range(NB):
                for half in range(2):
                    n = 2 * c + half
                    if n:
                        pe.wait_ge(s_ecs, n)
                        pe.wait_ge(s_seg, n)
                    for h in range(8):
                        last = mm(ps[:, h // 4, (h % 4) * P:(h % 4 + 1) * P], sel[:, 8 * half + h, :],
                                  csv[:, chunk(c)], start=True, stop=True)
                    last.then_inc(s_csb, 1)
                    if half == 0:
                        pe.wait_ge(s_tmrd, 2)
                        if c:
                            pe.wait_ge(s_cbm, c)
                        for g in range(NGR):
                            last = mm(ps[:, 4, g * P:(g + 1) * P], cv[:, 8 + g, chunk(c)], cv[:, 12 + g, chunk(c)],
                                      start=True, stop=True)
                        last.then_inc(s_cb, 1)
                        if c:
                            pe.wait_ge(s_st, c)
                        for k in range(KD):
                            last = nc.tensor.transpose(ps[:, 2 + k // 4, (k % 4) * P:(k % 4 + 1) * P],
                                                       cv[:, k, chunk(c)], ident)
                        last.then_inc(s_xt, 1)
                        if c:
                            pe.wait_ge(s_btm, c)
                        for g in range(NGR):
                            last = nc.tensor.transpose(ps[:, 5, g * P:(g + 1) * P], cv[:, 8 + g, chunk(c)], ident)
                        last.then_inc(s_bt, 1)
                pe.wait_ge(s_btm, c + 1)
                pe.wait_ge(s_xdd, c + 1)
                for g in range(NGR):
                    last = mm(ps[:, 2 + g // 2, (g % 2) * 256:(g % 2) * 256 + 256], btm[:, g, :],
                              xdd[:, 4 * g:4 * g + 4, :].rearrange("p h d -> p (h d)"), start=True, stop=True)
                last.then_inc(s_sps, 1)
                pe.wait_ge(s_m, c + 1)
                if c:
                    pe.wait_ge(s_cs, c)
                    pe.wait_ge(s_yev, c)
                for h in range(NH):
                    rows = slice(HD * (h % 2), HD * (h % 2) + HD)
                    k = h // 2
                    out = ps[rows, 6 + k // 4, (k % 4) * P:(k % 4 + 1) * P]
                    last = mm(out, xdt[:, h, :], lm[:, h, :], start=True, stop=(c == 0))
                    if c:
                        last = mm(out, st[:, h, :], cs_c[:, h, :], start=False, stop=True)
                last.then_inc(s_yps, 1)
            pe.wait_ge(s_st, NB)
            for k in range(KD):
                last = nc.tensor.transpose(ps[:, 2 + k // 4, (k % 4) * P:(k % 4 + 1) * P],
                                           st[:, 2 * k:2 * k + 2, :].rearrange("p h d -> p (h d)"), ident)
            last.then_inc(s_hops, 1)
            pe.wait_ge(s_yev, NB)
            for j in range(8):
                last = nc.tensor.transpose(ps[0:NS, 6 + j // 4, (j % 4) * P:(j % 4 + 1) * P], cv[:, 8 + j, L:T], ident)
            last.then_inc(s_bcps, 1)
            pe.wait_ge(s_bcs, 1)
            pe.wait_ge(s_ho, 8)
            for b in range(NS):
                if b >= 2:
                    pe.wait_ge(s_bbrd, b - 1)
                for j in range(2):
                    last = mm(ps[:, 2 * (b % 2) + j, :], sel[0:NS, b, :], bcs[:, j * 512:(j + 1) * 512],
                              start=True, stop=True)
                last.then_inc(s_bb, 1)
            pe.wait_ge(s_bbrd, NS)
            for g in range(NGR):
                pe.wait_ge(s_sq, 2 * g + 2)
                if g:
                    pe.wait_ge(s_var, g)
                for j in range(2):
                    for h in range(2):
                        last = mm(ps[:, h, 0:HALF], ones, sq[:, j, h * HALF:(h + 1) * HALF], start=(j == 0), stop=(j == 1))
                last.then_inc(s_nps, 1)
            pe.wait_ge(s_var, NGR)
            for n in range(NCV):
                last = nc.tensor.transpose(ps[0:11, n // 4, (n % 4) * P:(n % 4 + 1) * P], tail[:, n, :], ident)
            last.then_inc(s_tlps, 1)
            pe.wait_ge(s_yb, KD)
            pe.wait_ge(s_brw, 16)
            for m in range(KD):
                if m >= 2:
                    pe.wait_ge(s_brrd, m - 1)
                for k in range(KD):
                    for h in range(2):
                        last = mm(ps[:, 4 + 2 * (m % 2) + h, 0:HALF], brw[:, k, m * P:(m + 1) * P],
                                  cv[:, k, h * HALF:(h + 1) * HALF], start=(k == 0), stop=(k == KD - 1))
                last.then_inc(s_br, 1)

        @block.vector
        def _(dve):
            V = nc.vector
            link = Link(dve, s_dve)
            x, e, a, w, q, r = dtt
            stt, tt, ts = V.scalar_tensor_tensor, V.tensor_tensor, V.tensor_scalar
            dve.wait_ge(s_hp, 48)
            dve.wait_ge(s_dtp, 1)
            link(ts(cols(x), two(ps[0:NH, 6:8, :]), hp[:, 0:1], None, ALU.add))
            link(ts(a, x, -1.0, None, ALU.mult))
            link(tt(a, a, x, ALU.max))
            ts(e, a, -1.0, None, ALU.mult).then_inc(s_dts, 1)
            dve.wait_ge(s_setps, 1)
            V.tensor_copy(vT, ps[:, 4, 0:88]).then_inc(s_setrd, 1)
            V.tensor_copy(hist, ps[:, 5, 0:NCV * 24].rearrange("p (n j) -> p n j", n=NCV)).then_inc(s_setrd, 1)
            dve.wait_ge(s_dexp, 2)
            link(ts(a, e, 2.0, None, ALU.add))
            link(V.reciprocal(a, a))
            link(tt(a, a, e, ALU.mult))
            link(tt(w, a, a, ALU.mult))
            link(ts(q, w, 1.0 / 17, None, ALU.mult))
            for n in range(7, 0, -1):
                link(stt(out=q, in0=q, scalar=1.0 / (2 * n + 1), in1=w, op0=ALU.add, op1=ALU.mult))
            link(stt(out=q, in0=q, scalar=1.0, in1=a, op0=ALU.add, op1=ALU.mult))
            link(ts(x, x, 0.0, None, ALU.max))
            link(stt(out=dtv, in0=q, scalar=2.0, in1=x, op0=ALU.mult, op1=ALU.add))
            link(ts(hp[:, 5:6], hp[:, 4:5], -1.0, None, ALU.mult))
            link(ts(r, dtv, hp[:, 5:6], None, ALU.mult))
            link(V.tensor_copy(rex[:, 0:8], dtv[:, L:T]))
            link(V.tensor_copy(rex[:, 16:17], hp[:, 2:3]))
            V.tensor_copy(rex[:, 8:16], r[:, L:T]).then_inc(s_dta, 1)
            link(V.memset(e, 1.0))
            for c in range(NB):
                last = V.tensor_tensor_scan(csv[:, chunk(c)], e[:, 0:P], r[:, chunk(c)], 0.0, ALU.mult, ALU.add)
                if c < NB - 1:
                    link(last)
            last.then_inc(s_dta, 1)

            dve.wait_ge(s_setrd, 2)
            for n in range(NCV):
                dve.wait_ge(s_raw, 2 * n + 1)
                wj = [vT[:, CW + j * NCV + n:CW + j * NCV + n + 1] for j in range(4)]
                bj = vT[:, CB + n:CB + n + 1]
                out, smp, rw = cv[:, n, 0:L], cv[:, n, L:T], raw[n % 2]
                hj = hist[:, n, :].rearrange("p (b j) -> p j b", j=3)
                link(ts(out, rw[:, 0:L], wj[0], bj, ALU.mult, ALU.add))
                link(ts(smp, hj[:, 0, :], wj[0], bj, ALU.mult, ALU.add))
                for j in (1, 2):
                    link(stt(out=out, in0=rw[:, j:j + L], scalar=wj[j], in1=out, op0=ALU.mult, op1=ALU.add))
                    link(stt(out=smp, in0=hj[:, j, :], scalar=wj[j], in1=smp, op0=ALU.mult, op1=ALU.add))
                link(stt(out=out, in0=rw[:, 3:3 + L], scalar=wj[3], in1=out, op0=ALU.mult, op1=ALU.add))
                stt(out=smp, in0=rw[:, 3 + L:3 + T], scalar=wj[3], in1=smp, op0=ALU.mult,
                    op1=ALU.add).then_inc(s_conv, 1)

            dve.wait_ge(s_tmps, 1)
            V.tensor_copy(tm, ps[:, 4, 0:P].rearrange("p (c i h) -> p c i h", c=NB, i=2)).then_inc(s_tmrd, 1)
            V.tensor_copy(ex, ps[:, 4, 128:128 + KD * 17].rearrange("p (k j) -> p k j", j=17)).then_inc(s_tmrd, 1)
            dve.wait_ge(s_tmrd, 2)
            for c in range(NB):
                csb = ps[:, 0:2, :].rearrange("p a (h i) -> p (a h) i", i=P)
                for half in range(2):
                    hs = slice(8 * half, 8 * half + 8)
                    dve.wait_ge(s_ecs, 2 * c + half + 1)
                    if c:
                        dve.wait_ge(s_yps, c)
                    tt(lm[:, hs, :], csb, tm[:, c, 0, hs].unsqueeze(2).to_broadcast([P, 8, P]),
                       ALU.subtract).then_inc(s_seg, 1)
                    if half == 0:
                        dve.wait_ge(s_cb, c + 1)
                        tt(cbm, ps[:, 4, :].rearrange("p (g i) -> p g i", g=NGR),
                           mask.unsqueeze(1).to_broadcast([P, NGR, P]), ALU.mult).then_inc(s_cbm, 1)
                        dve.wait_ge(s_xt, c + 1)
                        tt(xdt, ps[:, 2:4, :].rearrange("p a (h d) -> p (a h) d", d=HD),
                           tm[:, c, 1, :].unsqueeze(2).to_broadcast([P, NH, HD]), ALU.mult).then_inc(s_xdt, 1)
                dve.wait_ge(s_seg, 2 * c + 2)
                ts(lm, lm, 0.0, None, ALU.min).then_inc(s_cl, 1)
                dve.wait_ge(s_el, c + 1)
                dve.wait_ge(s_xdt, c + 1)
                if c:
                    dve.wait_ge(s_sps, c)
                tt(xdd, xdt, lm[:, :, P - 1:P].to_broadcast([P, NH, HD]), ALU.mult).then_inc(s_xdd, 1)
                dve.wait_ge(s_xdd, c + 1)
                dve.wait_ge(s_cbm, c + 1)
                tt(by_group(lm), by_group(lm), cbm.unsqueeze(2).to_broadcast([P, NGR, HPG, P]),
                   ALU.mult).then_inc(s_m, 1)
                dve.wait_ge(s_yps, c + 1)
                for k in range(KD):
                    last = stt(out=cv[:, k, chunk(c)], in0=cv[:, k, chunk(c)], scalar=ex[:, k, 16:17],
                               in1=ps[:, 6 + k // 4, (k % 4) * P:(k % 4 + 1) * P], op0=ALU.mult, op1=ALU.add)
                last.then_inc(s_yev, 1)
                dve.wait_ge(s_sps, c + 1)
                sps = ps[:, 2:4, :].rearrange("p a (h d) -> p (a h) d", d=HD)
                if c == 0:
                    V.tensor_copy(st, sps).then_inc(s_st, 1)
                else:
                    dve.wait_ge(s_ecs, 2 * c + 2)
                    link(tt(st, st, ecs[:, :, P - 1:P].to_broadcast([P, NH, HD]), ALU.mult))
                    tt(st, st, sps, ALU.add).then_inc(s_st, 1)
                dve.wait_ge(s_st, c + 1)
            link(tt(xs_s, cv[:, 0:KD, L:T], ex[:, :, 0:8], ALU.mult))
            for b in range(NS):
                bb = ps[:, 2 * (b % 2):2 * (b % 2) + 2, :].rearrange("p i (g n) -> p i g n", g=NGR)
                B, C = (bb[:, i, :, :].unsqueeze(2).to_broadcast([P, NGR, 2, SN]) for i in range(2))
                g4 = lambda v: v.rearrange("p (g r) n -> p g r n", g=NGR)
                dve.wait_ge(s_bb, b + 1)
                link(tt(g4(tb), B, g4(xs_s[:, :, b:b + 1].to_broadcast([P, KD, SN])), ALU.mult))
                dve.wait_ge(s_dec, b + 1)
                tt(h0[b % 3], h0[b % 3], tb, ALU.add).then_inc(s_hnew, 1)
                dve.wait_ge(s_hnew, b + 1)
                tt(g4(tb), g4(h0[b % 3]), C, ALU.mult).then_inc(s_bbrd, 1)
                dve.wait_ge(s_bbrd, b + 1)
                V.tensor_reduce(ys_s[:, :, b:b + 1], tb, AX_X, ALU.add).then_inc(s_yd, 1)
                dve.wait_ge(s_yd, b + 1)
            link(tt(xs_s, cv[:, 0:KD, L:T], ex[:, :, 16:17].to_broadcast([P, KD, NS]), ALU.mult))
            link(tt(cv[:, 0:KD, L:T], xs_s, ys_s, ALU.add))
            dve.wait_ge(s_yev, NB)
            for k in range(KD):
                tt(cv[:, k, :], cv[:, k, :], zs[:, k, :], ALU.mult).then_inc(s_yg, 1)
            dve.wait_ge(s_yg, KD)
            for g in range(NGR):
                dve.wait_ge(s_nps, g + 1)
                link(ts(cols(rs), two(ps[:, 0:2, :]), 1.0 / 256, G_EPS, ALU.mult, ALU.add))
                V.reciprocal(rs, rs).then_inc(s_var, 1)
                dve.wait_ge(s_rt, g + 1)
                for j in range(2):
                    k = 2 * g + j
                    stt(out=cv[:, k, :], in0=cv[:, k, :], scalar=vT[:, GN + k:GN + k + 1], in1=rs, op0=ALU.mult,
                        op1=ALU.mult).then_inc(s_yb, 1)
                dve.wait_ge(s_yb, 2 * g + 2)
            for m in range(KD):
                dve.wait_ge(s_br, m + 1)
                tt(cols(tmpo), two(ps[:, 4 + 2 * (m % 2):6 + 2 * (m % 2), :]), cols(gB[:, m, :]),
                   ALU.mult).then_inc(s_brrd, 1)
                dve.wait_ge(s_brrd, m + 1)
                link(tt(mg[:, m, :], mg[:, m, :], tmpo, ALU.add))


def stage_query(nc, mem, sem, ps, A, mod_d):
    mg = mem(Map.MG, KD, T)
    ident = mem(Map.IDENT, P)
    h2T = mem(Map.HT, KD, T)
    wo = mem(Map.HT + KD * T, KD, D)
    x1, h2 = mem(Map.X1, 5, D), mem(Map.H2, 5, D)
    sc = mem(Map.SC, NB, 2 * PH, NK)
    scs = mem(Map.SCS, 2, NK)
    gate, scale, shift = (mem(Map.SC + i * 2 * D, 2, D) for i in range(3))
    g2, junk = mem(Map.SC + 6 * D, D), mem(Map.SC + 7 * D, D)
    M = Map.QLOCAL
    ring = [mem(M + i * KD * 512, KD, 512) for i in range(2)]; M += 2 * KD * 512
    kn = mem(M, 2 * PH, P); M += 2 * PH * P
    kT = mem(M, 2 * PH, NK); M += 2 * PH * NK
    qT = [mem(M + i * T, T) for i in range(2)]; M += 2 * T
    qpad = mem(M, 2 * PH, 64); M += 2 * PH * 64
    stat, rstd = mem(M, 8), mem(M + 8, 8); M += 16
    assert M <= Map.W, M

    s_wo, s_x, s_rows, s_k = (sem("qy_" + n) for n in ("wo", "x", "rows", "k"))
    s_w = [sem(f"qy_w{i}") for i in range(2)]
    s_o, s_ord, s_x1, s_sq, s_var, s_rt, s_h2 = (sem("qy_" + n) for n in ("o", "ord", "x1", "sq", "var", "rt", "h2"))
    s_tp, s_hT, s_kp, s_kT, s_q, s_qT = (sem("qy_" + n) for n in ("tp", "hT", "kp", "kT", "q", "qT"))
    s_s, s_srd, s_zero, s_dve, s_act = (sem("qy_" + n) for n in ("s", "srd", "zero", "dve", "act"))
    hparts = [(b, half) for b in range(5) for half in range(2)]

    def rows_of(b):
        return P if b < NB else NS

    with nc.Block() as block:
        @block.sync
        def _(sp):
            sp.dma_start(wo, A["w_out"][0].rearrange("(k p) n -> p k n", p=P)).then_inc(s_wo, 16)
            sp.dma_start(x1[:, 0:NB, :], A["x_prompt"][0].rearrange("(b p) d -> p b d", p=P)).then_inc(s_x, 16)
            sp.dma_start(x1[0:NS, NB, :], A["x_sample"].rearrange("b s d -> (b s) d")).then_inc(s_x, 16)
            for dst, m in ((gate, 2), (shift, 3), (scale, 4)):
                sp.dma_start(dst[:, 0, :], mod_d[NS:NC_ROWS, m * D:(m + 1) * D].partition_broadcast(P)).then_inc(s_rows, 16)
                sp.dma_start(dst[0:NS, 1, :], mod_d[0:NS, m * D:(m + 1) * D]).then_inc(s_rows, 16)
            sp.dma_start(g2, A["g_norm2"][0:1, :].partition_broadcast(P)).then_inc(s_rows, 16)
            sp.dma_start(kn, A["sub_keys"][0].rearrange("h s k d -> k (h s) d")).then_inc(s_k, 16)
            w = A["w_query"][0].rearrange("(k p) n -> p k n", p=P)
            for i in range(4):
                if i >= 2:
                    sp.wait_ge(s_q, 4 * (i - 1))
                sp.dma_start(ring[i % 2], w[:, :, i * 512:(i + 1) * 512]).then_inc(s_w[i % 2], 16)

        @block.gpsimd
        def _(pool):
            nc.gpsimd.memset(qpad, 0.0).then_inc(s_zero, 1)
            nc.gpsimd.memset(scs, 0.0).then_inc(s_zero, 1)

        @block.scalar
        def _(act):
            S = nc.scalar
            for b in range(5):
                n = rows_of(b)
                act.wait_ge(s_x1, b + 1)
                if b:
                    act.wait_ge(s_sq, b)
                S.activation(junk[0:n, :], x1[0:n, b, :], ACT.Square, accum_out=stat[0:n, b:b + 1]).then_inc(s_sq, 1)
                act.wait_ge(s_var, b + 1)
                S.activation(rstd[0:n, b:b + 1], stat[0:n, b:b + 1], ACT.Sqrt).then_inc(s_rt, 1)
            for n, (b, half) in enumerate(hparts):
                act.wait_ge(s_tp, n + 1)
                m = rows_of(b)
                S.activation(h2T[:, 4 * half:4 * half + 4, b * P:b * P + m],
                             ps[:, 4 + n % 4, :].rearrange("p (k t) -> p k t", k=4)[:, :, 0:m], ACT.Copy).then_inc(s_hT, 1)
            for i in range(4):
                act.wait_ge(s_kp, i + 1)
                S.activation(kT[:, 4 * i:4 * i + 4, :], ps[:, 4 + i, :].rearrange("p (k t) -> p k t", k=4),
                             ACT.Copy).then_inc(s_kT, 1)
            act.wait_ge(s_zero, 2)
            for t in range(2 * PH):
                act.wait_ge(s_q, t + 1)
                if t >= 2:
                    act.wait_ge(s_s, t - 1)
                S.activation(cols(qT[t % 2]), two(ps[:, 2 * (t % 2):2 * (t % 2) + 2, :]), ACT.Copy).then_inc(s_qT, 1)
                act.wait_ge(s_qT, 2 * t + 1)
                h = t // 2
                S.activation(qpad[:, t, NS * h:NS * h + NS], qT[t % 2][:, L:T], ACT.Copy).then_inc(s_qT, 1)

        @block.tensor
        def _(pe):
            mm = nc.tensor.matmul
            pe.wait_ge(s_wo, 16)
            for b in range(5):
                n = rows_of(b)
                if b >= 2:
                    pe.wait_ge(s_ord, b - 1)
                for j in range(2):
                    for k in range(KD):
                        last = mm(ps[0:n, 2 * (b % 2) + j, :], mg[:, k, b * P:b * P + n], wo[:, k, j * 512:(j + 1) * 512],
                                  start=(k == 0), stop=(k == KD - 1))
                last.then_inc(s_o, 1)
            for n, (b, half) in enumerate(hparts):
                pe.wait_ge(s_h2, b + 1)
                if n >= 4:
                    pe.wait_ge(s_hT, n - 3)
                m = rows_of(b)
                for k in range(4):
                    kk = 4 * half + k
                    last = nc.tensor.transpose(ps[:, 4 + n % 4, k * P:k * P + m],
                                               h2[0:m, b, kk * P:(kk + 1) * P], ident[0:m, 0:m])
                last.then_inc(s_tp, 1)
            pe.wait_ge(s_hT, 10)
            pe.wait_ge(s_k, 16)
            for i in range(4):
                for j in range(4):
                    last = nc.tensor.transpose(ps[:, 4 + i, j * P:(j + 1) * P], kn[:, 4 * i + j, :], ident)
                last.then_inc(s_kp, 1)

            def scores(t):
                pe.wait_ge(s_qT, 2 * t + 2)
                if t >= 2:
                    pe.wait_ge(s_srd, t - 1)
                for b in range(NB):
                    last = mm(ps[:, 4 + t % 2, b * P:(b + 1) * P], qT[t % 2][:, b * P:(b + 1) * P], kT[:, t, :],
                              start=True, stop=True)
                last = mm(ps[0:64, 6 + t % 2, 0:NK], qpad[:, t, :], kT[:, t, :], start=(t < 2), stop=(t >= 2 * PH - 2))
                last.then_inc(s_s, 1)

            pe.wait_ge(s_ord, 5)
            for t in range(2 * PH):
                if t % 4 == 0:
                    pe.wait_ge(s_w[(t // 4) % 2], 16 * (t // 8 + 1))
                if t >= 2:
                    pe.wait_ge(s_qT, 2 * (t - 2) + 1)
                for k in range(KD):
                    for h in range(2):
                        last = mm(ps[:, 2 * (t % 2) + h, 0:HALF], ring[(t // 4) % 2][:, k, (t % 4) * P:(t % 4 + 1) * P],
                                  h2T[:, k, h * HALF:(h + 1) * HALF], start=(k == 0), stop=(k == KD - 1))
                last.then_inc(s_q, 1)
                if t == 0:
                    pe.wait_ge(s_kT, 4)
                else:
                    scores(t - 1)
            scores(2 * PH - 1)

        @block.vector
        def _(dve):
            V = nc.vector
            link = Link(dve, s_dve)
            dve.wait_ge(s_rows, 16 * 7)
            for r, n in ((0, P), (1, NS)):
                link(V.scalar_tensor_tensor(out=scale[0:n, r, :], in0=scale[0:n, r, :], scalar=1.0, in1=g2[0:n, :],
                                            op0=ALU.add, op1=ALU.mult))
            dve.wait_ge(s_x, 32)
            for b in range(5):
                n, r = rows_of(b), b // NB
                dve.wait_ge(s_o, b + 1)
                V.tensor_tensor(h2[0:n, b, :], ps[0:n, 2 * (b % 2):2 * (b % 2) + 2, :].rearrange("p a n -> p (a n)"),
                                gate[0:n, r, :], ALU.mult).then_inc(s_ord, 1)
                dve.wait_ge(s_ord, b + 1)
                V.tensor_tensor(x1[0:n, b, :], x1[0:n, b, :], h2[0:n, b, :], ALU.add).then_inc(s_x1, 1)
                dve.wait_ge(s_sq, b + 1)
                st = stat[0:n, b:b + 1]
                link(V.tensor_scalar(st, st, 1.0 / D, EPS, ALU.mult, ALU.add))
                V.reciprocal(st, st).then_inc(s_var, 1)
                dve.wait_ge(s_rt, b + 1)
                link(V.scalar_tensor_tensor(out=h2[0:n, b, :], in0=x1[0:n, b, :], scalar=rstd[0:n, b:b + 1],
                                            in1=scale[0:n, r, :], op0=ALU.mult, op1=ALU.mult))
                V.tensor_tensor(h2[0:n, b, :], h2[0:n, b, :], shift[0:n, r, :], ALU.add).then_inc(s_h2, 1)
            dve.wait_ge(s_h2, 5)
            for t in range(2 * PH):
                dve.wait_ge(s_s, t + 1)
                V.tensor_copy(sc[:, :, t, :], ps[:, 4 + t % 2, :].rearrange("p (b k) -> p b k", b=NB)).then_inc(s_srd, 1)
            dve.wait_ge(s_zero, 2)
            for i in range(2):
                link(V.tensor_copy(scs[0:64, i, :], ps[0:64, 6 + i, 0:NK]))


GATE = 8
NGRP = 2 * TOPK // (2 * GATE)


def stage_peer(nc, mem, sem, ps, A, O, mod_d, integers):
    ident = mem(Map.IDENT, P)
    x1, h2 = mem(Map.X1, 5 * D), mem(Map.H2, 5 * D)
    scores = mem(Map.SC, (NB * PH + 1) * 2 * NK)
    U = [mem(256 + j * D, D) for j in range(GATE)]
    Vr = [mem(256 + (GATE + j) * D, D) for j in range(GATE)]
    M = Map.QLOCAL

    def take(*shape, rows=P):
        nonlocal M
        M += int(np.prod(shape))
        return mem(M - int(np.prod(shape)), *shape, rows=rows)

    diag = take(GATE, P)
    zero = take(P)
    gate, scale, shift = take(2, D), take(2, D), take(2, D)
    gf = take(D)
    xb = take(D)
    hb = take(D)
    yb = take(D)
    x64 = take(D)
    sel64 = take(PH, NS, rows=NS)
    r64 = take(NS)
    s_in, s_rep = take(2, NK), take(2, NK)
    val, idxf = take(2, TOPK), take(2, TOPK)
    cand, crep = take(TOPK, TOPK), take(TOPK, TOPK)
    fij = take(2, TOPK)
    oh = take(2 * TOPK, TOPK)
    r01 = take(2, TOPK)
    ef = take(TOPK)
    iota = take(TOPK)
    fv = take(TOPK)
    w = [take(TOPK) for _ in range(2)]
    ssum = take(8)
    dots = [take(GATE) for _ in range(2)]
    gel = [take(GATE) for _ in range(2)]
    actv = [take(GATE) for _ in range(2)]
    stat, rstd = take(1), take(1)
    sx1 = take(D, rows=NS)
    assert M <= Map.W, M
    idx = [integers["expert0"], integers["expert1"]]
    kix, fix, fiju, iotai = (integers[n] for n in ("keys", "pairs", "halves", "counting"))

    s_rows, s_const, s_pc = sem("pr_rows"), sem("pr_const"), sem("pr_pc")
    s_U = [sem(f"pr_U{j}") for j in range(GATE)]
    s_V = [sem(f"pr_V{j}") for j in range(GATE)]
    s_top, s_uused, s_vused = sem("pr_top"), sem("pr_uused"), sem("pr_vused")
    s_nmax, s_exp, s_gelu, s_actv, s_diag = (sem("pr_" + n) for n in ("nmax", "exp", "gelu", "actv", "diag"))
    s_blk, s_blkrd, s_x2, s_sq, s_var, s_rt, s_y, s_out = (sem("pr_" + n) for n in
                                                           ("blk", "blkrd", "x2", "sq", "var", "rt", "y", "out"))
    s_ps64, s_x64, s_gatep, s_dve = sem("pr_ps64"), sem("pr_x64"), sem("pr_gatep"), sem("pr_dve")
    down, up = A["expert_down"][0], A["expert_up"][0]
    NU = NB * PH

    with nc.Block() as block:
        @block.sync
        def _(sp):
            for dst, m in ((gate, 5), (shift, 6), (scale, 7)):
                sp.dma_start(dst[:, 0, :], mod_d[NS:NC_ROWS, m * D:(m + 1) * D].partition_broadcast(P)).then_inc(s_rows, 16)
                sp.dma_start(dst[0:NS, 1, :], mod_d[0:NS, m * D:(m + 1) * D]).then_inc(s_rows, 16)
            sp.dma_start(gf, A["g_final"].rearrange("(a n) -> a n", a=1).partition_broadcast(P)).then_inc(s_rows, 16)
            sp.sem_inc(s_out, 16)
            with sp.Fori(0, NB) as b:
                sp.wait_ge(s_y, b + 1)
                sp.dma_start(O[0][0].rearrange("(b p) d -> b p d", p=P)[bass.ds(b, 1), :, :].rearrange("a p d -> (a p) d"),
                             yb).then_inc(s_out, 16)
            sp.wait_ge(s_y, NB + 1)
            sp.dma_start(O[1].rearrange("b s d -> (b s) d"), yb[0:NS, :]).then_inc(s_out, 16)
            sp.wait_ge(s_out, 16 * (NB + 2))

        @block.gpsimd
        def _(pool):
            G = nc.gpsimd
            link = Link(pool, s_pc)
            link(G.memset(zero, 0.0))
            link(G.memset(sel64, 0.0))
            link(G.affine_select(out=sel64, in_=sel64, compare_op=ALU.not_equal, fill=1.0, base=0,
                                 pattern=[[0, PH], [-1, NS]], channel_multiplier=1))
            G.iota(iotai, pattern=[[1, TOPK]], base=0, channel_multiplier=0).then_inc(s_const, 1)

            def gathers(par, group, g, rows):
                sl = slice(0, rows)
                pool.wait_ge(s_uused, g + 1)
                pool.sem_inc(s_gatep, 1)
                for j in range(GATE):
                    k = group * GATE + j
                    G.indirect_dma_start(U[j][sl, :], None, down,
                                         bass.IndirectOffsetOnAxis(ap=idx[par][sl, k:k + 1], axis=0)).then_inc(s_U[j], 16)
                pool.wait_ge(s_vused, g + 1)
                pool.sem_inc(s_gatep, 1)
                for j in range(GATE):
                    k = group * GATE + j
                    G.indirect_dma_start(Vr[j][sl, :], None, up,
                                         bass.IndirectOffsetOnAxis(ap=idx[par][sl, k:k + 1], axis=0)).then_inc(s_V[j], 16)

            with pool.Fori(0, NU // 2) as it:
                for par in range(2):
                    pool.wait_ge(s_top, 2 * it + par + 1)
                    pool.sem_inc(s_gatep, 1)
                    for group in range(NGRP):
                        gathers(par, group, 4 * it + 2 * par + group, P)
            pool.wait_ge(s_top, NU + 1)
            pool.sem_inc(s_gatep, 1)
            for group in range(NGRP):
                gathers(0, group, 2 * NU + group, 64)

        @block.scalar
        def _(act):
            S = nc.scalar

            def softmax(n, par, rows=P):
                act.wait_ge(s_nmax, n)
                S.activation(w[par], fv, ACT.Exp, bias=ssum[:, 1:2], accum_out=ssum[:, 0:1]).then_inc(s_exp, 1)

            def weights(g, gp, rows, dst):
                act.wait_ge(s_uused, g + 2)
                S.activation(gel[gp][0:rows, :], dots[gp][0:rows, :], ACT.Gelu).then_inc(s_gelu, 1)
                act.wait_ge(s_actv, g + 1)
                act.wait_ge(s_vused, g + 1)
                for j in range(GATE):
                    S.activation(dst[j][0], dst[j][1], ACT.Copy, scale=actv[gp][0:rows, j:j + 1]).then_inc(s_diag, 1)

            full = [(diag[:, j, :], ident) for j in range(GATE)]
            small = [(diag[0:64, j, 0:NS], r64[0:64, :]) for j in range(GATE)]

            def norm(b):
                act.wait_ge(s_x2, b + 1)
                S.activation(ps[:, 5:7, :].rearrange("p a n -> p (a n)"), xb, ACT.Square, accum_out=stat).then_inc(s_sq, 1)
                act.wait_ge(s_var, b + 1)
                S.activation(rstd, stat, ACT.Sqrt).then_inc(s_rt, 1)

            softmax(1, 0)
            with act.Fori(0, NB) as b:
                with act.Fori(0, PH // 2) as hp:
                    for par in range(2):
                        g = 16 * b + 4 * hp + 2 * par
                        weights(g, 0, P, full)
                        softmax(8 * b + 2 * hp + par + 2, 1 - par)
                        weights(g + 1, 1, P, full)
                norm(b)
            act.wait_ge(s_x64, 2)
            for group in range(NGRP):
                weights(2 * NU + group, group, 64, small)
            act.wait_ge(s_x2, NB + 1)
            S.activation(ps[0:NS, 5:7, :].rearrange("p a n -> p (a n)"), xb[0:NS, :], ACT.Square, accum_out=stat[0:NS, :]).then_inc(s_sq, 1)
            act.wait_ge(s_var, NB + 1)
            S.activation(rstd[0:NS, :], stat[0:NS, :], ACT.Sqrt).then_inc(s_rt, 1)

        @block.tensor
        def _(pe):
            mm = nc.tensor.matmul
            pe.wait_ge(s_const, 1)
            nc.tensor.transpose(ps[0:64, 4, 0:NS], sel64.rearrange("p h b -> p (h b)"), ident[0:NS, 0:NS])
            for j in range(2):
                last = mm(ps[0:64, 2 + j, :], sel64.rearrange("p h b -> p (h b)"),
                          h2[0:NS, 4 * D + j * 512:4 * D + (j + 1) * 512], start=True, stop=True)
            last.then_inc(s_ps64, 1)
            pe.sem_inc(s_vused, 1)

            def open_sum(rows):
                for j in range(2):
                    mm(ps[0:rows, j, :], zero[:, 0:rows], U0, start=True, stop=False, skip_group_check=True)

            def close_sum(rows):
                for j in range(2):
                    last = mm(ps[0:rows, j, :], zero[:, 0:rows], U0, start=False, stop=True, skip_group_check=True)
                last.then_inc(s_blk, 1)

            U0 = h2[:, 0:512]

            def add(g, lhs, rows, kr):
                for j in range(GATE):
                    pe.wait_ge(s_V[j], 16 * g + 16)
                    pe.wait_ge(s_diag, GATE * g + j + 1)
                    for n in range(2):
                        last = mm(ps[0:rows, n, :], lhs[j], Vr[j][0:kr, n * 512:(n + 1) * 512], start=False, stop=False,
                                  skip_group_check=True)
                last.then_inc(s_vused, 1)

            full = [diag[:, j, :] for j in range(GATE)]
            small = [diag[0:64, j, 0:NS] for j in range(GATE)]
            with pe.Fori(0, NB) as b:
                pe.wait_ge(s_blkrd, b + 1)
                open_sum(P)
                with pe.Fori(0, PH // 2) as hp:
                    for group in range(2 * NGRP):
                        add(16 * b + 4 * hp + group, full, P, P)
                close_sum(P)
            pe.wait_ge(s_blkrd, NB + 1)
            open_sum(NS)
            for group in range(NGRP):
                add(2 * NU + group, small, NS, 64)
            close_sum(NS)

        @block.vector
        def _(dve):
            V = nc.vector
            tt, ts, stt = V.tensor_tensor, V.tensor_scalar, V.scalar_tensor_tensor

            def done(ins):
                dve.drain()

            def top16(vals, index, src, rep):
                done(V.max(vals[:, 0:8], src))
                V.max_index(index[:, 0:8], vals[:, 0:8], src)
                done(V.match_replace(rep, vals[:, 0:8], src, NEG))
                done(V.max(vals[:, 8:16], rep))
                V.max_index(index[:, 8:16], vals[:, 8:16], rep)

            def topk(unit, par, n):
                done(V.tensor_copy(s_in.rearrange("p s k -> p (s k)"), scores[:, bass.ds(unit * 2 * NK, 2 * NK)]))
                for s in range(2):
                    top16(val[:, s, :], kix[:, s * TOPK:(s + 1) * TOPK], s_in[:, s, :], s_rep[:, s, :])
                dve.drain()
                done(tt(cand, val[:, 0, :].unsqueeze(2).to_broadcast([P, TOPK, TOPK]),
                        val[:, 1, :].unsqueeze(1).to_broadcast([P, TOPK, TOPK]), ALU.add))
                flat = cand.rearrange("p a b -> p (a b)")
                top16(fv, fix, flat, crep.rearrange("p a b -> p (a b)"))
                ts(ssum[:, 1:2], fv[:, 0:1], -1.0, None, ALU.mult).then_inc(s_nmax, 1)
                dve.drain()
                ts(fiju[:, 0:TOPK], fix, 4, None, ALU.logical_shift_right)
                ts(fiju[:, TOPK:2 * TOPK], fix, TOPK - 1, None, ALU.bitwise_and)
                done(V.tensor_copy(idxf.rearrange("p s k -> p (s k)"), kix))
                done(V.tensor_copy(fij.rearrange("p s k -> p (s k)"), fiju))
                fl = fij.rearrange("p s k -> p (s k)")
                done(tt(oh, fl.unsqueeze(2).to_broadcast([P, 2 * TOPK, TOPK]),
                        iota.unsqueeze(1).to_broadcast([P, 2 * TOPK, TOPK]), ALU.is_equal))
                o4 = oh.rearrange("p (s k) m -> p s k m", s=2)
                done(tt(o4, o4, idxf.unsqueeze(2).to_broadcast([P, 2, TOPK, TOPK]), ALU.mult))
                done(V.tensor_reduce(r01.rearrange("p s k -> p (s k)"), oh, AX_X, ALU.add))
                done(stt(out=ef, in0=r01[:, 0, :], scalar=float(NK), in1=r01[:, 1, :], op0=ALU.mult, op1=ALU.add))
                dve.wait_ge(s_exp, n)
                done(V.reciprocal(ssum[:, 2:3], ssum[:, 0:1]))
                ts(w[par], w[par], ssum[:, 2:3], None, ALU.mult)
                V.tensor_copy(idx[par], ef).then_inc(s_top, 1)

            def products(g, gp, xrow, rows):
                for j in range(GATE):
                    dve.wait_ge(s_U[j], 16 * g + 16)
                    last = V.tensor_tensor_reduce(U[j][0:rows, :], U[j][0:rows, :], xrow, 1.0, 0.0, ALU.mult, ALU.add,
                                                  dots[gp][0:rows, j:j + 1])
                last.then_inc(s_uused, 1)

            def weight(g, gp, par, group, rows):
                dve.wait_ge(s_gelu, g + 1)
                tt(actv[gp][0:rows, :], gel[gp][0:rows, :], w[par][0:rows, group * GATE:(group + 1) * GATE],
                   ALU.mult).then_inc(s_actv, 1)

            def finish(b, n, r, x_in):
                dve.wait_ge(s_blk, b + 1)
                tt(xb[0:n, :], ps[0:n, 0:2, :].rearrange("p a n -> p (a n)"), gate[0:n, r, :], ALU.mult).then_inc(s_blkrd, 1)
                dve.drain()
                tt(xb[0:n, :], xb[0:n, :], x_in, ALU.add).then_inc(s_x2, 1)
                dve.wait_ge(s_sq, b + 1)
                done(ts(stat[0:n, :], stat[0:n, :], 1.0 / D, EPS, ALU.mult, ALU.add))
                V.reciprocal(stat[0:n, :], stat[0:n, :]).then_inc(s_var, 1)
                dve.wait_ge(s_rt, b + 1)
                done(stt(out=xb[0:n, :], in0=xb[0:n, :], scalar=rstd[0:n, :], in1=scale[0:n, r, :], op0=ALU.mult,
                         op1=ALU.mult))
                dve.wait_ge(s_out, 16 * b + 16)
                tt(yb[0:n, :], xb[0:n, :], shift[0:n, r, :], ALU.add).then_inc(s_y, 1)

            dve.wait_ge(s_const, 1)
            V.tensor_copy(iota, iotai)
            dve.wait_ge(s_ps64, 1)
            V.tensor_copy(r64[0:64, :], ps[0:64, 4, 0:NS]).then_inc(s_x64, 1)
            V.tensor_copy(x64[0:64, :], ps[0:64, 2:4, :].rearrange("p a n -> p (a n)")).then_inc(s_x64, 1)
            dve.wait_ge(s_rows, 16 * 7)
            for r, n in ((0, P), (1, NS)):
                stt(out=scale[0:n, r, :], in0=scale[0:n, r, :], scalar=1.0, in1=gf[0:n, :], op0=ALU.add, op1=ALU.mult)
            dve.drain()
            dve.sem_inc(s_uused, 1)
            dve.sem_inc(s_blkrd, 1)
            topk(0, 0, 1)
            with dve.Fori(0, NB) as b:
                done(V.tensor_copy(hb, h2[:, bass.ds(b * D, D)]))
                with dve.Fori(0, PH // 2) as hp:
                    for par in range(2):
                        g = 16 * b + 4 * hp + 2 * par
                        unit = 8 * b + 2 * hp + par
                        products(g, 0, hb, P)
                        weight(g, 0, par, 0, P)
                        dve.wait_ge(s_vused, g + 1)
                        topk(unit + 1, 1 - par, unit + 2)
                        products(g + 1, 1, hb, P)
                        weight(g + 1, 1, par, 1, P)
                finish(b, P, 0, x1[:, bass.ds(b * D, D)])
            for group in range(NGRP):
                products(2 * NU + group, group, x64[0:64, :], 64)
                weight(2 * NU + group, group, 0, group, 64)
            finish(NB, NS, 1, x1[0:NS, NB * D:(NB + 1) * D])


def program(nc, A, O):
    with ExitStack() as ctx:
        mem = Arena(ctx.enter_context(nc.sbuf_tensor("arena", [P, Map.W], F32)))
        ps = ctx.enter_context(nc.psum_tensor("ps", [P, 8, 512], F32))
        mod_d = nc.dram_tensor("mod_scratch", (NC_ROWS, NMOD * D), F32, kind="Internal").ap()

        integers = {name: ctx.enter_context(nc.sbuf_tensor(name, [P, n], dtype))[:, :] for name, n, dtype in
                    (("expert0", TOPK, U32), ("expert1", TOPK, U32), ("keys", 2 * TOPK, U32), ("pairs", TOPK, U32),
                     ("halves", 2 * TOPK, U32), ("counting", TOPK, I32))}

        for stage, more in ((constants, ()), (stage_condition, (ps, A, mod_d)), (stage_s5, (ps, A, O)),
                            (stage_ssd, (ps, A, O)), (stage_query, (ps, A, mod_d)),
                            (stage_peer, (ps, A, O, mod_d, integers))):
            with nc.cleanup_on_exit():
                stage(nc, mem, nc.alloc_semaphore, *more)


_INS = ['x_prompt', 'x_sample', 'state_s5_re', 'state_s5_im', 'state_ssm', 'state_conv', 'c_prompt', 'c_sample',
        'w_ada', 'b_ada', 'g_norm1', 'g_norm2', 'w_in', 's5_a_re', 's5_a_im', 's5_log_dt', 's5_b_re', 's5_b_im',
        's5_c_re', 's5_c_im', 's5_d', 's5_w_glu', 's5_b_glu', 'w_branch_a', 'conv_w', 'conv_b', 'dt_bias', 'a_log',
        'd_skip', 'g_ssm_norm', 'w_branch_b', 'w_out', 'w_query', 'sub_keys', 'expert_down', 'expert_up', 'g_final',
        'w_ada_final', 'b_ada_final']
_OUTS = [(1, L, D), (NS, 1, D), (1, 1, NG5, ST5), (1, 1, NG5, ST5), (1, 1, NH, HD, SN), (1, 1, 3, CD),
         (1, NS, NG5, ST5), (1, NS, NG5, ST5), (1, NS, NH, HD, SN), (1, NS, 3, CD)]


def kernel(**inputs):
    import numpy as _np
    import concourse.bacc as _bacc
    from concourse import mybir as _mybir
    from concourse.bass_utils import run_bass_kernel_spmd as _run

    nc = _bacc.Bacc("TRN2", target_bir_lowering=False, num_devices=1)
    arrays, args = {}, {}
    for name in _INS:
        a = _np.ascontiguousarray(inputs[name])
        arrays[f"in_{name}_dram"] = a
        args[name] = nc.dram_tensor(f"in_{name}_dram", a.shape, _mybir.dt.from_np(a.dtype), kind="ExternalInput").ap()
    outs = [nc.dram_tensor(f"out_{i}_dram", shape, _mybir.dt.float32, kind="ExternalOutput").ap()
            for i, shape in enumerate(_OUTS)]
    program(nc, args, outs)
    r = _run(nc, [arrays], core_ids=[0])
    return tuple(r.results[0][f"out_{i}_dram"] for i in range(len(_OUTS)))
```

```python
import math
from contextlib import ExitStack

import numpy as np

import concourse.bass as bass
from concourse import mybir

F32 = mybir.dt.float32
U32 = mybir.dt.uint32
I32 = mybir.dt.int32
ALU = mybir.AluOpType
ACT = mybir.ActivationFunctionType
AX_X = mybir.AxisListType.X

P = 128
D = 1024
KD = D // P
L = 512
NS = 8
T = L + NS
NB = L // P
HALF = T // 2
NC_ROWS = NS + 1
NMOD = 8
EPS = 1e-6
G_EPS = 1e-5

S5W = 512
NG5 = 32
G5 = 16
ST5 = 64
NS5 = NG5 * ST5 // P
TB5 = 256

CD = 2048
NCV = CD // P
NH = 16
HD = 64
SN = 128
NGR = 4
HPG = 4

PH = 8
NK = 128
TOPK = 16
DQ = PH * 256
NEG = -3.0e38


class Link:

    def __init__(self, eng, sem):
        self.eng, self.sem, self.n = eng, sem, 0

    def __call__(self, ins):
        self.n += 1
        ins.then_inc(self.sem, 1)
        self.eng.wait_ge(self.sem, self.n)


class Arena:
    def __init__(self, tensor):
        self.t = tensor

    def __call__(self, at, *shape, rows=P):
        n = int(np.prod(shape))
        v = self.t[0:rows, at:at + n]
        if len(shape) == 2:
            return v.rearrange("p (a b) -> p a b", b=shape[1])
        if len(shape) == 3:
            return v.rearrange("p (a b c) -> p a b c", b=shape[1], c=shape[2])
        return v


class Map:
    W = 53000
    IDENT = 0
    ONES = 128
    HT = 256
    ZS = HT + KD * T
    GB = ZS + KD * T
    MG = GB + KD * T
    LOCAL = MG + KD * T
    S5_RING = LOCAL + KD * T
    SSD_RING = S5_RING + 2 * KD * 512 + 2 * 16 * 256 + 4 * T + 1024
    X1 = LOCAL
    H2 = X1 + 5 * D
    SC = H2 + 5 * D
    SCS = SC + NB * PH * 2 * NK
    QUERY = SCS + 2 * NK
    PEER = QUERY + KD * T + 2 * KD * 256 + 2 * PH * NK + 2 * T + 2 * PH * 64


C_U, C_Z, C_X, C_DT, C_G = 0, S5W, S5W + D, S5W + D + CD, S5W + D + CD + NH


def w_in_columns(A, c0, n=512):
    return A["w_in"][0].rearrange("(k p) n -> p k n", p=P)[:, :, c0:c0 + n]


def two(ps_tile):
    return ps_tile[:, :, 0:HALF]


def cols(ap):
    return ap.rearrange("p (a b) -> p a b", b=HALF)


def constants(nc, mem, sem):
    ident, ones = mem(Map.IDENT, P), mem(Map.ONES, P)
    s_const = sem("s_const")
    with nc.Block() as block:
        @block.gpsimd
        def _(pool):
            link = Link(pool, s_const)
            link(nc.gpsimd.memset(mem(Map.IDENT, 2 * P), 1.0))
            link(nc.gpsimd.affine_select(out=ident, in_=ident, compare_op=ALU.is_equal, fill=0.0,
                                         base=0, pattern=[[-1, P]], channel_multiplier=1))


def stage_condition(nc, mem, sem, ps, A, mod_d, s_first):
    M = Map.LOCAL
    ring = [mem(M + i * KD * 512, KD, 512) for i in range(4)]
    M += 4 * KD * 512
    bias = mem(M, NMOD * D, rows=NC_ROWS); M += NMOD * D
    x = mem(M, 5, D); M += 5 * D
    c = mem(M, D, rows=NC_ROWS); M += D
    sc = mem(M, D, rows=NC_ROWS); M += D
    cT = mem(M, KD, NC_ROWS); M += KD * NC_ROWS
    stat = mem(M, 5); M += 8
    rstd = mem(M, 5); M += 8
    assert M <= Map.W
    g1 = mem(Map.ZS, D)
    shift = mem(Map.ZS + D, 2, D)
    scale = mem(Map.GB, 2, D)
    mod = mem(Map.MG, 4, D, rows=NC_ROWS)
    hT = mem(Map.HT, KD, T)
    ident = mem(Map.IDENT, P)

    s_c, s_bias, s_x, s_g = sem("cd_c"), sem("cd_bias"), sem("cd_x"), sem("cd_g")
    s_w = [sem(f"cd_w{i}") for i in range(4)]
    s_silu, s_cps, s_cT = sem("cd_silu"), sem("cd_cps"), sem("cd_cT")
    s_mm, s_mod = sem("cd_mm"), sem("cd_mod")
    s_modw = [sem(f"cd_modw{i}") for i in range(4)]
    s_rows = sem("cd_rows")
    s_zero, s_sq, s_var, s_rstd = sem("cd_zero"), sem("cd_sq"), sem("cd_var"), sem("cd_rstd")
    s_h, s_hps, s_hT = sem("cd_h"), sem("cd_hps"), sem("cd_hT")
    s_dve = sem("cd_dve")
    NCH = NMOD * D // 512
    hparts = [(b, half) for b in range(5) for half in range(2)]

    def rows_of(b):
        return P if b < NB else NS

    with nc.Block() as block:
        @block.sync
        def _(sp):
            sp.dma_start(c[0:NS, :], A["c_sample"]).then_inc(s_c, 16)
            sp.dma_start(c[NS:NC_ROWS, :], A["c_prompt"]).then_inc(s_c, 16)
            wa = A["w_ada"][0].rearrange("(k p) n -> p k n", p=P)
            wf = A["w_ada_final"].rearrange("(k p) n -> p k n", p=P)

            def load_w(i):
                src = wa[:, :, i * 512:(i + 1) * 512] if i < 12 else wf[:, :, (i - 12) * 512:(i - 11) * 512]
                if i >= 4:
                    sp.wait_ge(s_mm, i - 3)
                sp.dma_start(ring[i % 4], src).then_inc(s_w[i % 4], 16)

            load_w(0)
            sp.dma_start(bias[:, 0:6 * D], A["b_ada"][0:1, :].partition_broadcast(NC_ROWS)).then_inc(s_bias, 16)
            sp.dma_start(bias[:, 6 * D:], A["b_ada_final"].rearrange("(a n) -> a n", a=1)
                         .partition_broadcast(NC_ROWS)).then_inc(s_bias, 16)
            load_w(1)
            sp.dma_start(x[:, 0:NB, :], A["x_prompt"][0].rearrange("(b p) d -> p b d", p=P)).then_inc(s_x, 16)
            sp.dma_start(x[0:NS, NB, :], A["x_sample"].rearrange("b s d -> (b s) d")).then_inc(s_x, 16)
            sp.dma_start(g1, A["g_norm1"][0:1, :].partition_broadcast(P)).then_inc(s_g, 16)
            for i in range(2, NCH):
                load_w(i)
            sp.wait_ge(s_mm, NCH)
            sp.dma_start(mem(Map.S5_RING, KD, 512), w_in_columns(A, C_U)).then_inc(s_first, 16)

        @block.scalar
        def _(act):
            act.wait_ge(s_c, 32)
            nc.scalar.activation(sc, c, ACT.Silu).then_inc(s_silu, 1)
            act.wait_ge(s_x, 32)
            act.wait_ge(s_zero, 1)
            junk = mem(Map.HT, D)
            for b in range(5):
                n = rows_of(b)
                nc.scalar.activation(junk[0:n, :], x[0:n, b, :], ACT.Square,
                                     accum_out=stat[0:n, b:b + 1]).then_inc(s_sq, 1)
                act.wait_ge(s_sq, b + 1)
            act.wait_ge(s_var, 1)
            nc.scalar.activation(rstd, stat, ACT.Sqrt).then_inc(s_rstd, 1)

            def store_mod(m):
                act.wait_ge(s_mod, 2 * m + 2)
                act.dma_start(mod_d[:, m * D:(m + 1) * D], mod[:, m % 4, :]).then_inc(s_modw[m % 4], 16)

            store_mod(0)
            store_mod(1)
            act.wait_ge(s_modw[0], 16)
            act.wait_ge(s_modw[1], 16)
            for dst, m in ((shift, 0), (scale, 1)):
                act.dma_start(dst[:, 0, :], mod_d[NS:NC_ROWS, m * D:(m + 1) * D].partition_broadcast(P)).then_inc(s_rows, 16)
                act.dma_start(dst[0:NS, 1, :], mod_d[0:NS, m * D:(m + 1) * D]).then_inc(s_rows, 16)
            for m in range(2, NMOD):
                store_mod(m)
            for n, (b, half) in enumerate(hparts):
                act.wait_ge(s_hps, n + 1)
                m = rows_of(b)
                nc.scalar.activation(hT[:, 4 * half:4 * half + 4, b * P:b * P + m],
                                     ps[:, 4 + n % 4, :].rearrange("p (k t) -> p k t", k=4)[:, :, 0:m],
                                     ACT.Copy).then_inc(s_hT, 1)
            for w in s_modw:
                act.wait_ge(w, 16 * NMOD // 4)

        @block.tensor
        def _(pe):
            pe.wait_ge(s_silu, 1)
            for k in range(KD):
                last = nc.tensor.transpose(ps[:, 4, k * 16:k * 16 + NC_ROWS], sc[:, k * P:(k + 1) * P],
                                           ident[0:NC_ROWS, 0:NC_ROWS])
            last.then_inc(s_cps, 1)
            pe.wait_ge(s_cT, 1)
            for i in range(NCH):
                pe.wait_ge(s_w[i % 4], 16 * (i // 4 + 1))
                if i >= 4:
                    pe.wait_ge(s_mod, i - 3)
                for k in range(KD):
                    last = nc.tensor.matmul(ps[0:NC_ROWS, i % 4, :], cT[:, k, :], ring[i % 4][:, k, :],
                                            start=(k == 0), stop=(k == KD - 1))
                last.then_inc(s_mm, 1)
            for n, (b, half) in enumerate(hparts):
                pe.wait_ge(s_h, b + 1)
                if n >= 4:
                    pe.wait_ge(s_hT, n - 3)
                m = rows_of(b)
                for k in range(4):
                    kk = 4 * half + k
                    last = nc.tensor.transpose(ps[:, 4 + n % 4, k * P:k * P + m],
                                               x[0:m, b, kk * P:(kk + 1) * P], ident[0:m, 0:m])
                last.then_inc(s_hps, 1)

        @block.vector
        def _(dve):
            link = Link(dve, s_dve)
            nc.vector.memset(stat, 1.0).then_inc(s_zero, 1)
            dve.wait_ge(s_cps, 1)
            nc.vector.tensor_copy(cT, ps[:, 4, 0:KD * 16].rearrange("p (k c) -> p k c", c=16)[:, :, 0:NC_ROWS])\
                .then_inc(s_cT, 1)
            dve.wait_ge(s_sq, 5)
            link(nc.vector.tensor_scalar(stat, stat, 1.0 / D, EPS, ALU.mult, ALU.add))
            nc.vector.reciprocal(stat, stat).then_inc(s_var, 1)
            dve.wait_ge(s_bias, 32)

            def evict(i):
                dve.wait_ge(s_mm, i + 1)
                if i >= 8:
                    dve.wait_ge(s_modw[(i // 2) % 4], 16)
                nc.vector.tensor_tensor(mod[:, (i // 2) % 4, (i % 2) * 512:(i % 2 + 1) * 512],
                                        ps[0:NC_ROWS, i % 4, :], bias[:, i * 512:(i + 1) * 512],
                                        ALU.add).then_inc(s_mod, 1)

            for i in range(6):
                evict(i)
            dve.wait_ge(s_rstd, 1)
            dve.wait_ge(s_g, 16)
            dve.wait_ge(s_rows, 64)
            link(nc.vector.scalar_tensor_tensor(out=scale[:, 0, :], in0=scale[:, 0, :], scalar=1.0, in1=g1,
                                                op0=ALU.add, op1=ALU.mult))
            link(nc.vector.scalar_tensor_tensor(out=scale[0:NS, 1, :], in0=scale[0:NS, 1, :], scalar=1.0,
                                                in1=g1[0:NS, :], op0=ALU.add, op1=ALU.mult))
            for b in range(5):
                n, r = rows_of(b), b // NB
                link(nc.vector.scalar_tensor_tensor(out=x[0:n, b, :], in0=x[0:n, b, :], scalar=rstd[0:n, b:b + 1],
                                                    in1=scale[0:n, r, :], op0=ALU.mult, op1=ALU.mult))
                nc.vector.tensor_tensor(x[0:n, b, :], x[0:n, b, :], shift[0:n, r, :], ALU.add).then_inc(s_h, 1)
                evict(6 + 2 * b)
                evict(7 + 2 * b)


TWO_PI = 2.0 * math.pi
CW1 = 6.28125
CW2 = float(np.float32(int((TWO_PI - CW1) * 2 ** 20) / 2 ** 20))
CW3 = TWO_PI - CW1 - CW2
ROUND = 1.5 * 2.0 ** 23
NLEV = 9
V_MAG, V_AR, V_AI, V_FR, V_FI, V_COS = 0, 1, 2, 3, 4, 5
V_SIN = V_COS + NLEV
NV = V_SIN + NLEV


def stage_s5(nc, mem, sem, ps, A, O, s_first, s_ssd):
    hT, zs, gB, mg = (mem(m, KD, T) for m in (Map.HT, Map.ZS, Map.GB, Map.MG))
    ident = mem(Map.IDENT, P)
    M = Map.LOCAL

    def take(n):
        nonlocal M
        M += n
        return M - n

    gA = mem(take(KD * T), KD, T)
    ring = [mem(take(KD * 512), KD, 512) for _ in range(2)]
    tabs = take(2 * NS5 * TB5)
    RC, RS = mem(tabs, NS5, TB5), mem(tabs + NS5 * TB5, NS5, TB5)
    u = mem(take(4 * T), 4, T)
    LB = mem(take(2 * 4 * P), 2, 4, P)
    CTW = NS5 * P + P
    assert M == Map.SSD_RING
    ct = take(2 * CTW)
    CT = [mem(ct + i * CTW, NS5, P) for i in range(2)]
    parbase = Map.ZS
    par = mem(parbase, NV, P, rows=NS5)
    PT = mem(take(NV * NS5), NV, NS5)
    tmp = Map.ZS + NV * P
    ye = take(4 * 512)
    vec = mem(take(P), P, rows=8)
    vT = mem(take(8), 8)
    ldt = mem(take(8), 8, rows=NS5)
    fin = mem(take(2 * NS5), 2, NS5)
    work = take(8 * 512)
    s0 = mem(work + 2560, 2, P)
    s0T = mem(take(2 * P), 2, P)
    sn = mem(take(2 * P), 2, NS, NS5)
    so = mem(work + 2048, 2, P)
    fo = mem(work + 2304, 2, P, rows=NS5)
    mark = mem(take(1), 1)
    assert M <= Map.W, M
    bn = mem(work, 2, NS5, G5)
    bb = mem(work + 512, 2, NS5, G5)
    t16 = mem(work + 1024, NS5, G5)
    cn = mem(work + 1536, 2, 4, P)
    X = mem(Map.LOCAL, 2, NS5 * P)
    X3 = mem(Map.LOCAL, 2 * NS5, P)
    tt = [mem(at + i * 2048, NS5, P) for at in (Map.ZS, Map.MG) for i in range(2)]
    wide = [mem(Map.MG + i * NLEV * P, NLEV * P, rows=NS5) for i in range(2)]
    prod = [mem(Map.MG + i * 512, 2, 256) for i in range(4)]
    wk = [mem(work + i * 512, 2, 256) for i in range(8)]
    yg = mem(tabs, 4, T)
    ya = mem(tabs + 4 * T, 4, T)
    sg = mem(tabs + 8 * T, T)

    s_par, s_vec, s_bc, s_st = sem("s5_par"), sem("s5_vec"), sem("s5_bc"), sem("s5_st")
    s_w = [sem(f"s5_w{i}") for i in range(2)]
    s_proj, s_pev = sem("s5_proj"), sem("s5_pev")
    s_exp, s_ang, s_trig, s_parok = sem("s5_exp"), sem("s5_ang"), sem("s5_trig"), sem("s5_parok")
    s_tps, s_PT, s_X, s_Xps, s_LB = sem("s5_tps"), sem("s5_PT"), sem("s5_X"), sem("s5_Xps"), sem("s5_LB")
    s_cps, s_CT, s_zero = sem("s5_cps"), sem("s5_CT"), sem("s5_zero")
    s_bu, s_buread, s_S = sem("s5_bu"), sem("s5_buread"), sem("s5_S")
    s_y, s_yread, s_g, s_gelu = sem("s5_y"), sem("s5_yread"), sem("s5_g"), sem("s5_gelu")
    s_new, s_glu, s_sig, s_ya, s_br, s_brread = (sem("s5_" + n) for n in ("new", "glu", "sig", "ya", "br", "brread"))
    s_bb, s_ops, s_ocp, s_out, s_dve, s_fin = (sem("s5_" + n) for n in ("bb", "ops", "ocp", "out", "dve", "fin"))
    s_wg, s_wbr = sem("s5_wg"), sem("s5_wbr")

    dest = ([(u[:, i, :], ACT.Copy) for i in range(4)] + [(gB[:, i, :], ACT.Sigmoid) for i in range(KD)]
            + [(gA[:, i, :], ACT.Sigmoid) for i in range(KD)] + [(zs[:, i, :], ACT.Silu) for i in range(KD)])
    col0 = [C_U, C_G + D, C_G + D + 512, C_G, C_G + 512, C_Z, C_Z + 512]
    NP = len(dest)
    EARLY = 4 + KD
    LATE = 3
    glu_w = mem(0 + Map.LOCAL + KD * T, 4, 512)
    br_w = mem(Map.LOCAL + KD * T + KD * 512, 4, D)

    def S_of(i):
        return (wk[4 + 2 * (i % 2)], wk[5 + 2 * (i % 2)])

    with nc.Block() as block:
        @block.sync
        def _(sp):
            w = A["w_in"][0].rearrange("(k p) n -> p k n", p=P)
            for v, name in ((V_AR, "s5_a_re"), (V_AI, "s5_a_im")):
                sp.dma_start(par[:, v, :], A[name][0].rearrange("(s g) p -> s (g p)", g=2)).then_inc(s_par, 16)
            sp.dma_start(ldt[:, 0:2], A["s5_log_dt"][0].rearrange("(s g) -> s g", g=2)).then_inc(s_par, 16)
            sp.dma_start(ring[1], w[:, :, col0[1]:col0[1] + 512]).then_inc(s_w[1], 16)
            sp.dma_start(vec[0:4, :], A["s5_d"][0].rearrange("(u g) h -> u (g h)", u=4)).then_inc(s_vec, 16)
            sp.dma_start(vec[4:8, :], A["s5_b_glu"][0].rearrange("(u c) -> u c", u=4)).then_inc(s_vec, 16)
            for i, (b, c) in enumerate((("s5_b_re", "s5_c_re"), ("s5_b_im", "s5_c_im"))):
                sp.dma_start(bn[:, i, :, :], A[b][0].rearrange("(s g) p h -> (g p) s h", g=2)).then_inc(s_bc, 16)
                for dup in range(2):
                    sp.dma_start(cn[:, i, :, dup * 64:dup * 64 + 64],
                                 A[c][0].rearrange("(u g) h p -> (g h) u p", u=4)).then_inc(s_bc, 16)
            for i, name in enumerate(("state_s5_re", "state_s5_im")):
                sp.dma_start(s0[:, i, :], A[name][0].rearrange("b (s g) p -> (b s) (g p)", g=2)).then_inc(s_st, 16)
            for i in range(2, 7):
                sp.wait_ge(s_proj, 4 * (i - 1))
                sp.dma_start(ring[i % 2], w[:, :, col0[i]:col0[i] + 512]).then_inc(s_w[i % 2], 16)
            sp.wait_ge(s_proj, NP)
            sp.dma_start(glu_w, A["s5_w_glu"][0].rearrange("(k p) n -> p k n", p=P)).then_inc(s_wg, 16)
            sp.dma_start(br_w, A["w_branch_a"][0].rearrange("(k p) n -> p k n", p=P)).then_inc(s_wbr, 16)
            sp.wait_ge(s_y, NS5 + 1)
            sp.dma_start(mem(Map.SSD_RING, KD, 512), w_in_columns(A, C_X)).then_inc(s_ssd, 16)
            sp.wait_ge(s_ocp, 4)
            for i in range(2):
                sp.dma_start(O[2 + i][0, 0].rearrange("(s g) p -> s (g p)", g=2), fo[:, i, :]).then_inc(s_out, 16)
                sp.dma_start(O[6 + i][0].rearrange("b (s g) p -> (b s) (g p)", g=2), so[:, i, :]).then_inc(s_out, 16)
            sp.wait_ge(s_out, 64)

        @block.gpsimd
        def _(pool):
            nc.gpsimd.memset(X, 0.0).then_inc(s_zero, 1)
            nc.gpsimd.memset(mem(ct, 2 * CTW), 0.0).then_inc(s_zero, 1)
            pool.wait_ge(s_zero, 2)
            pool.wait_ge(s_bb, 1)
            for g in range(2):
                rows = slice(64 * g, 64 * g + 64)
                if g:
                    pool.wait_ge(s_X, 1)
                for j in range(2):
                    for ut in range(4):
                        flat = X[rows, j, 512 * ut:512 * ut + 512]
                        for q in range(4):
                            last = nc.gpsimd.tensor_copy(flat[:, 160 * q + 16 * g:160 * q + 16 * g + 16],
                                                         bb[rows, j, 4 * ut + q, :])
                last.then_inc(s_X, 1)

        @block.scalar
        def _(act):
            def evict(n):
                act.wait_ge(s_proj, n + 1)
                nc.scalar.activation(cols(dest[n][0]), two(ps[:, 5:7, :]), dest[n][1]).then_inc(s_pev, 1)

            act.wait_ge(s_par, 48)
            nc.scalar.activation(ldt[:, 2:4], ldt[:, 0:2], ACT.Exp).then_inc(s_exp, 1)
            act.wait_ge(s_ang, 1)
            nc.scalar.activation(par[:, V_MAG, :], par[:, V_MAG, :], ACT.Exp).then_inc(s_exp, 1)
            for n in range(4):
                evict(n)
            act.wait_ge(s_ang, 2)
            sc = mem(parbase + V_COS * P, 2 * NLEV * P, rows=NS5)
            nc.scalar.activation(sc, sc, ACT.Sin).then_inc(s_trig, 1)
            for n in range(4, 9):
                evict(n)
            act.wait_ge(s_Xps, 1)
            for i in range(2):
                nc.scalar.activation(LB[:, i, :, :], ps[:, i, :].rearrange("p (u n) -> p u n", u=4),
                                     ACT.Copy).then_inc(s_LB, 1)
            act.wait_ge(s_cps, 1)
            act.wait_ge(s_zero, 2)
            for i in range(2):
                for ut in range(4):
                    for half in range(2):
                        rows = slice(64 * half, 64 * half + 64)
                        dst = mem(ct + i * CTW + 512 * ut, 4, 160)[rows, :, 16 * half:16 * half + 16]
                        src = ps[rows, 2 + i, ut * P:(ut + 1) * P].rearrange("p (q r) -> p q r", q=4)[
                            :, :, 16 * half:16 * half + 16]
                        nc.scalar.activation(dst, src, ACT.Copy, scale=1.0 - 2.0 * i).then_inc(s_CT, 1)
            for n in range(9, EARLY):
                evict(n)
            n = EARLY
            for i in range(NS5):
                if n < NP - LATE:
                    evict(n)
                    n += 1
                act.wait_ge(s_S, i + 1)
                for j in range(2):
                    nc.scalar.activation(fin[:, j, i:i + 1], S_of(i)[j][:, 1, 255:256], ACT.Copy).then_inc(s_fin, 1)
            while n < NP:
                evict(n)
                n += 1
            for ut in range(4):
                act.wait_ge(s_g, ut + 1)
                nc.scalar.activation(yg[:, ut, 0:L], yg[:, ut, 0:L], ACT.Gelu).then_inc(s_gelu, 1)
            act.wait_ge(s_g, 5)
            nc.scalar.activation(yg[:, :, L:T], yg[:, :, L:T], ACT.Gelu).then_inc(s_gelu, 1)
            for m in range(4):
                act.wait_ge(s_glu, m + 1)
                if m:
                    act.wait_ge(s_ya, m)
                nc.scalar.activation(cols(sg), two(ps[:, 2 * (m % 2):2 * (m % 2) + 2, :]), ACT.Sigmoid,
                                     bias=vT[:, 4 + m:5 + m]).then_inc(s_sig, 1)
            act.wait_ge(s_ops, 1)
            for i in range(2):
                nc.scalar.activation(fo[:, i, :], ps[0:NS5, 4, i * P:(i + 1) * P], ACT.Copy).then_inc(s_ocp, 1)
                nc.scalar.activation(so[:, i, :], ps[:, 4, (2 + i) * P:(3 + i) * P], ACT.Copy).then_inc(s_ocp, 1)

        @block.tensor
        def _(pe):
            def proj(n):
                i, m = n // 4, n % 4
                if n == 0:
                    pe.wait_ge(s_first, 16)
                elif m == 0:
                    pe.wait_ge(s_w[i % 2], 16 * ((i + 1) // 2))
                if n:
                    pe.wait_ge(s_pev, n)
                for k in range(KD):
                    for h in range(2):
                        last = nc.tensor.matmul(ps[:, 5 + h, 0:HALF], ring[i % 2][:, k, m * P:(m + 1) * P],
                                                hT[:, k, h * HALF:(h + 1) * HALF], start=(k == 0), stop=(k == KD - 1))
                last.then_inc(s_proj, 1)

            for n in range(6):
                proj(n)
            pe.wait_ge(s_parok, 1)
            for v in range(NV):
                last = nc.tensor.transpose(ps[:, 4, v * NS5:(v + 1) * NS5], par[:, v, :], ident[0:NS5, 0:NS5])
            pe.wait_ge(s_vec, 32)
            last = nc.tensor.transpose(ps[:, 4, NV * NS5:NV * NS5 + 8], vec, ident[0:8, 0:8])
            pe.wait_ge(s_st, 32)
            for i in range(2):
                last = nc.tensor.transpose(ps[:, 7, i * P:(i + 1) * P], s0[:, i, :], ident)
            last.then_inc(s_tps, 1)
            for n in range(6, 9):
                proj(n)
            pe.wait_ge(s_X, 2)
            for i in range(2):
                for ut in range(4):
                    for q in range(4):
                        last = nc.tensor.matmul(ps[:, i, ut * P:(ut + 1) * P], X3[:, NS5 * i + 4 * ut + q, :], ident,
                                                start=(q == 0), stop=(q == 3))
            last.then_inc(s_Xps, 1)
            pe.wait_ge(s_bc, 96)
            for i in range(2):
                for ut in range(4):
                    last = nc.tensor.transpose(ps[:, 2 + i, ut * P:(ut + 1) * P], cn[:, i, ut, :], ident)
            last.then_inc(s_cps, 1)
            for n in range(9, EARLY):
                proj(n)

            def bu(i):
                if i == 0:
                    pe.wait_ge(s_LB, 2)
                    pe.wait_ge(s_PT, 1)
                    pe.wait_ge(s_pev, 4)
                if i == 1:
                    pe.wait_ge(s_CT, 16)
                if i >= 2:
                    pe.wait_ge(s_buread, i - 1)
                ut, q = i // 4, i % 4
                rows = slice(32 * q, 32 * q + 32)
                for j in range(2):
                    nc.tensor.matmul(ps[:, 2 * (i % 2) + j, :], LB[rows, j, ut, :], u[rows, ut, 0:L],
                                     start=True, stop=True)
                if i:
                    pe.wait_ge(s_bu, i)
                for j in range(2):
                    last = nc.tensor.matmul(ps[:, 4, j * P + i * NS:j * P + (i + 1) * NS], LB[rows, j, ut, :],
                                            u[rows, ut, L:T], start=True, stop=True)
                last.then_inc(s_bu, 1)

            def y(i):
                ut, q = i // 4, i % 4
                pe.wait_ge(s_S, i + 1)
                if q == 0 and ut:
                    pe.wait_ge(s_yread, ut)
                for j in range(2):
                    last = nc.tensor.matmul(ps[:, 7, :], CT[j][:, i, :], S_of(i)[j].rearrange("p a b -> p (a b)"),
                                            start=(q == 0 and j == 0), stop=(q == 3 and j == 1))
                last.then_inc(s_y, 1)

            n = EARLY
            bu(0)
            for i in range(NS5):
                if n < NP - LATE:
                    proj(n)
                    n += 1
                if i + 1 < NS5:
                    bu(i + 1)
                if i >= 1:
                    y(i - 1)
            y(NS5 - 1)
            while n < NP:
                proj(n)
                n += 1
            pe.wait_ge(s_new, 1)
            for ut in range(4):
                for q in range(4):
                    for j in range(2):
                        last = nc.tensor.matmul(ps[:, 3, ut * NS:(ut + 1) * NS], CT[j][:, 4 * ut + q, :],
                                                sn[:, j, :, 4 * ut + q], start=(q == 0 and j == 0),
                                                stop=(q == 3 and j == 1))
            last.then_inc(s_y, 1)
            pe.wait_ge(s_fin, 2 * NS5)
            for i in range(2):
                nc.tensor.transpose(ps[0:NS5, 4, i * P:(i + 1) * P], fin[:, i, :], ident)
                last = nc.tensor.transpose(ps[:, 4, (2 + i) * P:(3 + i) * P],
                                           sn[:, i, :, :].rearrange("p b s -> p (b s)"), ident)
            last.then_inc(s_ops, 1)
            pe.wait_ge(s_gelu, 5)
            pe.wait_ge(s_wg, 16)
            for m in range(4):
                if m >= 2:
                    pe.wait_ge(s_sig, m - 1)
                for k in range(4):
                    for h in range(2):
                        last = nc.tensor.matmul(ps[:, 2 * (m % 2) + h, 0:HALF], glu_w[:, k, m * P:(m + 1) * P],
                                                yg[:, k, h * HALF:(h + 1) * HALF], start=(k == 0), stop=(k == 3))
                last.then_inc(s_glu, 1)
            pe.wait_ge(s_ya, 4)
            pe.wait_ge(s_wbr, 16)
            for m in range(KD):
                if m >= 2:
                    pe.wait_ge(s_brread, m - 1)
                for k in range(4):
                    for h in range(2):
                        last = nc.tensor.matmul(ps[:, 2 * (m % 2) + h, 0:HALF], br_w[:, k, m * P:(m + 1) * P],
                                                ya[:, k, h * HALF:(h + 1) * HALF], start=(k == 0), stop=(k == 3))
                last.then_inc(s_br, 1)

        @block.vector
        def _(dve):
            link = Link(dve, s_dve)
            V = nc.vector
            t = [mem(tmp + i * P, P, rows=NS5) for i in range(8)]
            ar, ai, mag = par[:, V_AR, :], par[:, V_AI, :], par[:, V_MAG, :]
            dve.wait_ge(s_exp, 1)
            dtb = ldt[:, 2:4].unsqueeze(2).to_broadcast([NS5, 2, 64])
            g2 = lambda x: x.rearrange("p (g n) -> p g n", g=2)
            V.tensor_tensor(g2(mag), g2(ar), dtb, ALU.mult).then_inc(s_ang, 1)
            link(V.tensor_tensor(g2(t[0]), g2(ai), dtb, ALU.mult))
            sn_all, cs_all = (mem(parbase + v * P, NLEV * P, rows=NS5) for v in (V_SIN, V_COS))
            for j in range(NLEV):
                last = V.tensor_scalar(par[:, V_SIN + j, :], t[0], 2.0 ** j, None, ALU.mult)
            link(last)
            link(V.tensor_scalar(wide[0], sn_all, 1.0 / TWO_PI, ROUND, ALU.mult, ALU.add))
            link(V.tensor_scalar(wide[0], wide[0], ROUND, None, ALU.subtract))
            for cw in (CW1, CW2, CW3):
                link(V.scalar_tensor_tensor(out=sn_all, in0=wide[0], scalar=-cw, in1=sn_all, op0=ALU.mult, op1=ALU.add))
            link(V.tensor_scalar(sn_all, sn_all, 3.1415925, -3.1415925, ALU.min, ALU.max))
            link(V.tensor_scalar(wide[1], sn_all, -1.0, None, ALU.mult))
            link(V.tensor_tensor(wide[1], wide[1], sn_all, ALU.max))
            link(V.tensor_scalar(cs_all, wide[1], -1.0, math.pi / 2, ALU.mult, ALU.add))
            V.memset(t[3], 0.0).then_inc(s_ang, 1)
            link(V.tensor_tensor(t[4], ar, ar, ALU.mult))
            link(V.tensor_tensor(t[5], ai, ai, ALU.mult))
            link(V.tensor_tensor(t[4], t[4], t[5], ALU.add))
            link(V.reciprocal(t[4], t[4]))
            dve.wait_ge(s_trig, 1)
            dve.wait_ge(s_exp, 2)
            link(V.tensor_tensor(t[0], mag, par[:, V_COS, :], ALU.mult))
            link(V.tensor_tensor(t[1], mag, par[:, V_SIN, :], ALU.mult))
            link(V.tensor_scalar(t[2], t[0], -1.0, None, ALU.add))
            fr, fi = par[:, V_FR, :], par[:, V_FI, :]
            link(V.tensor_tensor(t[5], t[2], ar, ALU.mult))
            link(V.tensor_tensor(t[6], t[1], ai, ALU.mult))
            link(V.tensor_tensor(t[5], t[5], t[6], ALU.add))
            link(V.tensor_tensor(fr, t[5], t[4], ALU.mult))
            link(V.tensor_tensor(t[5], t[1], ar, ALU.mult))
            link(V.tensor_tensor(t[6], t[2], ai, ALU.mult))
            link(V.tensor_tensor(t[5], t[5], t[6], ALU.subtract))
            link(V.tensor_tensor(fi, t[5], t[4], ALU.mult))
            link(V.tensor_copy(ar, t[0]))
            V.tensor_copy(ai, t[1]).then_inc(s_parok, 1)
            dve.wait_ge(s_tps, 1)
            link(V.tensor_copy(vT, ps[:, 4, NV * NS5:NV * NS5 + 8]))
            link(V.tensor_copy(s0T, ps[:, 7, 0:2 * P].rearrange("p (i n) -> p i n", i=2)))
            V.tensor_copy(PT, ps[:, 4, 0:NV * NS5].rearrange("p (v s) -> p v s", v=NV)).then_inc(s_PT, 1)
            dve.wait_ge(s_PT, 1)
            dve.wait_ge(s_bc, 96)
            frb, fib = (PT[:, v, :].unsqueeze(2).to_broadcast([P, NS5, G5]) for v in (V_FR, V_FI))
            for j, (p, q, op) in enumerate(((0, 1, ALU.subtract), (1, 0, ALU.add))):
                link(V.tensor_tensor(bb[:, j, :, :], frb, bn[:, p, :, :], ALU.mult))
                link(V.tensor_tensor(t16, fib, bn[:, q, :, :], ALU.mult))
                link(V.tensor_tensor(bb[:, j, :, :], bb[:, j, :, :], t16, op))
            V.memset(t[7], 0.0).then_inc(s_bb, 1)
            link(V.memset(RC[:, :, 0:1], 1.0))
            link(V.memset(RS[:, :, 0:1], 0.0))
            for j in range(NLEV - 1):
                m = 2 ** j
                ec, es = (PT[:, v + j, :].unsqueeze(2).to_broadcast([P, NS5, m]) for v in (V_COS, V_SIN))
                cc, ss, cs, sc = (x[:, :, 0:m] for x in tt)
                V.tensor_tensor(cc, RC[:, :, 0:m], ec, ALU.mult)
                V.tensor_tensor(ss, RS[:, :, 0:m], es, ALU.mult)
                V.tensor_tensor(cs, RC[:, :, 0:m], es, ALU.mult)
                link(V.tensor_tensor(sc, RS[:, :, 0:m], ec, ALU.mult))
                V.tensor_tensor(RC[:, :, m:2 * m], cc, ss, ALU.subtract)
                link(V.tensor_tensor(RS[:, :, m:2 * m], cs, sc, ALU.add))

            def y_of(ut):
                dve.wait_ge(s_y, 4 * ut + 4)
                V.scalar_tensor_tensor(out=yg_early(ut), in0=u[:, ut, 0:L], scalar=vT[:, ut:ut + 1], in1=ps[:, 7, :],
                                       op0=ALU.mult, op1=ALU.add).then_inc(s_yread, 1)

            def yg_early(ut):
                return mem(ye + ut * 512, 512)

            for i in range(NS5):
                br, bi = (ps[:, 2 * (i % 2) + j, :].rearrange("p (a b) -> p a b", a=2) for j in range(2))
                c, s = (x[:, i:i + 1, :].to_broadcast([P, 2, TB5]) for x in (RC, RS))
                wr, wi = wk[0], wk[1]
                t1, t2, t3, t4 = prod
                sr, si = S_of(i)
                dve.wait_ge(s_bu, i + 1)
                if i:
                    dve.wait_ge(s_S, i)
                V.tensor_tensor(t1, br, c, ALU.mult)
                V.tensor_tensor(t2, bi, s, ALU.mult)
                V.tensor_tensor(t3, bi, c, ALU.mult)
                V.tensor_tensor(t4, br, s, ALU.mult).then_inc(s_buread, 1)
                dve.wait_ge(s_buread, i + 1)
                V.tensor_tensor(wr, t1, t2, ALU.add)
                link(V.tensor_tensor(wi, t3, t4, ALU.subtract))
                magb = PT[:, V_MAG, i:i + 1].to_broadcast([P, TB5])
                ec, es = PT[:, V_COS + NLEV - 1, i:i + 1], PT[:, V_SIN + NLEV - 1, i:i + 1]
                V.tensor_tensor_scan(wr[:, 0, :], magb, wr[:, 0, :], 0.0, ALU.mult, ALU.add)
                link(V.tensor_tensor_scan(wi[:, 0, :], magb, wi[:, 0, :], 0.0, ALU.mult, ALU.add))
                er, ei = wr[:, 0, 255:256], wi[:, 0, 255:256]
                q = [t1[:, 0, x:x + 1] for x in range(4)]
                V.tensor_tensor(q[0], ei, es, ALU.mult)
                link(V.tensor_tensor(q[1], ei, ec, ALU.mult))
                V.scalar_tensor_tensor(out=q[2], in0=er, scalar=ec, in1=q[0], op0=ALU.mult, op1=ALU.subtract)
                link(V.scalar_tensor_tensor(out=q[3], in0=er, scalar=es, in1=q[1], op0=ALU.mult, op1=ALU.add))
                V.tensor_tensor_scan(wr[:, 1, :], magb, wr[:, 1, :], q[2], ALU.mult, ALU.add)
                link(V.tensor_tensor_scan(wi[:, 1, :], magb, wi[:, 1, :], q[3], ALU.mult, ALU.add))
                V.tensor_tensor(t1, wr, c, ALU.mult)
                V.tensor_tensor(t2, wi, s, ALU.mult)
                V.tensor_tensor(t3, wr, s, ALU.mult)
                link(V.tensor_tensor(t4, wi, c, ALU.mult))
                if i >= 2:
                    dve.wait_ge(s_y, i - 1)
                    dve.wait_ge(s_fin, 2 * (i - 1))
                V.tensor_tensor(sr, t1, t2, ALU.subtract)
                V.tensor_tensor(si, t3, t4, ALU.add).then_inc(s_S, 1)
                if i >= 4 and i % 4 == 1:
                    y_of(i // 4 - 1)
            y_of(3)
            dve.wait_ge(s_yread, 4)
            bus = [ps[:, 4, j * P:(j + 1) * P].rearrange("p (s b) -> p s b", b=NS) for j in range(2)]
            old = [s0T[:, j, :].rearrange("p (b s) -> p s b", s=NS5) for j in range(2)]
            new = [sn[:, j, :, :].rearrange("p b s -> p s b") for j in range(2)]
            abr, abi = (PT[:, v, :].unsqueeze(2).to_broadcast([P, NS5, NS]) for v in (V_AR, V_AI))
            w1, w2 = (mem(work + 1024 + x * P, NS5, NS) for x in range(2))
            for j, (p, q, op) in enumerate(((0, 1, ALU.subtract), (1, 0, ALU.add))):
                link(V.tensor_tensor(w1, abr, old[p], ALU.mult))
                link(V.tensor_tensor(w2, abi, old[q], ALU.mult))
                link(V.tensor_tensor(w1, w1, w2, op))
                link(V.tensor_tensor(new[j], w1, bus[j], ALU.add))
            V.memset(mark, 0.0).then_inc(s_new, 1)
            for ut in range(4):
                V.tensor_copy(yg[:, ut, 0:L], yg_early(ut)).then_inc(s_g, 1)
            dve.wait_ge(s_y, NS5 + 1)
            for ut in range(4):
                last = V.scalar_tensor_tensor(out=yg[:, ut, L:T], in0=u[:, ut, L:T], scalar=vT[:, ut:ut + 1],
                                              in1=ps[:, 3, ut * NS:(ut + 1) * NS], op0=ALU.mult, op1=ALU.add)
                if ut < 3:
                    link(last)
            last.then_inc(s_g, 1)
            for m in range(4):
                dve.wait_ge(s_sig, m + 1)
                V.tensor_tensor(ya[:, m, :], yg[:, m, :], sg, ALU.mult).then_inc(s_ya, 1)
            for m in range(KD):
                dve.wait_ge(s_br, m + 1)
                V.tensor_tensor(cols(mg[:, m, :]), two(ps[:, 2 * (m % 2):2 * (m % 2) + 2, :]),
                                cols(gA[:, m, :]), ALU.mult).then_inc(s_brread, 1)


def stage_ssd(nc, mem, sem, ps, A, O, bc_d, s_ssd):
    hT, zs, gB, mg = (mem(m, KD, T) for m in (Map.HT, Map.ZS, Map.GB, Map.MG))
    ident, ones = mem(Map.IDENT, P), mem(Map.ONES, P)
    M = Map.LOCAL

    def take(n):
        nonlocal M
        M += n
        return M - n

    cv = mem(take(NCV * T), NCV, T)
    raw = [mem(take(528), 528) for _ in range(2)]
    scr = take(10240)
    ecs, lm, cs_c = mem(scr, NH, P), mem(scr + 2048, NH, P), mem(scr + 4096, NH, P)
    xdt, xdd = mem(scr + 6144, NH, HD), mem(scr + 7168, NH, HD)
    btm, cbm = mem(scr + 8192, NGR, P), mem(scr + 8704, NGR, P)
    st = mem(scr + 9216, NH, HD)
    sel = mem(take(NH * P), NH, P, rows=NH)
    ek = mem(take(KD * P), KD, P, rows=NH)
    mask = mem(take(P), P)
    vn = mem(scr + 4096, P, rows=88)
    vT = mem(take(88), 88)
    hn = mem(scr, CD, rows=3 * NS)
    hist = mem(take(NCV * 3 * NS), NCV, 3 * NS)
    tail = mem(take(NCV * 11), NCV, 11)
    tl = mem(scr + 7168, CD, rows=11)
    assert M <= Map.SSD_RING
    ring_at = Map.SSD_RING
    M = ring_at + 2 * KD * 512
    ring = [mem(ring_at + i * KD * 512, KD, 512) for i in range(2)]
    brw = mem(ring_at, KD, D)
    dtw = mem(take(KD * NH), KD, NH)
    hp = mem(take(8), 8, rows=NH)
    dtv, csv = mem(take(T), T, rows=NH), mem(take(L), L, rows=NH)
    rex = mem(take(17), 17, rows=NH)
    ex = mem(take(KD * 17), KD, 17)
    tm = mem(take(P), NB, 2, NH)
    xs_s = mem(take(KD * NS), KD, NS)
    ys_s = mem(take(KD * NS), KD, NS)
    h0 = [mem(ring_at + i * KD * SN, KD, SN) for i in range(3)]
    tb = mem(ring_at + 3 * D, KD, SN)
    bcb = [mem(ring_at + (4 + i) * D, 2, NGR, SN) for i in range(2)]
    bcs = mem(ring_at + 6 * D, D, rows=NS)
    hout = mem(scr + 9216, KD, SN)
    sq = mem(scr, KD, T)
    tmpo = mem(scr + KD * T, T)
    rs = [mem(scr + (KD + 1 + g) * T, T) for g in range(NGR)]
    dtt = [mem(scr + 6144 + i * T, T, rows=NH) for i in range(6)]
    assert M <= Map.W, M
    CW, CB, GN = 0, 4 * NCV, 5 * NCV

    s_w = [sem(f"sd_w{i}") for i in range(2)]
    (s_dtw, s_vn, s_hn, s_hp, s_brw) = (sem("sd_" + n) for n in ("dtw", "vn", "hn", "hp", "brw"))
    s_sel, s_gp = sem("sd_sel"), sem("sd_gp")
    s_dtp, s_proj, s_raw, s_conv, s_silu = (sem("sd_" + n) for n in ("dtp", "proj", "raw", "conv", "silu"))
    s_setps, s_setrd, s_dts, s_dexp, s_dta = (sem("sd_" + n) for n in ("setps", "setrd", "dts", "dexp", "dta"))
    s_tmps, s_tmrd = sem("sd_tmps"), sem("sd_tmrd")
    s_csb, s_seg, s_ecs, s_cl, s_el = (sem("sd_" + n) for n in ("csb", "seg", "ecs", "cl", "el"))
    s_cb, s_cbm, s_xt, s_xdt, s_xdd, s_bt, s_btm = (sem("sd_" + n) for n in
                                                    ("cb", "cbm", "xt", "xdt", "xdd", "bt", "btm"))
    s_m, s_cs, s_yps, s_yev, s_sps, s_st = (sem("sd_" + n) for n in ("m", "cs", "yps", "yev", "sps", "st"))
    s_tlps, s_tl, s_bcps, s_bcs, s_hops, s_ho = (sem("sd_" + n) for n in ("tlps", "tl", "bcps", "bcs", "hops", "ho"))
    s_h0 = [sem(f"sd_h0{i}") for i in range(3)]
    s_h0w = [sem(f"sd_h0w{i}") for i in range(3)]
    s_bcl = [sem(f"sd_bcl{i}") for i in range(2)]
    s_dec, s_bcw, s_bbrd, s_hnew, s_yd = (sem("sd_" + n) for n in ("dec", "bcw", "bbrd", "hnew", "yd"))
    s_yg, s_sq, s_nps, s_var, s_rt, s_yb, s_br, s_brrd = (sem("sd_" + n) for n in
                                                         ("yg", "sq", "nps", "var", "rt", "yb", "br", "brrd"))
    s_out, s_dve = sem("sd_out"), sem("sd_dve")

    def chunk(c):
        return slice(c * P, (c + 1) * P)

    def by_group(x):
        return x.rearrange("p (g r) n -> p g r n", g=NGR)

    with nc.Block() as block:
        @block.sync
        def _(sp):
            w = A["w_in"][0].rearrange("(k p) n -> p k n", p=P)
            sp.dma_start(dtw, w[:, :, C_DT:C_DT + NH]).then_inc(s_dtw, 16)
            for j, name in enumerate(("dt_bias", "a_log", "d_skip")):
                sp.dma_start(hp[:, j:j + 1], A[name][0].rearrange("(h a) -> h a", a=1)).then_inc(s_hp, 16)
            sp.dma_start(vn[0:64, :], A["conv_w"][0].rearrange("j (t c) -> (j t) c", c=P)).then_inc(s_vn, 16)
            sp.dma_start(vn[64:80, :], A["conv_b"][0].rearrange("(t c) -> t c", c=P)).then_inc(s_vn, 16)
            sp.dma_start(vn[80:88, :], A["g_ssm_norm"][0].rearrange("(t c) -> t c", c=P)).then_inc(s_vn, 16)
            sp.dma_start(hn, A["state_conv"][0].rearrange("b j c -> (b j) c")).then_inc(s_hn, 16)
            sp.dma_start(ring[1], w[:, :, C_X + 512:C_X + 1024]).then_inc(s_w[1], 16)
            for i in range(2, 4):
                sp.wait_ge(s_proj, 4 * (i - 1))
                sp.dma_start(ring[i % 2], w[:, :, C_X + i * 512:C_X + (i + 1) * 512]).then_inc(s_w[i % 2], 16)
            sp.dma_start(O[9][0, :, 0:2, :], A["state_conv"][0, :, 1:3, :]).then_inc(s_out, 16)
            sp.wait_ge(s_proj, NCV)

            def load_state(b):
                sp.dma_start(h0[b % 3], A["state_ssm"][0, b].rearrange("(k q) p n -> (q p) k n", q=2))\
                    .then_inc(s_h0[b % 3], 16)

            def load_bc(b):
                sp.dma_start(bcb[b % 2].rearrange("p i g n -> p (i g n)"), bc_d[b:b + 1, :].partition_broadcast(P))\
                    .then_inc(s_bcl[b % 2], 16)

            for b in range(3):
                load_state(b)
            sp.wait_ge(s_bcs, 1)
            sp.dma_start(bc_d, bcs).then_inc(s_bcw, 16)
            sp.wait_ge(s_bcw, 16)
            for b in range(2):
                load_bc(b)
            for b in range(NS):
                sp.wait_ge(s_hnew, b + 1)
                sp.dma_start(O[8][0, b].rearrange("(k q) p n -> (q p) k n", q=2), h0[b % 3]).then_inc(s_h0w[b % 3], 16)
                if b + 2 < NS:
                    sp.wait_ge(s_bbrd, b + 1)
                    load_bc(b + 2)
                if b + 3 < NS:
                    sp.wait_ge(s_h0w[b % 3], 16 * (b // 3 + 1))
                    load_state(b + 3)
            sp.wait_ge(s_yd, NS)
            for i in range(3):
                sp.wait_ge(s_h0w[i], 16 * ((NS - 1 - i) // 3 + 1))
            sp.dma_start(brw, A["w_branch_b"][0].rearrange("(k p) n -> p k n", p=P)).then_inc(s_brw, 16)
            sp.wait_ge(s_ho, 8)
            sp.dma_start(O[4][0, 0].rearrange("(k q) p n -> (q p) k n", q=2), hout).then_inc(s_out, 16)
            sp.wait_ge(s_tl, 1)
            sp.dma_start(O[5][0, 0], tl[0:3, :]).then_inc(s_out, 16)
            sp.dma_start(O[9][0, :, 2, :], tl[3:11, :]).then_inc(s_out, 16)
            sp.wait_ge(s_out, 64)

        @block.gpsimd
        def _(pool):
            G = nc.gpsimd
            link = Link(pool, s_gp)
            for r in raw:
                link(G.memset(r, 0.0))
            link(G.memset(sel, 0.0))
            link(G.affine_select(out=sel, in_=sel, compare_op=ALU.not_equal, fill=1.0, base=0,
                                 pattern=[[-1, NH], [0, P]], channel_multiplier=1))
            link(G.memset(ek, 1.0))
            link(G.affine_select(out=ek, in_=ek, compare_op=ALU.is_ge, fill=0.0, base=0,
                                 pattern=[[P, KD], [1, P]], channel_multiplier=-HD))
            link(G.affine_select(out=ek, in_=ek, compare_op=ALU.is_ge, fill=0.0, base=HD - 1,
                                 pattern=[[-P, KD], [-1, P]], channel_multiplier=HD))
            link(G.memset(mask, 1.0))
            G.affine_select(out=mask, in_=mask, compare_op=ALU.is_ge, fill=0.0, base=0,
                            pattern=[[1, P]], channel_multiplier=-1).then_inc(s_sel, 1)
            def decay(b):
                pool.wait_ge(s_h0[b % 3], 16 * (b // 3 + 1))
                G.tensor_tensor(h0[b % 3], h0[b % 3], ex[:, :, 8 + b:9 + b].to_broadcast([P, KD, SN]),
                                ALU.mult).then_inc(s_dec, 1)

            pool.wait_ge(s_tmrd, 2)
            decay(0)
            decay(1)
            pool.wait_ge(s_silu, NCV)
            for c in range(1, NB):
                decay(2 * c)
                decay(2 * c + 1)
                pool.wait_ge(s_ecs, 2 * (c + 1))
                if c > 1:
                    pool.wait_ge(s_yps, c)
                G.tensor_tensor(by_group(cs_c), cv[:, 12:16, chunk(c)].unsqueeze(2).to_broadcast([P, NGR, HPG, P]),
                                by_group(ecs), ALU.mult).then_inc(s_cs, 1)

        @block.scalar
        def _(act):
            S = nc.scalar
            act.wait_ge(s_gp, 2)
            act.wait_ge(s_hp, 48)
            S.activation(hp[:, 4:5], hp[:, 1:2], ACT.Exp).then_inc(s_dexp, 1)
            act.wait_ge(s_dts, 1)
            S.activation(dtt[1], dtt[1], ACT.Exp).then_inc(s_dexp, 1)

            def silu(n):
                act.wait_ge(s_conv, n + 1)
                S.activation(cv[:, n, :], cv[:, n, :], ACT.Silu).then_inc(s_silu, 1)

            for n in range(NCV):
                act.wait_ge(s_proj, n + 1)
                if n >= 2:
                    act.wait_ge(s_conv, n - 1)
                S.activation(cols(raw[n % 2][:, 3:3 + T]), two(ps[:, 2 * (n % 2):2 * (n % 2) + 2, :]),
                             ACT.Copy).then_inc(s_raw, 1)
                act.wait_ge(s_raw, 2 * n + 1)
                S.activation(tail[:, n, :], raw[n % 2][:, L:L + 11], ACT.Copy).then_inc(s_raw, 1)
                if n >= 1:
                    silu(n - 1)
            silu(NCV - 1)
            act.wait_ge(s_dta, 1)
            S.activation(rex[:, 8:16], rex[:, 8:16], ACT.Exp).then_inc(s_dexp, 1)
            act.wait_ge(s_bcps, 1)
            S.activation(bcs, ps[0:NS, 6:8, :].rearrange("p a n -> p (a n)"), ACT.Copy).then_inc(s_bcs, 1)
            for c in range(NB):
                for half in range(2):
                    act.wait_ge(s_csb, 2 * c + half + 1)
                    if c >= 2:
                        act.wait_ge(s_cs, c - 1)
                    if c >= 1:
                        act.wait_ge(s_st, c)
                    S.activation(ecs[:, 8 * half:8 * half + 8, :], ps[:, 0:2, :].rearrange("p a (h i) -> p (a h) i", i=P),
                                 ACT.Exp).then_inc(s_ecs, 1)
                act.wait_ge(s_cl, c + 1)
                S.activation(lm, lm, ACT.Exp).then_inc(s_el, 1)
                act.wait_ge(s_bt, c + 1)
                if c:
                    act.wait_ge(s_sps, c)
                S.activation(btm, ps[:, 5, :].rearrange("p (g n) -> p g n", g=NGR), ACT.Copy).then_inc(s_btm, 1)
            act.wait_ge(s_hops, 1)
            for k in range(KD):
                S.activation(hout[:, k, :], ps[:, 2 + k // 4, (k % 4) * P:(k % 4 + 1) * P], ACT.Copy).then_inc(s_ho, 1)
            for k in range(KD):
                act.wait_ge(s_yg, k + 1)
                S.activation(sq[:, k, :], cv[:, k, :], ACT.Square).then_inc(s_sq, 1)
            for g in range(NGR):
                act.wait_ge(s_var, g + 1)
                S.activation(rs[g], rs[g], ACT.Sqrt).then_inc(s_rt, 1)
            act.wait_ge(s_tlps, 1)
            S.activation(tl, ps[0:11, 0:4, :].rearrange("p a n -> p (a n)"), ACT.Copy).then_inc(s_tl, 1)

        @block.tensor
        def _(pe):
            mm = nc.tensor.matmul
            pe.wait_ge(s_dtw, 16)
            for k in range(KD):
                for h in range(2):
                    last = mm(ps[0:NH, 6 + h, 0:HALF], dtw[:, k, :], hT[:, k, h * HALF:(h + 1) * HALF],
                              start=(k == 0), stop=(k == KD - 1))
            last.then_inc(s_dtp, 1)
            pe.wait_ge(s_vn, 48)
            pe.wait_ge(s_hn, 16)
            nc.tensor.transpose(ps[:, 4, 0:88], vn, ident[0:88, 0:88])
            for n in range(NCV):
                last = nc.tensor.transpose(ps[:, 5, n * 24:(n + 1) * 24], hn[:, n * P:(n + 1) * P],
                                           ident[0:24, 0:24])
            last.then_inc(s_setps, 1)
            for n in range(NCV):
                i, m = n // 4, n % 4
                if n == 0:
                    pe.wait_ge(s_ssd, 16)
                elif m == 0:
                    pe.wait_ge(s_w[i % 2], 16 * ((i + 1) // 2))
                if n >= 2:
                    pe.wait_ge(s_raw, 2 * (n - 2) + 1)
                for k in range(KD):
                    for h in range(2):
                        last = mm(ps[:, 2 * (n % 2) + h, 0:HALF], ring[i % 2][:, k, m * P:(m + 1) * P],
                                  hT[:, k, h * HALF:(h + 1) * HALF], start=(k == 0), stop=(k == KD - 1))
                last.then_inc(s_proj, 1)
            pe.wait_ge(s_dta, 2)
            for c in range(NB):
                nc.tensor.transpose(ps[:, 4, c * 32:c * 32 + 16], csv[:, chunk(c)], ident[0:NH, 0:NH])
                nc.tensor.transpose(ps[:, 4, c * 32 + 16:c * 32 + 32], dtv[:, chunk(c)], ident[0:NH, 0:NH])
            pe.wait_ge(s_dexp, 3)
            pe.wait_ge(s_sel, 1)
            for k in range(KD):
                last = mm(ps[:, 4, 128 + 17 * k:145 + 17 * k], ek[:, k, :], rex, start=True, stop=True)
            last.then_inc(s_tmps, 1)
            pe.wait_ge(s_silu, NCV)
            pe.wait_ge(s_raw, 2 * NCV)
            for j in range(8):
                last = nc.tensor.transpose(ps[0:NS, 6 + j // 4, (j % 4) * P:(j % 4 + 1) * P], cv[:, 8 + j, L:T], ident)
            last.then_inc(s_bcps, 1)
            for c in range(NB):
                for half in range(2):
                    n = 2 * c + half
                    if n:
                        pe.wait_ge(s_ecs, n)
                        pe.wait_ge(s_seg, n)
                    for h in range(8):
                        last = mm(ps[:, h // 4, (h % 4) * P:(h % 4 + 1) * P], sel[:, 8 * half + h, :],
                                  csv[:, chunk(c)], start=True, stop=True)
                    last.then_inc(s_csb, 1)
                    if half == 0:
                        pe.wait_ge(s_tmrd, 2)
                        if c:
                            pe.wait_ge(s_cbm, c)
                        for g in range(NGR):
                            last = mm(ps[:, 4, g * P:(g + 1) * P], cv[:, 8 + g, chunk(c)], cv[:, 12 + g, chunk(c)],
                                      start=True, stop=True)
                        last.then_inc(s_cb, 1)
                        if c:
                            pe.wait_ge(s_st, c)
                        for k in range(KD):
                            last = nc.tensor.transpose(ps[:, 2 + k // 4, (k % 4) * P:(k % 4 + 1) * P],
                                                       cv[:, k, chunk(c)], ident)
                        last.then_inc(s_xt, 1)
                        if c:
                            pe.wait_ge(s_btm, c)
                        for g in range(NGR):
                            last = nc.tensor.transpose(ps[:, 5, g * P:(g + 1) * P], cv[:, 8 + g, chunk(c)], ident)
                        last.then_inc(s_bt, 1)
                pe.wait_ge(s_btm, c + 1)
                pe.wait_ge(s_xdd, c + 1)
                for g in range(NGR):
                    last = mm(ps[:, 2 + g // 2, (g % 2) * 256:(g % 2) * 256 + 256], btm[:, g, :],
                              xdd[:, 4 * g:4 * g + 4, :].rearrange("p h d -> p (h d)"), start=True, stop=True)
                last.then_inc(s_sps, 1)
                pe.wait_ge(s_m, c + 1)
                if c:
                    pe.wait_ge(s_cs, c)
                    pe.wait_ge(s_yev, c)
                else:
                    pe.wait_ge(s_bcs, 1)
                for h in range(NH):
                    rows = slice(HD * (h % 2), HD * (h % 2) + HD)
                    k = h // 2
                    out = ps[rows, 6 + k // 4, (k % 4) * P:(k % 4 + 1) * P]
                    last = mm(out, xdt[:, h, :], lm[:, h, :], start=True, stop=(c == 0))
                    if c:
                        last = mm(out, st[:, h, :], cs_c[:, h, :], start=False, stop=True)
                last.then_inc(s_yps, 1)
            pe.wait_ge(s_st, NB)
            for k in range(KD):
                last = nc.tensor.transpose(ps[:, 2 + k // 4, (k % 4) * P:(k % 4 + 1) * P],
                                           st[:, 2 * k:2 * k + 2, :].rearrange("p h d -> p (h d)"), ident)
            last.then_inc(s_hops, 1)
            pe.wait_ge(s_ho, 8)
            for g in range(NGR):
                pe.wait_ge(s_sq, 2 * g + 2)
                if g >= 2:
                    pe.wait_ge(s_var, g - 1)
                for j in range(2):
                    for h in range(2):
                        last = mm(ps[:, 2 * (g % 2) + h, 0:HALF], ones, sq[:, 2 * g + j, h * HALF:(h + 1) * HALF],
                                  start=(j == 0), stop=(j == 1))
                last.then_inc(s_nps, 1)
            pe.wait_ge(s_var, NGR)
            for n in range(NCV):
                last = nc.tensor.transpose(ps[0:11, n // 4, (n % 4) * P:(n % 4 + 1) * P], tail[:, n, :], ident)
            last.then_inc(s_tlps, 1)
            pe.wait_ge(s_yb, KD)
            pe.wait_ge(s_brw, 16)
            for m in range(KD):
                if m >= 2:
                    pe.wait_ge(s_brrd, m - 1)
                for k in range(KD):
                    for h in range(2):
                        last = mm(ps[:, 4 + 2 * (m % 2) + h, 0:HALF], brw[:, k, m * P:(m + 1) * P],
                                  cv[:, k, h * HALF:(h + 1) * HALF], start=(k == 0), stop=(k == KD - 1))
                last.then_inc(s_br, 1)

        @block.vector
        def _(dve):
            V = nc.vector
            link = Link(dve, s_dve)
            x, e, a, w, q, r = dtt
            stt, tt, ts = V.scalar_tensor_tensor, V.tensor_tensor, V.tensor_scalar
            dve.wait_ge(s_hp, 48)
            dve.wait_ge(s_dtp, 1)
            link(ts(cols(x), two(ps[0:NH, 6:8, :]), hp[:, 0:1], None, ALU.add))
            link(ts(a, x, -1.0, None, ALU.mult))
            link(tt(a, a, x, ALU.max))
            ts(e, a, -1.0, None, ALU.mult).then_inc(s_dts, 1)
            dve.wait_ge(s_setps, 1)
            V.tensor_copy(vT, ps[:, 4, 0:88]).then_inc(s_setrd, 1)
            V.tensor_copy(hist, ps[:, 5, 0:NCV * 24].rearrange("p (n j) -> p n j", n=NCV)).then_inc(s_setrd, 1)
            dve.wait_ge(s_dexp, 2)
            link(ts(a, e, 2.0, None, ALU.add))
            link(V.reciprocal(a, a))
            link(tt(a, a, e, ALU.mult))
            link(tt(w, a, a, ALU.mult))
            link(ts(q, w, 1.0 / 17, None, ALU.mult))
            for n in range(7, 0, -1):
                link(stt(out=q, in0=q, scalar=1.0 / (2 * n + 1), in1=w, op0=ALU.add, op1=ALU.mult))
            link(stt(out=q, in0=q, scalar=1.0, in1=a, op0=ALU.add, op1=ALU.mult))
            link(ts(x, x, 0.0, None, ALU.max))
            link(stt(out=dtv, in0=q, scalar=2.0, in1=x, op0=ALU.mult, op1=ALU.add))
            link(ts(hp[:, 5:6], hp[:, 4:5], -1.0, None, ALU.mult))
            link(ts(r, dtv, hp[:, 5:6], None, ALU.mult))
            link(V.tensor_copy(rex[:, 0:8], dtv[:, L:T]))
            link(V.tensor_copy(rex[:, 16:17], hp[:, 2:3]))
            V.tensor_copy(rex[:, 8:16], r[:, L:T]).then_inc(s_dta, 1)
            link(V.memset(e, 1.0))
            for c in range(NB):
                last = V.tensor_tensor_scan(csv[:, chunk(c)], e[:, 0:P], r[:, chunk(c)], 0.0, ALU.mult, ALU.add)
                if c < NB - 1:
                    link(last)
            last.then_inc(s_dta, 1)

            dve.wait_ge(s_setrd, 2)
            for n in range(NCV):
                dve.wait_ge(s_raw, 2 * n + 1)
                wj = [vT[:, CW + j * NCV + n:CW + j * NCV + n + 1] for j in range(4)]
                bj = vT[:, CB + n:CB + n + 1]
                out, smp, rw = cv[:, n, 0:L], cv[:, n, L:T], raw[n % 2]
                hj = hist[:, n, :].rearrange("p (b j) -> p j b", j=3)
                link(ts(out, rw[:, 0:L], wj[0], bj, ALU.mult, ALU.add))
                link(ts(smp, hj[:, 0, :], wj[0], bj, ALU.mult, ALU.add))
                for j in (1, 2):
                    link(stt(out=out, in0=rw[:, j:j + L], scalar=wj[j], in1=out, op0=ALU.mult, op1=ALU.add))
                    link(stt(out=smp, in0=hj[:, j, :], scalar=wj[j], in1=smp, op0=ALU.mult, op1=ALU.add))
                link(stt(out=out, in0=rw[:, 3:3 + L], scalar=wj[3], in1=out, op0=ALU.mult, op1=ALU.add))
                stt(out=smp, in0=rw[:, 3 + L:3 + T], scalar=wj[3], in1=smp, op0=ALU.mult,
                    op1=ALU.add).then_inc(s_conv, 1)

            dve.wait_ge(s_tmps, 1)
            V.tensor_copy(tm, ps[:, 4, 0:P].rearrange("p (c i h) -> p c i h", c=NB, i=2)).then_inc(s_tmrd, 1)
            V.tensor_copy(ex, ps[:, 4, 128:128 + KD * 17].rearrange("p (k j) -> p k j", j=17)).then_inc(s_tmrd, 1)
            dve.wait_ge(s_tmrd, 2)
            dve.wait_ge(s_silu, NCV)
            link(tt(xs_s, cv[:, 0:KD, L:T], ex[:, :, 0:8], ALU.mult))

            def sample(b):
                B, C = (bcb[b % 2][:, i, :, :].unsqueeze(2).to_broadcast([P, NGR, 2, SN]) for i in range(2))
                g4 = lambda v: v.rearrange("p (g r) n -> p g r n", g=NGR)
                dve.wait_ge(s_bcl[b % 2], 16 * (b // 2 + 1))
                link(tt(g4(tb), B, g4(xs_s[:, :, b:b + 1].to_broadcast([P, KD, SN])), ALU.mult))
                dve.wait_ge(s_dec, b + 1)
                tt(h0[b % 3], h0[b % 3], tb, ALU.add).then_inc(s_hnew, 1)
                dve.wait_ge(s_hnew, b + 1)
                tt(g4(tb), g4(h0[b % 3]), C, ALU.mult).then_inc(s_bbrd, 1)
                dve.wait_ge(s_bbrd, b + 1)
                V.tensor_reduce(ys_s[:, :, b:b + 1], tb, AX_X, ALU.add).then_inc(s_yd, 1)
                dve.wait_ge(s_yd, b + 1)

            for c in range(NB):
                csb = ps[:, 0:2, :].rearrange("p a (h i) -> p (a h) i", i=P)
                for half in range(2):
                    hs = slice(8 * half, 8 * half + 8)
                    dve.wait_ge(s_ecs, 2 * c + half + 1)
                    if c:
                        dve.wait_ge(s_yps, c)
                    tt(lm[:, hs, :], csb, tm[:, c, 0, hs].unsqueeze(2).to_broadcast([P, 8, P]),
                       ALU.subtract).then_inc(s_seg, 1)
                    if half == 0:
                        dve.wait_ge(s_cb, c + 1)
                        tt(cbm, ps[:, 4, :].rearrange("p (g i) -> p g i", g=NGR),
                           mask.unsqueeze(1).to_broadcast([P, NGR, P]), ALU.mult).then_inc(s_cbm, 1)
                        dve.wait_ge(s_xt, c + 1)
                        tt(xdt, ps[:, 2:4, :].rearrange("p a (h d) -> p (a h) d", d=HD),
                           tm[:, c, 1, :].unsqueeze(2).to_broadcast([P, NH, HD]), ALU.mult).then_inc(s_xdt, 1)
                dve.wait_ge(s_seg, 2 * c + 2)
                ts(lm, lm, 0.0, None, ALU.min).then_inc(s_cl, 1)
                sample(2 * c)
                dve.wait_ge(s_el, c + 1)
                dve.wait_ge(s_xdt, c + 1)
                if c:
                    dve.wait_ge(s_sps, c)
                tt(xdd, xdt, lm[:, :, P - 1:P].to_broadcast([P, NH, HD]), ALU.mult).then_inc(s_xdd, 1)
                dve.wait_ge(s_xdd, c + 1)
                dve.wait_ge(s_cbm, c + 1)
                tt(by_group(lm), by_group(lm), cbm.unsqueeze(2).to_broadcast([P, NGR, HPG, P]),
                   ALU.mult).then_inc(s_m, 1)
                sample(2 * c + 1)
                dve.wait_ge(s_yps, c + 1)
                for k in range(KD):
                    last = stt(out=cv[:, k, chunk(c)], in0=cv[:, k, chunk(c)], scalar=ex[:, k, 16:17],
                               in1=ps[:, 6 + k // 4, (k % 4) * P:(k % 4 + 1) * P], op0=ALU.mult, op1=ALU.add)
                last.then_inc(s_yev, 1)
                dve.wait_ge(s_sps, c + 1)
                sps = ps[:, 2:4, :].rearrange("p a (h d) -> p (a h) d", d=HD)
                if c == 0:
                    V.tensor_copy(st, sps).then_inc(s_st, 1)
                else:
                    dve.wait_ge(s_ecs, 2 * c + 2)
                    link(tt(st, st, ecs[:, :, P - 1:P].to_broadcast([P, NH, HD]), ALU.mult))
                    tt(st, st, sps, ALU.add).then_inc(s_st, 1)
                dve.wait_ge(s_st, c + 1)
            link(tt(xs_s, cv[:, 0:KD, L:T], ex[:, :, 16:17].to_broadcast([P, KD, NS]), ALU.mult))
            link(tt(cv[:, 0:KD, L:T], xs_s, ys_s, ALU.add))
            dve.wait_ge(s_yev, NB)
            for k in range(KD):
                tt(cv[:, k, :], cv[:, k, :], zs[:, k, :], ALU.mult).then_inc(s_yg, 1)
            dve.wait_ge(s_yg, KD)
            def scaled(g):
                dve.wait_ge(s_rt, g + 1)
                for k in (2 * g, 2 * g + 1):
                    stt(out=cv[:, k, :], in0=cv[:, k, :], scalar=vT[:, GN + k:GN + k + 1], in1=rs[g], op0=ALU.mult,
                        op1=ALU.mult).then_inc(s_yb, 1)

            dve.wait_ge(s_sq, KD)
            for g in range(NGR):
                dve.wait_ge(s_nps, g + 1)
                link(ts(cols(rs[g]), two(ps[:, 2 * (g % 2):2 * (g % 2) + 2, :]), 1.0 / 256, G_EPS, ALU.mult, ALU.add))
                V.reciprocal(rs[g], rs[g]).then_inc(s_var, 1)
                if g:
                    scaled(g - 1)
            scaled(NGR - 1)
            for m in range(KD):
                dve.wait_ge(s_br, m + 1)
                tt(cols(tmpo), two(ps[:, 4 + 2 * (m % 2):6 + 2 * (m % 2), :]), cols(gB[:, m, :]),
                   ALU.mult).then_inc(s_brrd, 1)
                dve.wait_ge(s_brrd, m + 1)
                link(tt(mg[:, m, :], mg[:, m, :], tmpo, ALU.add))


class Query:

    def __init__(self, mem):
        M = Map.QUERY
        self.h2T = mem(M, KD, T); M += KD * T
        self.ring = [mem(M + i * KD * 256, KD, 256) for i in range(2)]; M += 2 * KD * 256
        self.kT = mem(M, 2 * PH, NK); M += 2 * PH * NK
        self.qT = [mem(M + i * T, T) for i in range(2)]; M += 2 * T
        self.qpad = mem(M, 2 * PH, 64); M += 2 * PH * 64
        assert M == Map.PEER
        self.sc = mem(Map.SC, NB, 2 * PH, NK)

    def load(self, eng, A, i):
        w = A["w_query"][0].rearrange("(k p) n -> p k n", p=P)
        return eng.dma_start(self.ring[i % 2], w[:, :, i * 256:(i + 1) * 256])

    def project(self, nc, ps, t):
        for k in range(KD):
            for h in range(2):
                last = nc.tensor.matmul(ps[:, 2 + h, 0:HALF], self.ring[(t // 2) % 2][:, k, (t % 2) * P:(t % 2 + 1) * P],
                                        self.h2T[:, k, h * HALF:(h + 1) * HALF], start=(k == 0), stop=(k == KD - 1))
        return last

    def keep(self, nc, ps, t):
        return nc.scalar.activation(cols(self.qT[t % 2]), two(ps[:, 2:4, :]), ACT.Copy)

    def keep_samples(self, nc, t):
        h = t // 2
        return nc.scalar.activation(self.qpad[:, t, NS * h:NS * h + NS], self.qT[t % 2][:, L:T], ACT.Copy)

    def score(self, nc, ps, t):
        for b in range(NB):
            nc.tensor.matmul(ps[:, 4 + t % 2, b * P:(b + 1) * P], self.qT[t % 2][:, b * P:(b + 1) * P], self.kT[:, t, :],
                             start=True, stop=True)
        return nc.tensor.matmul(ps[0:64, 6 + t % 2, 0:NK], self.qpad[:, t, :], self.kT[:, t, :], start=(t < 2),
                                stop=(t >= 2 * PH - 2))

    def store(self, nc, ps, t):
        return nc.vector.tensor_copy(self.sc[:, :, t, :], ps[:, 4 + t % 2, :].rearrange("p (b k) -> p b k", b=NB))


def stage_query(nc, mem, sem, ps, A, mod_d):
    mg = mem(Map.MG, KD, T)
    ident = mem(Map.IDENT, P)
    Q = Query(mem)
    h2T, kT = Q.h2T, Q.kT
    wo = mem(Map.HT + KD * T, KD, D)
    x1, h2 = mem(Map.X1, 5, D), mem(Map.H2, 5, D)
    scs = mem(Map.SCS, 2, NK)
    gate, scale, shift = (mem(Map.SC + i * 2 * D, 2, D) for i in range(3))
    g2, junk = mem(Map.SC + 6 * D, D), mem(Map.SC + 7 * D, D)
    M = Map.PEER
    kn = mem(M, 2 * PH, P); M += 2 * PH * P
    stat, rstd = mem(M, 8), mem(M + 8, 8); M += 16
    assert M <= Map.W, M

    s_wo = [sem(f"qy_wo{i}") for i in range(4)]
    s_x, s_rows, s_k = (sem("qy_" + n) for n in ("x", "rows", "k"))
    s_w = [sem(f"qy_w{i}") for i in range(2)]
    s_o, s_ord, s_x1, s_sq, s_var, s_rt, s_h2 = (sem("qy_" + n) for n in ("o", "ord", "x1", "sq", "var", "rt", "h2"))
    s_tp, s_hT, s_kp, s_kT, s_q, s_qT = (sem("qy_" + n) for n in ("tp", "hT", "kp", "kT", "q", "qT"))
    s_s, s_srd, s_zero, s_dve = (sem("qy_" + n) for n in ("s", "srd", "zero", "dve"))
    hparts = [(b, half) for b in range(5) for half in range(2)]

    def rows_of(b):
        return P if b < NB else NS

    with nc.Block() as block:
        @block.sync
        def _(sp):
            for i in range(4):
                sp.dma_start(wo[:, 2 * i:2 * i + 2, :], A["w_out"][0].rearrange("(k p) n -> p k n", p=P)
                             [:, 2 * i:2 * i + 2, :]).then_inc(s_wo[i], 16)
            sp.dma_start(x1[:, 0:NB, :], A["x_prompt"][0].rearrange("(b p) d -> p b d", p=P)).then_inc(s_x, 16)
            sp.dma_start(x1[0:NS, NB, :], A["x_sample"].rearrange("b s d -> (b s) d")).then_inc(s_x, 16)
            for dst, m in ((gate, 2), (shift, 3), (scale, 4)):
                sp.dma_start(dst[:, 0, :], mod_d[NS:NC_ROWS, m * D:(m + 1) * D].partition_broadcast(P)).then_inc(s_rows, 16)
                sp.dma_start(dst[0:NS, 1, :], mod_d[0:NS, m * D:(m + 1) * D]).then_inc(s_rows, 16)
            sp.dma_start(g2, A["g_norm2"][0:1, :].partition_broadcast(P)).then_inc(s_rows, 16)
            sp.dma_start(kn, A["sub_keys"][0].rearrange("h s k d -> k (h s) d")).then_inc(s_k, 16)
            for i in range(2):
                Q.load(sp, A, i).then_inc(s_w[i], 16)

        @block.gpsimd
        def _(pool):
            nc.gpsimd.memset(Q.qpad, 0.0).then_inc(s_zero, 1)
            nc.gpsimd.memset(scs, 0.0).then_inc(s_zero, 1)

        @block.scalar
        def _(act):
            S = nc.scalar
            for b in range(5):
                n = rows_of(b)
                act.wait_ge(s_x1, b + 1)
                if b:
                    act.wait_ge(s_sq, b)
                S.activation(junk[0:n, :], x1[0:n, b, :], ACT.Square, accum_out=stat[0:n, b:b + 1]).then_inc(s_sq, 1)
                act.wait_ge(s_var, b + 1)
                S.activation(rstd[0:n, b:b + 1], stat[0:n, b:b + 1], ACT.Sqrt).then_inc(s_rt, 1)
            for n, (b, half) in enumerate(hparts):
                act.wait_ge(s_tp, n + 1)
                m = rows_of(b)
                S.activation(h2T[:, 4 * half:4 * half + 4, b * P:b * P + m],
                             ps[:, 4 + n % 4, :].rearrange("p (k t) -> p k t", k=4)[:, :, 0:m], ACT.Copy).then_inc(s_hT, 1)
            for i in range(4):
                act.wait_ge(s_kp, i + 1)
                S.activation(kT[:, 4 * i:4 * i + 4, :], ps[:, 4 + i, :].rearrange("p (k t) -> p k t", k=4),
                             ACT.Copy).then_inc(s_kT, 1)
            act.wait_ge(s_zero, 2)
            for t in range(2):
                act.wait_ge(s_q, t + 1)
                Q.keep(nc, ps, t).then_inc(s_qT, 1)
                act.wait_ge(s_qT, 2 * t + 1)
                Q.keep_samples(nc, t).then_inc(s_qT, 1)

        @block.tensor
        def _(pe):
            mm = nc.tensor.matmul
            for b in range(5):
                n = rows_of(b)
                if b >= 2:
                    pe.wait_ge(s_ord, b - 1)
                for k in range(KD):
                    if b == 0 and k % 2 == 0:
                        pe.wait_ge(s_wo[k // 2], 16)
                    for j in range(2):
                        last = mm(ps[0:n, 2 * (b % 2) + j, :], mg[:, k, b * P:b * P + n], wo[:, k, j * 512:(j + 1) * 512],
                                  start=(k == 0), stop=(k == KD - 1))
                last.then_inc(s_o, 1)
            for n, (b, half) in enumerate(hparts):
                pe.wait_ge(s_h2, b + 1)
                if n >= 4:
                    pe.wait_ge(s_hT, n - 3)
                m = rows_of(b)
                for k in range(4):
                    kk = 4 * half + k
                    last = nc.tensor.transpose(ps[:, 4 + n % 4, k * P:k * P + m],
                                               h2[0:m, b, kk * P:(kk + 1) * P], ident[0:m, 0:m])
                last.then_inc(s_tp, 1)
            pe.wait_ge(s_hT, 10)
            pe.wait_ge(s_k, 16)
            for i in range(4):
                for j in range(4):
                    last = nc.tensor.transpose(ps[:, 4 + i, j * P:(j + 1) * P], kn[:, 4 * i + j, :], ident)
                last.then_inc(s_kp, 1)

            pe.wait_ge(s_ord, 5)
            pe.wait_ge(s_w[0], 16)
            for t in range(2):
                if t:
                    pe.wait_ge(s_qT, 1)
                Q.project(nc, ps, t).then_inc(s_q, 1)
            pe.wait_ge(s_kT, 4)
            for t in range(2):
                pe.wait_ge(s_qT, 2 * t + 2)
                Q.score(nc, ps, t).then_inc(s_s, 1)
            pe.wait_ge(s_w[1], 16)

        @block.vector
        def _(dve):
            V = nc.vector
            link = Link(dve, s_dve)
            dve.wait_ge(s_rows, 16 * 7)
            for r, n in ((0, P), (1, NS)):
                link(V.scalar_tensor_tensor(out=scale[0:n, r, :], in0=scale[0:n, r, :], scalar=1.0, in1=g2[0:n, :],
                                            op0=ALU.add, op1=ALU.mult))
            dve.wait_ge(s_x, 32)
            for b in range(5):
                n, r = rows_of(b), b // NB
                dve.wait_ge(s_o, b + 1)
                V.tensor_tensor(h2[0:n, b, :], ps[0:n, 2 * (b % 2):2 * (b % 2) + 2, :].rearrange("p a n -> p (a n)"),
                                gate[0:n, r, :], ALU.mult).then_inc(s_ord, 1)
                dve.wait_ge(s_ord, b + 1)
                V.tensor_tensor(x1[0:n, b, :], x1[0:n, b, :], h2[0:n, b, :], ALU.add).then_inc(s_x1, 1)
                dve.wait_ge(s_sq, b + 1)
                st = stat[0:n, b:b + 1]
                link(V.tensor_scalar(st, st, 1.0 / D, EPS, ALU.mult, ALU.add))
                V.reciprocal(st, st).then_inc(s_var, 1)
                dve.wait_ge(s_rt, b + 1)
                link(V.scalar_tensor_tensor(out=h2[0:n, b, :], in0=x1[0:n, b, :], scalar=rstd[0:n, b:b + 1],
                                            in1=scale[0:n, r, :], op0=ALU.mult, op1=ALU.mult))
                V.tensor_tensor(h2[0:n, b, :], h2[0:n, b, :], shift[0:n, r, :], ALU.add).then_inc(s_h2, 1)
            dve.wait_ge(s_h2, 5)
            for t in range(2):
                dve.wait_ge(s_s, t + 1)
                Q.store(nc, ps, t).then_inc(s_srd, 1)


GATE = 8
HG = GATE // 2
NGRP = 2 * TOPK // (2 * GATE)


def stage_peer(nc, mem, sem, ps, A, O, mod_d, integers):
    ident = mem(Map.IDENT, P)
    x1, h2 = mem(Map.X1, 5 * D), mem(Map.H2, 5 * D)
    scores = mem(Map.SC, (NB * PH + 1) * 2 * NK)
    U = [mem(256 + j * D, D) for j in range(GATE)]
    Vr = [mem(256 + (GATE + j) * D, D) for j in range(GATE)]
    Q = Query(mem)
    M = Map.QUERY

    def take(*shape, rows=P):
        nonlocal M
        M += int(np.prod(shape))
        return mem(M - int(np.prod(shape)), *shape, rows=rows)

    gate, scale, shift = take(2, D), take(2, D), take(2, D)
    gf = take(D)
    xb = take(D)
    yb = take(D)
    x64 = take(D)
    assert M <= Map.PEER
    M = Map.PEER
    diag = take(GATE, P)
    zero = take(P)
    hb = take(D)
    sel64 = take(PH, NS, rows=NS)
    r64 = take(NS)
    s_in, s_rep = take(2, NK), take(2, NK)
    val, idxf = take(2, TOPK), take(2, TOPK)
    cand, crep = take(TOPK, TOPK), take(TOPK, TOPK)
    fij = take(2, TOPK)
    oh = take(2 * TOPK, TOPK)
    r01 = take(2, TOPK)
    ef = take(TOPK)
    iota = take(TOPK)
    fv = take(TOPK)
    w = [take(TOPK) for _ in range(2)]
    ssum = take(8)
    dots = [take(GATE) for _ in range(2)]
    gel = [take(GATE) for _ in range(2)]
    actv = [take(GATE) for _ in range(2)]
    stat, rstd = take(1), take(1)
    assert M <= Map.W, M
    idx = [integers["expert0"], integers["expert1"]]
    kix, fix, fiju, iotai = (integers[n] for n in ("keys", "pairs", "halves", "counting"))

    s_rows, s_const, s_pc = sem("pr_rows"), sem("pr_const"), sem("pr_pc")
    s_U = [sem(f"pr_U{j}") for j in range(GATE)]
    s_V = [sem(f"pr_V{j}") for j in range(GATE)]
    s_top, s_uused, s_vused = sem("pr_top"), sem("pr_uused"), sem("pr_vused")
    s_nmax, s_exp, s_gelu, s_actv, s_diag = (sem("pr_" + n) for n in ("nmax", "exp", "gelu", "actv", "diag"))
    s_blk, s_blkrd, s_x2, s_sq, s_var, s_rt, s_y, s_out = (sem("pr_" + n) for n in
                                                           ("blk", "blkrd", "x2", "sq", "var", "rt", "y", "out"))
    s_ps64, s_x64, s_gatep = sem("pr_ps64"), sem("pr_x64"), sem("pr_gatep")
    s_w = [sem(f"pr_w{i}") for i in range(2)]
    s_q, s_qT, s_s, s_srd = (sem("pr_" + n) for n in ("q", "qT", "s", "srd"))
    NQ = 2 * PH - 2
    down, up = A["expert_down"][0], A["expert_up"][0]
    NU = NB * PH

    with nc.Block() as block:
        @block.sync
        def _(sp):
            for i in range(2, PH):
                if i > 2:
                    sp.wait_ge(s_q, 2 * (i - 2))
                Q.load(sp, A, i).then_inc(s_w[i % 2], 16)
            sp.wait_ge(s_s, NQ)
            for dst, m in ((gate, 5), (shift, 6), (scale, 7)):
                sp.dma_start(dst[:, 0, :], mod_d[NS:NC_ROWS, m * D:(m + 1) * D].partition_broadcast(P)).then_inc(s_rows, 16)
                sp.dma_start(dst[0:NS, 1, :], mod_d[0:NS, m * D:(m + 1) * D]).then_inc(s_rows, 16)
            sp.dma_start(gf, A["g_final"].rearrange("(a n) -> a n", a=1).partition_broadcast(P)).then_inc(s_rows, 16)
            sp.sem_inc(s_out, 16)
            with sp.Fori(0, NB) as b:
                sp.wait_ge(s_y, b + 1)
                sp.dma_start(O[0][0].rearrange("(b p) d -> b p d", p=P)[bass.ds(b, 1), :, :].rearrange("a p d -> (a p) d"),
                             yb).then_inc(s_out, 16)
            sp.wait_ge(s_y, NB + 1)
            sp.dma_start(O[1].rearrange("b s d -> (b s) d"), yb[0:NS, :]).then_inc(s_out, 16)
            sp.wait_ge(s_out, 16 * (NB + 2))

        @block.gpsimd
        def _(pool):
            G = nc.gpsimd
            link = Link(pool, s_pc)
            pool.sem_inc(s_uused, 1)
            link(G.memset(zero, 0.0))
            link(G.memset(sel64, 0.0))
            link(G.affine_select(out=sel64, in_=sel64, compare_op=ALU.not_equal, fill=1.0, base=0,
                                 pattern=[[0, PH], [-1, NS]], channel_multiplier=1))
            G.iota(iotai, pattern=[[1, TOPK]], base=0, channel_multiplier=0).then_inc(s_const, 1)

            def gathers(par, group, g, rows):
                sl = slice(0, rows)
                pool.wait_ge(s_uused, g + 1)
                pool.sem_inc(s_gatep, 1)
                for j in range(GATE):
                    k = group * GATE + j
                    G.indirect_dma_start(U[j][sl, :], None, down,
                                         bass.IndirectOffsetOnAxis(ap=idx[par][sl, k:k + 1], axis=0)).then_inc(s_U[j], 16)
                for j in range(GATE):
                    if j % HG == 0:
                        pool.wait_ge(s_vused, 2 * g + 1 + j // HG)
                        pool.sem_inc(s_gatep, 1)
                    k = group * GATE + j
                    G.indirect_dma_start(Vr[j][sl, :], None, up,
                                         bass.IndirectOffsetOnAxis(ap=idx[par][sl, k:k + 1], axis=0)).then_inc(s_V[j], 16)

            with pool.Fori(0, NU // 2) as it:
                for par in range(2):
                    pool.wait_ge(s_top, 2 * it + par + 1)
                    pool.sem_inc(s_gatep, 1)
                    for group in range(NGRP):
                        gathers(par, group, 4 * it + 2 * par + group, P)
            pool.wait_ge(s_top, NU + 1)
            pool.sem_inc(s_gatep, 1)
            for group in range(NGRP):
                gathers(0, group, 2 * NU + group, 64)

        @block.scalar
        def _(act):
            S = nc.scalar

            def softmax(n, par, rows=P):
                act.wait_ge(s_nmax, n)
                S.activation(w[par], fv, ACT.Exp, bias=ssum[:, 1:2], accum_out=ssum[:, 0:1]).then_inc(s_exp, 1)

            def weights(g, gp, rows, dst):
                act.wait_ge(s_uused, g + 2)
                S.activation(gel[gp][0:rows, :], dots[gp][0:rows, :], ACT.Gelu).then_inc(s_gelu, 1)
                act.wait_ge(s_actv, g + 1)
                for j in range(GATE):
                    if j % HG == 0:
                        act.wait_ge(s_vused, 2 * g + 1 + j // HG)
                    S.activation(dst[j][0], dst[j][1], ACT.Copy, scale=actv[gp][0:rows, j:j + 1]).then_inc(s_diag, 1)

            full = [(diag[:, j, :], ident) for j in range(GATE)]
            small = [(diag[0:64, j, 0:NS], r64[0:64, :]) for j in range(GATE)]

            def norm(b, n):
                act.wait_ge(s_x2, b + 1)
                S.activation(ps[0:n, 5:7, :].rearrange("p a n -> p (a n)"), xb[0:n, :], ACT.Square,
                             accum_out=stat[0:n, :]).then_inc(s_sq, 1)
                act.wait_ge(s_var, b + 1)
                S.activation(rstd[0:n, :], stat[0:n, :], ACT.Sqrt).then_inc(s_rt, 1)

            def keep(t):
                n = t - 2
                act.wait_ge(s_q, n + 1)
                if n >= 2:
                    act.wait_ge(s_s, n - 1)
                Q.keep(nc, ps, t).then_inc(s_qT, 1)
                act.wait_ge(s_qT, 2 * n + 1)
                Q.keep_samples(nc, t).then_inc(s_qT, 1)

            softmax(1, 0)
            keep(2)
            for u in range(PH):
                if u + 1 < PH:
                    keep(2 * u + 3)
                weights(2 * u, 0, P, full)
                softmax(u + 2, (u + 1) % 2)
                if u + 2 < PH:
                    keep(2 * u + 4)
                weights(2 * u + 1, 1, P, full)
            weights(2 * PH, 0, P, full)
            norm(0, P)

            def rest(b):
                softmax(8 * b + 2, 1)
                weights(16 * b + 1, 1, P, full)
                weights(16 * b + 2, 0, P, full)
                softmax(8 * b + 3, 0)
                weights(16 * b + 3, 1, P, full)
                with act.Fori(1, PH // 2) as hp:
                    for par in range(2):
                        g = 16 * b + 4 * hp + 2 * par
                        weights(g, 0, P, full)
                        softmax(8 * b + 2 * hp + par + 2, 1 - par)
                        weights(g + 1, 1, P, full)

            with act.Fori(1, NB - 1) as b:
                rest(b)
                weights(16 * b + 16, 0, P, full)
                norm(b, P)
            rest(NB - 1)
            act.wait_ge(s_x64, 2)
            weights(2 * NU, 0, 64, small)
            norm(NB - 1, P)
            weights(2 * NU + 1, 1, 64, small)
            norm(NB, NS)

        @block.tensor
        def _(pe):
            mm = nc.tensor.matmul
            pe.wait_ge(s_const, 1)
            pe.sem_inc(s_vused, 2)

            def open_sum(rows):
                for j in range(2):
                    mm(ps[0:rows, j, :], zero[:, 0:rows], U0, start=True, stop=False, skip_group_check=True)

            def close_sum(rows):
                for j in range(2):
                    last = mm(ps[0:rows, j, :], zero[:, 0:rows], U0, start=False, stop=True, skip_group_check=True)
                last.then_inc(s_blk, 1)

            U0 = h2[:, 0:512]

            def add(g, lhs, rows, kr):
                for j in range(GATE):
                    pe.wait_ge(s_V[j], 16 * g + 16)
                    pe.wait_ge(s_diag, GATE * g + j + 1)
                    for n in range(2):
                        last = mm(ps[0:rows, n, :], lhs[j], Vr[j][0:kr, n * 512:(n + 1) * 512], start=False, stop=False,
                                  skip_group_check=True)
                    if j % HG == HG - 1:
                        last.then_inc(s_vused, 1)

            full = [diag[:, j, :] for j in range(GATE)]
            small = [diag[0:64, j, 0:NS] for j in range(GATE)]
            def ask(t):
                if t % 2 == 0 and t > 2:
                    pe.wait_ge(s_w[(t // 2) % 2], 16 * (t // 4))
                if t > 2:
                    pe.wait_ge(s_qT, 2 * t - 5)
                Q.project(nc, ps, t).then_inc(s_q, 1)

            ask(2)
            open_sum(P)
            for u in range(PH):
                if u + 1 < PH:
                    ask(2 * u + 3)
                    for t in (2 * u + 2, 2 * u + 3):
                        n = t - 2
                        pe.wait_ge(s_qT, 2 * n + 2)
                        if n >= 2:
                            pe.wait_ge(s_srd, n - 1)
                        Q.score(nc, ps, t).then_inc(s_s, 1)
                add(2 * u, full, P, P)
                if u + 2 < PH:
                    ask(2 * u + 4)
                add(2 * u + 1, full, P, P)
            close_sum(P)
            pe.wait_ge(s_srd, NQ)
            nc.tensor.transpose(ps[0:64, 4, 0:NS], sel64.rearrange("p h b -> p (h b)"), ident[0:NS, 0:NS])
            for j in range(2):
                last = mm(ps[0:64, 2 + j, :], sel64.rearrange("p h b -> p (h b)"),
                          h2[0:NS, 4 * D + j * 512:4 * D + (j + 1) * 512], start=True, stop=True)
            last.then_inc(s_ps64, 1)
            with pe.Fori(1, NB) as b:
                pe.wait_ge(s_blkrd, b)
                open_sum(P)
                with pe.Fori(0, PH // 2) as hp:
                    for group in range(2 * NGRP):
                        add(16 * b + 4 * hp + group, full, P, P)
                close_sum(P)
            pe.wait_ge(s_blkrd, NB)
            open_sum(NS)
            for group in range(NGRP):
                add(2 * NU + group, small, NS, 64)
            close_sum(NS)

        @block.vector
        def _(dve):
            V = nc.vector
            tt, ts, stt = V.tensor_tensor, V.tensor_scalar, V.scalar_tensor_tensor

            def done(ins):
                dve.drain()

            def top16(vals, index, src, rep):
                done(V.max(vals[:, 0:8], src))
                V.max_index(index[:, 0:8], vals[:, 0:8], src)
                done(V.match_replace(rep, vals[:, 0:8], src, NEG))
                done(V.max(vals[:, 8:16], rep))
                V.max_index(index[:, 8:16], vals[:, 8:16], rep)

            def topk(unit, par, n):
                done(V.tensor_copy(s_in.rearrange("p s k -> p (s k)"), scores[:, bass.ds(unit * 2 * NK, 2 * NK)]))
                for s in range(2):
                    top16(val[:, s, :], kix[:, s * TOPK:(s + 1) * TOPK], s_in[:, s, :], s_rep[:, s, :])
                dve.drain()
                done(tt(cand, val[:, 0, :].unsqueeze(2).to_broadcast([P, TOPK, TOPK]),
                        val[:, 1, :].unsqueeze(1).to_broadcast([P, TOPK, TOPK]), ALU.add))
                flat = cand.rearrange("p a b -> p (a b)")
                top16(fv, fix, flat, crep.rearrange("p a b -> p (a b)"))
                ts(ssum[:, 1:2], fv[:, 0:1], -1.0, None, ALU.mult).then_inc(s_nmax, 1)
                dve.drain()
                ts(fiju[:, 0:TOPK], fix, 4, None, ALU.logical_shift_right)
                ts(fiju[:, TOPK:2 * TOPK], fix, TOPK - 1, None, ALU.bitwise_and)
                done(V.tensor_copy(idxf.rearrange("p s k -> p (s k)"), kix))
                done(V.tensor_copy(fij.rearrange("p s k -> p (s k)"), fiju))
                fl = fij.rearrange("p s k -> p (s k)")
                done(tt(oh, fl.unsqueeze(2).to_broadcast([P, 2 * TOPK, TOPK]),
                        iota.unsqueeze(1).to_broadcast([P, 2 * TOPK, TOPK]), ALU.is_equal))
                o4 = oh.rearrange("p (s k) m -> p s k m", s=2)
                done(tt(o4, o4, idxf.unsqueeze(2).to_broadcast([P, 2, TOPK, TOPK]), ALU.mult))
                done(V.tensor_reduce(r01.rearrange("p s k -> p (s k)"), oh, AX_X, ALU.add))
                done(stt(out=ef, in0=r01[:, 0, :], scalar=float(NK), in1=r01[:, 1, :], op0=ALU.mult, op1=ALU.add))
                dve.wait_ge(s_exp, n)
                done(V.reciprocal(ssum[:, 2:3], ssum[:, 0:1]))
                ts(w[par], w[par], ssum[:, 2:3], None, ALU.mult)
                V.tensor_copy(idx[par], ef).then_inc(s_top, 1)

            def products(g, gp, xrow, rows):
                for j in range(GATE):
                    dve.wait_ge(s_U[j], 16 * g + 16)
                    last = V.tensor_tensor_reduce(U[j][0:rows, :], U[j][0:rows, :], xrow, 1.0, 0.0, ALU.mult, ALU.add,
                                                  dots[gp][0:rows, j:j + 1])
                last.then_inc(s_uused, 1)

            def weight(g, gp, par, group, rows):
                dve.wait_ge(s_gelu, g + 1)
                tt(actv[gp][0:rows, :], gel[gp][0:rows, :], w[par][0:rows, group * GATE:(group + 1) * GATE],
                   ALU.mult).then_inc(s_actv, 1)

            def close(b, n, r, x_in):
                dve.wait_ge(s_blk, b + 1)
                tt(xb[0:n, :], ps[0:n, 0:2, :].rearrange("p a n -> p (a n)"), gate[0:n, r, :], ALU.mult).then_inc(s_blkrd, 1)
                dve.drain()
                tt(xb[0:n, :], xb[0:n, :], x_in, ALU.add).then_inc(s_x2, 1)

            def normed(b, n, r):
                dve.wait_ge(s_sq, b + 1)
                done(ts(stat[0:n, :], stat[0:n, :], 1.0 / D, EPS, ALU.mult, ALU.add))
                V.reciprocal(stat[0:n, :], stat[0:n, :]).then_inc(s_var, 1)
                dve.wait_ge(s_rt, b + 1)
                done(stt(out=xb[0:n, :], in0=xb[0:n, :], scalar=rstd[0:n, :], in1=scale[0:n, r, :], op0=ALU.mult,
                         op1=ALU.mult))
                dve.wait_ge(s_out, 16 * b + 16)
                tt(yb[0:n, :], xb[0:n, :], shift[0:n, r, :], ALU.add).then_inc(s_y, 1)

            def second(unit, g, par):
                dve.wait_ge(s_vused, 2 * g)
                topk(unit + 1, 1 - par, unit + 2)
                products(g, 1, hb, P)
                weight(g, 1, par, 1, P)

            def rest(b):
                second(8 * b, 16 * b + 1, 0)
                products(16 * b + 2, 0, hb, P)
                weight(16 * b + 2, 0, 1, 0, P)
                second(8 * b + 1, 16 * b + 3, 1)
                with dve.Fori(1, PH // 2) as hp:
                    for par in range(2):
                        g = 16 * b + 4 * hp + 2 * par
                        products(g, 0, hb, P)
                        weight(g, 0, par, 0, P)
                        second(8 * b + 2 * hp + par, g + 1, par)

            dve.wait_ge(s_const, 1)
            done(V.tensor_copy(iota, iotai))
            topk(0, 0, 1)
            done(V.tensor_copy(hb, h2[:, 0:D]))
            for u in range(PH):
                products(2 * u, 0, hb, P)
                weight(2 * u, 0, u % 2, 0, P)
                if u + 1 < PH:
                    for t in (2 * u + 2, 2 * u + 3):
                        dve.wait_ge(s_s, t - 1)
                        Q.store(nc, ps, t).then_inc(s_srd, 1)
                    dve.drain()
                second(u, 2 * u + 1, u % 2)
            for i in range(2):
                V.tensor_copy(mem(Map.SCS, 2, NK)[0:64, i, :], ps[0:64, 6 + i, 0:NK])
            done(V.tensor_copy(hb, h2[:, D:2 * D]))
            products(2 * PH, 0, hb, P)
            dve.wait_ge(s_ps64, 1)
            V.tensor_copy(r64[0:64, :], ps[0:64, 4, 0:NS]).then_inc(s_x64, 1)
            V.tensor_copy(x64[0:64, :], ps[0:64, 2:4, :].rearrange("p a n -> p (a n)")).then_inc(s_x64, 1)
            dve.wait_ge(s_rows, 16 * 7)
            for r, n in ((0, P), (1, NS)):
                stt(out=scale[0:n, r, :], in0=scale[0:n, r, :], scalar=1.0, in1=gf[0:n, :], op0=ALU.add, op1=ALU.mult)
            close(0, P, 0, x1[:, 0:D])
            weight(2 * PH, 0, 0, 0, P)
            normed(0, P, 0)
            with dve.Fori(1, NB - 1) as b:
                rest(b)
                done(V.tensor_copy(hb, h2[:, bass.ds(b * D + D, D)]))
                products(16 * b + 16, 0, hb, P)
                close(b, P, 0, x1[:, bass.ds(b * D, D)])
                weight(16 * b + 16, 0, 0, 0, P)
                normed(b, P, 0)
            rest(NB - 1)
            products(2 * NU, 0, x64[0:64, :], 64)
            close(NB - 1, P, 0, x1[:, (NB - 1) * D:NB * D])
            weight(2 * NU, 0, 0, 0, 64)
            normed(NB - 1, P, 0)
            products(2 * NU + 1, 1, x64[0:64, :], 64)
            weight(2 * NU + 1, 1, 0, 1, 64)
            close(NB, NS, 1, x1[0:NS, NB * D:(NB + 1) * D])
            normed(NB, NS, 1)


def program(nc, A, O):
    with nc.cleanup_on_exit(), ExitStack() as ctx:
        mem = Arena(ctx.enter_context(nc.sbuf_tensor("arena", [P, Map.W], F32)))
        ps = ctx.enter_context(nc.psum_tensor("ps", [P, 8, 512], F32))
        mod_d = nc.dram_tensor("mod_scratch", (NC_ROWS, NMOD * D), F32, kind="Internal").ap()
        bc_d = nc.dram_tensor("bc_scratch", (NS, D), F32, kind="Internal").ap()

        integers = {name: ctx.enter_context(nc.sbuf_tensor(name, [P, n], dtype))[:, :] for name, n, dtype in
                    (("expert0", TOPK, U32), ("expert1", TOPK, U32), ("keys", 2 * TOPK, U32), ("pairs", TOPK, U32),
                     ("halves", 2 * TOPK, U32), ("counting", TOPK, I32))}

        s_s5, s_ssd = nc.alloc_semaphore("first_s5"), nc.alloc_semaphore("first_ssd")
        for stage, more in ((constants, ()), (stage_condition, (ps, A, mod_d, s_s5)),
                            (stage_s5, (ps, A, O, s_s5, s_ssd)), (stage_ssd, (ps, A, O, bc_d, s_ssd)), (stage_query, (ps, A, mod_d)),
                            (stage_peer, (ps, A, O, mod_d, integers))):
            with nc.cleanup_on_exit():
                stage(nc, mem, nc.alloc_semaphore, *more)


_INS = ['x_prompt', 'x_sample', 'state_s5_re', 'state_s5_im', 'state_ssm', 'state_conv', 'c_prompt', 'c_sample',
        'w_ada', 'b_ada', 'g_norm1', 'g_norm2', 'w_in', 's5_a_re', 's5_a_im', 's5_log_dt', 's5_b_re', 's5_b_im',
        's5_c_re', 's5_c_im', 's5_d', 's5_w_glu', 's5_b_glu', 'w_branch_a', 'conv_w', 'conv_b', 'dt_bias', 'a_log',
        'd_skip', 'g_ssm_norm', 'w_branch_b', 'w_out', 'w_query', 'sub_keys', 'expert_down', 'expert_up', 'g_final',
        'w_ada_final', 'b_ada_final']
_OUTS = [(1, L, D), (NS, 1, D), (1, 1, NG5, ST5), (1, 1, NG5, ST5), (1, 1, NH, HD, SN), (1, 1, 3, CD),
         (1, NS, NG5, ST5), (1, NS, NG5, ST5), (1, NS, NH, HD, SN), (1, NS, 3, CD)]


def kernel(**inputs):
    import numpy as _np
    import concourse.bacc as _bacc
    from concourse import mybir as _mybir
    from concourse.bass_utils import run_bass_kernel_spmd as _run

    nc = _bacc.Bacc("TRN2", target_bir_lowering=False, num_devices=1)
    arrays, args = {}, {}
    for name in _INS:
        a = _np.ascontiguousarray(inputs[name])
        arrays[f"in_{name}_dram"] = a
        args[name] = nc.dram_tensor(f"in_{name}_dram", a.shape, _mybir.dt.from_np(a.dtype), kind="ExternalInput").ap()
    outs = [nc.dram_tensor(f"out_{i}_dram", shape, _mybir.dt.float32, kind="ExternalOutput").ap()
            for i, shape in enumerate(_OUTS)]
    program(nc, args, outs)
    r = _run(nc, [arrays], core_ids=[0])
    return tuple(r.results[0][f"out_{i}_dram"] for i in range(len(_OUTS)))
```
